# Optimizing a Trainium2 kernel written in Bass

```python
import jax
import jax.numpy as jnp
from jax import lax

D_MODEL = 2048
BATCH = 1
SEQ = 1024
DEPTH = 1

CHUNK = 64
D_MIX = D_MODEL
RMS_EPS = 1e-6

RWKV_WIDTH = D_MIX // 2
RWKV_HEAD = 64
RWKV_HEADS = RWKV_WIDTH // RWKV_HEAD
DECAY_RANK = max(32, int(round(1.8 * RWKV_WIDTH ** 0.5 / 32)) * 32)
ICLR_RANK = max(32, int(round(1.8 * RWKV_WIDTH ** 0.5 / 32)) * 32)
GATE_RANK = max(32, int(round(0.6 * RWKV_WIDTH ** 0.8 / 32)) * 32)
RWKV_GN_EPS = 64e-5
RWKV_IN = 3 * RWKV_WIDTH + DECAY_RANK + ICLR_RANK + GATE_RANK

ATTN_WIDTH = D_MIX - RWKV_WIDTH
ATTN_HEAD_DIM = 64
ATTN_HEADS = ATTN_WIDTH // ATTN_HEAD_DIM
ATTN_KV_HEADS = max(1, ATTN_HEADS // 8)
WINDOW = 128
WINDOW_CHUNKS = WINDOW // CHUNK
ATTN_IN = ATTN_WIDTH + 2 * ATTN_KV_HEADS * ATTN_HEAD_DIM

IN_TOTAL = RWKV_IN + ATTN_IN

N_GROUPS = 4
EXPERTS_PER_GROUP = 8
N_EXPERTS = N_GROUPS * EXPERTS_PER_GROUP
TOP_K = 2
EXPERT_HIDDEN = D_MODEL // 4
MOE_BLOCK = 128

kernel_name = 'hybrid_rwkv7_swa_sink_hier_moe'

def _rmsnorm(x, g):
    xf = x.astype(jnp.float32)
    y = xf * lax.rsqrt(jnp.mean(xf * xf, axis=-1, keepdims=True) + RMS_EPS)
    return (y * g.astype(jnp.float32)).astype(x.dtype)

def _wkv7_scan(r, decay, k, v, a, b):
    bsz, _, nh, n = r.shape

    def step(state, inp):
        r_t, w_t, k_t, v_t, a_t, b_t = inp
        sa = jnp.einsum('bhvk,bhk->bhv', state, a_t)
        state = (state * w_t[:, :, None, :] + sa[..., None] * b_t[:, :, None, :]
                 + v_t[..., None] * k_t[:, :, None, :])
        return state, jnp.einsum('bhvk,bhk->bhv', state, r_t)

    xs = tuple(jnp.moveaxis(u, 1, 0) for u in (r, decay, k, v, a, b))
    s0 = jnp.zeros((bsz, nh, n, n), jnp.float32)
    _, ys = lax.scan(step, s0, xs)
    return jnp.moveaxis(ys, 0, 1)

def _rwkv7_time_mix(z, w0, w_lora_up, a0, a_lora_up, g_lora_up, k_k, k_a, r_k, ln_x_g, ln_x_b):
    f32 = jnp.float32
    bsz, t, _ = z.shape
    nh, n, c = RWKV_HEADS, RWKV_HEAD, RWKV_WIDTH
    zf = z.astype(f32)
    r = zf[..., :c]
    k = zf[..., c:2 * c]
    v = zf[..., 2 * c:3 * c]
    o = 3 * c
    wd = zf[..., o:o + DECAY_RANK]
    o += DECAY_RANK
    ad = zf[..., o:o + ICLR_RANK]
    o += ICLR_RANK
    gd = zf[..., o:o + GATE_RANK]
    w_log = -jax.nn.softplus(-(w0.astype(f32) + jnp.tanh(wd) @ w_lora_up.astype(f32))) - 0.5
    decay = jnp.exp(-jnp.exp(w_log))
    a = jax.nn.sigmoid(a0.astype(f32) + ad @ a_lora_up.astype(f32))
    g = jax.nn.sigmoid(gd) @ g_lora_up.astype(f32)

    def heads(u):
        return u.reshape(bsz, t, nh, n)

    kk = heads(k * k_k.astype(f32))
    kk = kk / jnp.maximum(jnp.sqrt(jnp.sum(kk * kk, axis=-1, keepdims=True)), 1e-12)
    k = k * (1.0 + (a - 1.0) * k_a.astype(f32))
    rh, kh, vh = heads(r), heads(k), heads(v)
    y = _wkv7_scan(rh, heads(decay), kh, vh, -kk, kk * heads(a))
    mu = jnp.mean(y, axis=-1, keepdims=True)
    var = jnp.mean(jnp.square(y - mu), axis=-1, keepdims=True)
    y = ((y - mu) * lax.rsqrt(var + RWKV_GN_EPS)).reshape(bsz, t, c)
    y = y * ln_x_g.astype(f32) + ln_x_b.astype(f32)
    bonus = jnp.sum(rh * kh * r_k.astype(f32), axis=-1, keepdims=True) * vh
    out = (y + bonus.reshape(bsz, t, c)) * g
    return out.astype(z.dtype)

def _swa_sink_alibi(q, k, v, sinks):
    f32 = jnp.float32
    bsz, t, nh, hd = q.shape
    nkv = k.shape[2]
    grp = nh // nkv
    nc = t // CHUNK
    lk = WINDOW_CHUNKS * CHUNK
    qc = q.reshape(bsz, nc, CHUNK, nkv, grp, hd)
    kc = k.reshape(bsz, nc, CHUNK, nkv, hd)
    vc = v.reshape(bsz, nc, CHUNK, nkv, hd)
    pad = ((0, 0), (WINDOW_CHUNKS - 1, 0), (0, 0), (0, 0), (0, 0))
    kp = jnp.pad(kc, pad)
    vp = jnp.pad(vc, pad)
    kb = jnp.concatenate([kp[:, m:m + nc] for m in range(WINDOW_CHUNKS)], axis=2)
    vb = jnp.concatenate([vp[:, m:m + nc] for m in range(WINDOW_CHUNKS)], axis=2)
    s = jnp.einsum('bcikgd,bcjkd->bckgij', qc, kb).astype(f32) * (hd ** -0.5)
    qi = jnp.arange(CHUNK)[:, None]
    kj = jnp.arange(lk)[None, :]
    dist = jnp.abs(qi + (WINDOW_CHUNKS - 1) * CHUNK - kj).astype(f32)
    slopes = (2.0 ** (-8.0 * jnp.arange(1, nh + 1, dtype=f32) / nh)).reshape(nkv, grp)
    s = s - slopes[:, :, None, None] * dist
    valid = (jnp.arange(nc)[:, None] - (WINDOW_CHUNKS - 1) + kj // CHUNK) >= 0
    s = jnp.where(valid[None, :, None, None, None, :], s, -jnp.inf)
    sink = jnp.broadcast_to(sinks.astype(f32).reshape(nkv, grp)[None, None, :, :, None, None],
                            s.shape[:-1] + (1,))
    p = jax.nn.softmax(jnp.concatenate([s, sink], axis=-1), axis=-1)[..., :-1]
    out = jnp.einsum('bckgij,bcjkd->bcikgd', p.astype(vb.dtype), vb)
    return out.reshape(bsz, t, nh * hd)

def _hier_moe(h, rg_w, rg_b, re_w, re_b, wg, wu, wd):
    f32 = jnp.float32
    bsz, t, d = h.shape
    xt = h.reshape(-1, d)
    ntok = xt.shape[0]
    gl = (xt @ rg_w + rg_b).astype(f32)
    gp = jax.nn.softmax(gl, axis=-1)
    _, gi = lax.top_k(gl, 1)
    p_grp = jnp.take_along_axis(gp, gi, axis=-1)
    el_all = jnp.einsum('nd,gde->nge', xt, re_w) + re_b
    el = jnp.take_along_axis(el_all, gi[:, :, None], axis=1)[:, 0].astype(f32)
    top_v, top_i = lax.top_k(el, TOP_K)
    weights = p_grp * jax.nn.softmax(top_v, axis=-1)
    expert = gi * EXPERTS_PER_GROUP + top_i

    m = ntok * TOP_K
    nb = -(-m // MOE_BLOCK) + N_EXPERTS
    flat_e = expert.reshape(-1)
    order = jnp.argsort(flat_e)
    sorted_e = flat_e[order]
    sorted_tok = (order // TOP_K).astype(jnp.int32)
    sorted_w = weights.reshape(-1)[order]
    counts = jnp.bincount(flat_e, length=N_EXPERTS)
    starts = jnp.cumsum(counts) - counts
    pcounts = ((counts + MOE_BLOCK - 1) // MOE_BLOCK) * MOE_BLOCK
    pends = jnp.cumsum(pcounts)
    pstarts = pends - pcounts
    dest = pstarts[sorted_e] + (jnp.arange(m) - starts[sorted_e])
    slot_tok = jnp.zeros((nb * MOE_BLOCK,), jnp.int32).at[dest].set(sorted_tok)
    slot_w = jnp.zeros((nb * MOE_BLOCK,), f32).at[dest].set(sorted_w)
    block_e = jnp.clip(jnp.searchsorted(pends, jnp.arange(nb) * MOE_BLOCK, side='right'),
                       0, N_EXPERTS - 1)
    xb = xt[slot_tok].reshape(nb, MOE_BLOCK, d)

    def expert_block(args):
        xblk, e = args
        hid = jax.nn.silu(xblk @ wg[e]) * (xblk @ wu[e])
        return hid @ wd[e]

    yb = lax.map(expert_block, (xb, block_e)).reshape(nb * MOE_BLOCK, d)
    yb = yb * slot_w[:, None].astype(yb.dtype)
    out = jnp.zeros((ntok, d), yb.dtype).at[slot_tok].add(yb)
    return out.reshape(bsz, t, d)

def setup_inputs(seed: int = 0) -> dict:
    key = jax.random.key(seed)
    ks = jax.random.split(key, 32)
    f32 = jnp.float32

    def nrm(k, shape, scale):
        return jax.random.normal(k, shape, f32) * scale

    def unif(k, shape, lo, hi):
        return jax.random.uniform(k, shape, f32, lo, hi)

    L = DEPTH
    return {
        'x': nrm(ks[0], (BATCH, SEQ, D_MODEL), 1.0),
        'norm_mix_g': 1.0 + nrm(ks[1], (L, D_MODEL), 0.02),
        'w_in': nrm(ks[2], (L, D_MODEL, IN_TOTAL), D_MODEL ** -0.5),
        'shift_mu': unif(ks[3], (L, RWKV_IN), 0.0, 1.0),
        'w0': unif(ks[4], (L, RWKV_WIDTH), -6.0, -1.0),
        'w_lora_up': nrm(ks[5], (L, DECAY_RANK, RWKV_WIDTH), DECAY_RANK ** -0.5),
        'a0': nrm(ks[6], (L, RWKV_WIDTH), 0.1),
        'a_lora_up': nrm(ks[7], (L, ICLR_RANK, RWKV_WIDTH), 0.5 * ICLR_RANK ** -0.5),
        'g_lora_up': nrm(ks[8], (L, GATE_RANK, RWKV_WIDTH), GATE_RANK ** -0.5),
        'k_k': 0.85 + nrm(ks[9], (L, RWKV_WIDTH), 0.05),
        'k_a': 1.0 + nrm(ks[10], (L, RWKV_WIDTH), 0.05),
        'r_k': nrm(ks[11], (L, RWKV_HEADS, RWKV_HEAD), 0.1),
        'ln_x_g': 1.0 + nrm(ks[12], (L, RWKV_WIDTH), 0.02),
        'ln_x_b': nrm(ks[13], (L, RWKV_WIDTH), 0.02),
        'attn_sinks': nrm(ks[14], (L, ATTN_HEADS), 1.0),
        'w_out': nrm(ks[15], (L, D_MIX, D_MODEL), D_MIX ** -0.5),
        'norm_ffn_g': 1.0 + nrm(ks[16], (L, D_MODEL), 0.02),
        'router_group_w': nrm(ks[17], (L, D_MODEL, N_GROUPS), D_MODEL ** -0.5),
        'router_group_b': nrm(ks[18], (L, N_GROUPS), 0.01),
        'router_expert_w': nrm(ks[19], (L, N_GROUPS, D_MODEL, EXPERTS_PER_GROUP), D_MODEL ** -0.5),
        'router_expert_b': nrm(ks[20], (L, N_GROUPS, EXPERTS_PER_GROUP), 0.01),
        'expert_w_gate': nrm(ks[21], (L, N_EXPERTS, D_MODEL, EXPERT_HIDDEN), D_MODEL ** -0.5),
        'expert_w_up': nrm(ks[22], (L, N_EXPERTS, D_MODEL, EXPERT_HIDDEN), D_MODEL ** -0.5),
        'expert_w_down': nrm(ks[23], (L, N_EXPERTS, EXPERT_HIDDEN, D_MODEL), EXPERT_HIDDEN ** -0.5),
        'norm_final_g': 1.0 + nrm(ks[24], (D_MODEL,), 0.02),
    }

def reference(x, norm_mix_g, w_in, shift_mu, w0, w_lora_up, a0, a_lora_up, g_lora_up,
              k_k, k_a, r_k, ln_x_g, ln_x_b, attn_sinks, w_out, norm_ffn_g,
              router_group_w, router_group_b, router_expert_w, router_expert_b,
              expert_w_gate, expert_w_up, expert_w_down, norm_final_g):
    h = x
    bsz, t, _ = x.shape
    for l in range(DEPTH):
        hn = _rmsnorm(h, norm_mix_g[l])
        z = hn @ w_in[l]
        zr = z[..., :RWKV_IN]
        za = z[..., RWKV_IN:]
        zr_prev = jnp.pad(zr, ((0, 0), (1, 0), (0, 0)))[:, :-1]
        zr = zr + (zr_prev - zr) * shift_mu[l]
        y_rwkv = _rwkv7_time_mix(zr, w0[l], w_lora_up[l], a0[l], a_lora_up[l], g_lora_up[l],
                                 k_k[l], k_a[l], r_k[l], ln_x_g[l], ln_x_b[l])
        kvw = ATTN_KV_HEADS * ATTN_HEAD_DIM
        q = za[..., :ATTN_WIDTH].reshape(bsz, t, ATTN_HEADS, ATTN_HEAD_DIM)
        k = za[..., ATTN_WIDTH:ATTN_WIDTH + kvw].reshape(bsz, t, ATTN_KV_HEADS, ATTN_HEAD_DIM)
        v = za[..., ATTN_WIDTH + kvw:].reshape(bsz, t, ATTN_KV_HEADS, ATTN_HEAD_DIM)
        y_attn = _swa_sink_alibi(q, k, v, attn_sinks[l])
        h = h + jnp.concatenate([y_rwkv, y_attn], axis=-1) @ w_out[l]
        h = h + _hier_moe(_rmsnorm(h, norm_ffn_g[l]), router_group_w[l], router_group_b[l],
                          router_expert_w[l], router_expert_b[l], expert_w_gate[l],
                          expert_w_up[l], expert_w_down[l])
    return _rmsnorm(h, norm_final_g)


_drawn_inputs = setup_inputs


def setup_inputs(seed=0):
    import zlib

    import numpy as np

    out = dict(_drawn_inputs(seed))
    spreads = {}
    factors = {'ln_x_g': 2.848,
     'ln_x_b': 3.167,
     'router_group_b': 4.256,
     'router_expert_b': 4.147,
     'norm_final_g': 8.063,
     'norm_ffn_g': 2.836}
    for name, (base, spread) in spreads.items():
        noise = np.random.default_rng([zlib.crc32(name.encode()), seed]).standard_normal(out[name].shape)
        drawn = base * np.exp(spread * noise) if base else spread * noise
        out[name] = jnp.asarray(drawn.astype(out[name].dtype))
    for name, factor in factors.items():
        out[name] = (out[name] * factor).astype(out[name].dtype)
    return out
```

```python
import math
from contextlib import ExitStack

import numpy as np
import concourse.bass as bass
from concourse import mybir

F32 = mybir.dt.float32
F32R = mybir.dt.float32r
I32 = mybir.dt.int32
U32 = mybir.dt.uint32
U8 = mybir.dt.uint8
ALU = mybir.AluOpType
ACT = mybir.ActivationFunctionType
AXX = mybir.AxisListType.X

P = 128
SEQ = 1024
D = 2048
TT = SEQ // P
KT = D // P
HALF = 512
NH = SEQ // HALF
RMS_EPS = 1e-6

HEAD = 64
RW = 1024
RANK_W, RANK_A, RANK_G = 64, 64, 160
RWKV_IN = 3 * RW + RANK_W + RANK_A + RANK_G
AW = 1024
KVW = 128
IN_TOTAL = RWKV_IN + AW + 2 * KVW
PAIRS = RW // P
GN_EPS = 64e-5

COLT = IN_TOTAL // P
COL_TAIL = IN_TOTAL - COLT * P


def semaphores(nc, ctx):
    taken = []

    def give_back():
        nc.clear_and_free_semaphores(taken)
        nc.all_engine_barrier()
    ctx.callback(give_back)

    def take(name):
        taken.append(nc.alloc_semaphore(name))
        return taken[-1]
    return take


def project_in(nc, x, norm_g, w_in, zT, ident_d):
    xv = x.rearrange("(t p) d -> p t d", p=P)
    RAW = 3
    with ExitStack() as ctx:
        sb = lambda n, s, d=F32: ctx.enter_context(nc.sbuf_tensor(n, s, d))
        sem = semaphores(nc, ctx)
        hn_hi = sb("hn_hi", [P, KT, SEQ], F32R)
        hn_lo = sb("hn_lo", [P, KT, SEQ], F32R)
        ident = sb("ident_a", [P, P])
        g_col = sb("g_col", [P, KT])
        ss = sb("ss", [P, TT])
        rstd = sb("rstd", [P, TT])
        mhalf = sb("mhalf", [P, 1])
        ps = [ctx.enter_context(nc.psum_tensor(f"psA{i}", [P, HALF], F32)) for i in range(8)]
        x_loaded = [sem(f"x_loaded{t}") for t in range(TT)]
        c_loaded = sem("c_loaded")
        squared, mean_ready, rstd_ready, scaled = sem("squared"), sem("mean_ready"), sem("rstd_ready"), sem("scaled")
        transposed, hi_ready, lo_ready = sem("transposed"), sem("hi_ready"), sem("lo_ready")
        half_set = sem("half_set")

        with ExitStack() as ctx2:
            xt = ctx2.enter_context(nc.sbuf_tensor("xt", [P, 4, D], F32))
            junk = ctx2.enter_context(nc.sbuf_tensor("junk", [P, D], F32))
            with nc.Block() as block:
                @block.sync
                def _(sp):
                    sp.dma_start(ident[:, :], ident_d).then_inc(c_loaded, 16)
                    sp.dma_start(g_col[:, :], norm_g).then_inc(c_loaded, 16)
                    for t in range(TT):
                        if t >= 4:
                            sp.wait_ge(transposed, KT)
                        sp.dma_start(xt[:, t % 4, :], xv[:, t, :]).then_inc(x_loaded[t], 16)

                @block.gpsimd
                def _(pool):
                    nc.gpsimd.memset(mhalf[:, :], -0.5).then_inc(half_set, 1)
                    pool.wait_ge(half_set, 1)
                    for t in range(TT):
                        pool.wait_ge(mean_ready, t + 1)
                        nc.gpsimd.tensor_tensor(rstd[:, t:t + 1], ss[:, t:t + 1], mhalf[:, :], ALU.pow).then_inc(rstd_ready, 1)

                @block.scalar
                def _(act):
                    def evacuate(h):
                        for k in range(KT):
                            n = h * KT + k
                            act.wait_ge(transposed, n + 1)
                            nc.scalar.activation(hn_hi[:, k, h * HALF:(h + 1) * HALF], ps[n % 4][:, :], ACT.Copy,
                                                 scale=g_col[:, k:k + 1]).then_inc(hi_ready, 1)
                    act.wait_ge(c_loaded, 32)
                    for h in range(NH):
                        for i in range(4):
                            t = 4 * h + i
                            act.wait_ge(x_loaded[t], 16)
                            if t:
                                act.wait_ge(squared, t)
                            nc.scalar.activation(junk[:, :], xt[:, i, :], ACT.Square, accum_out=ss[:, t:t + 1]).then_inc(squared, 1)
                        evacuate(h)

                @block.vector
                def _(dve):
                    dve.wait_ge(c_loaded, 32)
                    for h in range(NH):
                        for i in range(4):
                            t = 4 * h + i
                            dve.wait_ge(squared, t + 1)
                            nc.vector.tensor_scalar(ss[:, t:t + 1], ss[:, t:t + 1], 1.0 / D, RMS_EPS, ALU.mult, ALU.add).then_inc(mean_ready, 1)
                            dve.wait_ge(rstd_ready, t + 1)
                            nc.vector.tensor_scalar(xt[:, i, :], xt[:, i, :], rstd[:, t:t + 1], None, ALU.mult).then_inc(scaled, 1)
                        for k in range(KT):
                            n = h * KT + k
                            dve.wait_ge(hi_ready, n + 1)
                            nc.vector.scalar_tensor_tensor(hn_lo[:, k, h * HALF:(h + 1) * HALF], ps[n % 4][:, :], g_col[:, k:k + 1],
                                                           hn_hi[:, k, h * HALF:(h + 1) * HALF].bitcast(F32), ALU.mult, ALU.subtract).then_inc(lo_ready, 1)

                @block.tensor
                def _(pe):
                    pe.wait_ge(c_loaded, 32)
                    for h in range(NH):
                        pe.wait_ge(scaled, 4 * (h + 1))
                        for k in range(KT):
                            n = h * KT + k
                            if n >= 4:
                                pe.wait_ge(lo_ready, n - 3)
                            for i in range(4):
                                last = nc.tensor.transpose(ps[n % 4][:, i * P:(i + 1) * P], xt[:, i, k * P:(k + 1) * P], ident[:, :])
                            last.then_inc(transposed, 1)

        wraw = sb("wraw", [P, 2, KT, P])
        w_hi = sb("w_hi", [P, 2, KT, P], F32R)
        w_lo = sb("w_lo", [P, 2, KT, P], F32R)
        z_sb = sb("z_sb", [P, 2, SEQ])
        w_loaded = [sem("w_loaded0"), sem("w_loaded1")]
        z_stored = [sem("z_stored0"), sem("z_stored1")]
        hi_split, lo_split = [sem("hi_split0"), sem("hi_split1")], [sem("lo_split0"), sem("lo_split1")]
        z_done, z_copied = [sem("z_done0"), sem("z_done1")], [sem("z_copied0"), sem("z_copied1")]
        TURNS = COLT // 2
        with nc.Block() as block:
            def load_w(sp, turn, b, first):
                if not first:
                    sp.wait_ge(lo_split[b], turn)
                sp.dma_start(wraw[:, b, :, :], w_in[bass.ds(2 * turn + b, 1), :, :, :].rearrange("a p k n -> (a p) k n")).then_inc(w_loaded[b], 16)

            def store_z(sp, turn, b):
                sp.wait_ge(z_copied[b], 2 * turn + 2)
                sp.dma_start(zT[bass.ds((2 * turn + b) * P, P), :], z_sb[:, b, :]).then_inc(z_stored[b], 16)

            @block.sync
            def _(sp):
                for b in range(2):
                    load_w(sp, 0, b, True)
                with sp.Fori(1, TURNS) as turn:
                    for b in range(2):
                        load_w(sp, turn, b, False)
                        store_z(sp, turn - 1, b)
                load_w(sp, TURNS, 0, False)
                for b in range(2):
                    store_z(sp, TURNS - 1, b)
                sp.wait_ge(z_copied[0], 2 * TURNS + 2)
                sp.dma_start(zT[COLT * P:, :], z_sb[P - COL_TAIL:, 0, :]).then_inc(z_stored[0], 16)
                sp.wait_ge(z_stored[0], 16 * (TURNS + 1))
                sp.wait_ge(z_stored[1], 16 * TURNS)

            def split_hi(act, turn, b, first):
                act.wait_ge(w_loaded[b], 16 * turn + 16)
                if not first:
                    act.wait_ge(z_done[b], 2 * turn)
                nc.scalar.activation(w_hi[:, b, :, :], wraw[:, b, :, :], ACT.Copy).then_inc(hi_split[b], 1)

            def copy_z(act, turn, b, first):
                if not first:
                    act.wait_ge(z_stored[b], 16 * turn)
                for h in range(NH):
                    act.wait_ge(z_done[b], 2 * turn + h + 1)
                    nc.scalar.activation(z_sb[:, b, h * HALF:(h + 1) * HALF], ps[2 * b + h][:, :], ACT.Copy).then_inc(z_copied[b], 1)

            @block.scalar
            def _(act):
                split_hi(act, 0, 0, True)
                split_hi(act, 0, 1, True)
                copy_z(act, 0, 0, True)
                split_hi(act, 1, 0, False)
                copy_z(act, 0, 1, True)
                with act.Fori(1, TURNS) as turn:
                    split_hi(act, turn, 1, False)
                    copy_z(act, turn, 0, False)
                    split_hi(act, turn + 1, 0, False)
                    copy_z(act, turn, 1, False)
                copy_z(act, TURNS, 0, False)

            def split_lo(dve, turn, b):
                dve.wait_ge(hi_split[b], turn + 1)
                nc.vector.tensor_tensor(w_lo[:, b, :, :], wraw[:, b, :, :], w_hi[:, b, :, :].bitcast(F32), ALU.subtract).then_inc(lo_split[b], 1)

            @block.vector
            def _(dve):
                with dve.Fori(0, TURNS) as turn:
                    for b in range(2):
                        split_lo(dve, turn, b)
                split_lo(dve, TURNS, 0)

            def multiply(pe, turn, b, first):
                pe.wait_ge(lo_split[b], turn + 1)
                for h in range(NH):
                    if not first:
                        pe.wait_ge(z_copied[b], 2 * turn - 1 + h)
                    cols = slice(h * HALF, (h + 1) * HALF)
                    for k in range(KT):
                        nc.tensor.matmul(ps[2 * b + h][:, :], w_hi[:, b, k, :], hn_hi[:, k, cols], start=k == 0, stop=False)
                        nc.tensor.matmul(ps[2 * b + h][:, :], w_hi[:, b, k, :], hn_lo[:, k, cols], start=False, stop=False)
                        last = nc.tensor.matmul(ps[2 * b + h][:, :], w_lo[:, b, k, :], hn_hi[:, k, cols], start=False, stop=k == KT - 1)
                    last.then_inc(z_done[b], 1)

            @block.tensor
            def _(pe):
                for b in range(2):
                    multiply(pe, 0, b, True)
                with pe.Fori(1, TURNS) as turn:
                    for b in range(2):
                        multiply(pe, turn, b, False)
                multiply(pe, TURNS, 0, False)


C0 = -0.5 * math.exp(-0.5)
UNITS = TT * 2
LEVELS = 7
GROUPS = UNITS // 4
(MU_R, MU_K, MU_V, OMU_R, OMU_K, OMU_V, W0_H, A0_H, K_K, K_A, ONE_M_KA, R_K, LNX_G, LNX_B) = range(14)
NPAR = 11


class Count:

    def __init__(self, sem, per_turn):
        self.sem, self.per_turn = sem, per_turn

    def at(self, turn, n):
        return turn * self.per_turn + n


def rwkv(nc, zT, params, mu_lora, w_up, a_up, g_up, consts, yT):
    ident_d, ones_d, sel_d, score_mask_d, level_mask_d = consts
    with ExitStack() as ctx:
        sb = lambda n, s, d=F32: ctx.enter_context(nc.sbuf_tensor(n, s, d))
        sem = semaphores(nc, ctx)
        cnt = lambda n, k: Count(sem(n), k)
        ident, ones = sb("ident_b", [P, P]), sb("ones_b", [P, P])
        sel = sb("sel_b", [P, 2])
        score_mask = sb("score_mask", [P, 4 * P], U8)
        level_mask = sb("level_mask", [P, LEVELS, 4, P], U8)
        par_all = sb("par_all", [P, PAIRS, 10])
        par = sb("par", [P, 14])
        mul, oml = sb("mul", [P, 3]), sb("oml", [P, 3])
        z3 = sb("z3", [P, 3, SEQ + 1])
        mix = sb("mix", [P, 3, SEQ])
        wa_act, g1_act, g2_act = sb("wa_act", [P, SEQ]), sb("g1_act", [P, SEQ]), sb("g2_act", [32, SEQ])
        wa_w = sb("wa_w", [P, P])
        g1_w, g2_w = sb("g1_w", [P, P]), sb("g2_w", [32, P])
        lw, ac, Lc, La, ER = (sb(n, [P, SEQ]) for n in ("lw", "ac", "Lc", "La", "ER"))
        kk, sq, k2, bv, gT = (sb(n, [P, SEQ]) for n in ("kkn", "sq", "k2", "bv", "gT"))
        BT, KTt = sb("BT", [P, SEQ]), sb("KTt", [P, SEQ])
        AR = sb("AR", [P, TT, 2, P])
        nat = sb("nat", [P, TT, 3, P])
        SC = sb("SC", [P, UNITS, 4, P])
        masks_wide = SC[...].rearrange("p u a c -> p (u a c)")[:, 0:(LEVELS + 1) * 4 * P]
        X, Y = sb("X", [P, UNITS, P]), sb("Y", [P, UNITS, P])
        T1 = sb("T1", [P, LEVELS, 2, 4 * P])
        m_half, m_sum, dec = sb("m_half", [P, TT]), sb("m_sum", [P, TT]), sb("dec", [P, TT])
        nrm, rn, mh = sb("nrm", [P, UNITS]), sb("rn", [P, UNITS]), sb("mh", [P, UNITS])
        RU, Un = sb("RU", [P, P]), sb("Un", [P, P])
        Ss = sb("Ss", [P, 2, P])
        st, ag = sb("st", [P, UNITS, 6]), sb("ag", [P, UNITS, 2])
        var = sb("var", [P, UNITS])
        rng_ = sb("rng_", [P, UNITS])
        ynat, ER_ = sq, ER
        rrk, qk = lw, bv
        ps = [ctx.enter_context(nc.psum_tensor(f"psB{i}", [P, HALF], F32)) for i in range(8)]

        const_loaded = sem("const_loaded")
        zl_loaded = sem("zl_loaded")
        masks_set, zeros_set = sem("masks_set"), sem("zeros_set")
        lora_a, lora_v = sem("lora_a"), sem("lora_v")
        turn_over, seen = sem("turn_over"), sem("seen_b")
        pair_loaded = cnt("pair_loaded", 16 * 6)
        par_set = cnt("par_set", 3)
        scaled, mixed = cnt("scaled_b", 3), cnt("mixed", 3)
        lora_done, tanhed, gated = cnt("lora_done", 6), cnt("tanhed", 4), cnt("gated", 2)
        kk_raw, squared, summed, norm_set, norm_pow, norm_wide, kk_set = (
            cnt("kk_raw", 1), cnt("squared_b", 1), cnt("summed", 1), cnt("norm_set", 1), cnt("norm_pow", 1),
            cnt("norm_wide", 2), cnt("kk_set", 2))
        dve_step = cnt("dve_step", 11 + TT)
        cum_set, exped = cnt("cum_set", 3), cnt("exped", 4)
        bonus_in, bonus_done = cnt("bonus_in", 1), cnt("bonus_done", 2)
        ops_set = cnt("ops_set", 4)
        nat_done, nat_set = cnt("nat_done", TT), cnt("nat_set", TT)
        scored, score_set = cnt("scored", UNITS), cnt("score_set", UNITS)
        t_done, t_set = cnt("t_done", LEVELS * GROUPS), cnt("t_set", LEVELS * GROUPS)
        y_done, y_set = cnt("y_done", (LEVELS - 1) * GROUPS), cnt("y_set", LEVELS * GROUPS)
        x_done, x_set = cnt("x_done", (LEVELS - 1) * GROUPS), cnt("x_set", (LEVELS - 1) * GROUPS)
        rhs_done, rhs_set, u_done, u_set = (cnt(n, TT) for n in ("rhs_done", "rhs_set", "u_done", "u_set"))
        s_done, s_set, out_done, out_set = cnt("s_done", TT - 1), cnt("s_set", TT), cnt("out_done", TT), cnt("out_set", TT)
        stat_set, aggr_set, var_set, gn_pow, gn_set = (cnt("stat_set", TT), cnt("aggr_set", TT), cnt("var_set", 1),
                                                       cnt("gn_pow", 1), cnt("gn_set", TT))
        flipped, affine, plus_bonus, y_ready = cnt("flipped", 2), cnt("affine", 2), cnt("plus_bonus", 2), cnt("y_ready", 2)
        y_stored = sem("y_stored")
        mh_set = sem("mh_set")
        g2_loaded = cnt("g2_loaded", 16)
        s_sum = cnt("s_sum", TT - 1)
        norm_rep = cnt("norm_rep", 1)
        half = lambda h: slice(h * HALF, (h + 1) * HALF)
        tile = lambda j: slice(j * P, (j + 1) * P)
        ENG = 4

        def wait(eng, c, turn, n):
            eng.wait_ge(c.sem, c.at(turn, n))

        def start_turn(eng, turn):
            eng.wait_ge(turn_over, (turn + 1) * ENG)

        with nc.Block() as block:
            @block.sync
            def _(sp):
                for o, i in ((ident[...], ident_d), (ones[...], ones_d), (sel[...], sel_d), (par_all[...], params), (mul[...], mu_lora),
                             (masks_wide[:, 0:4 * P], score_mask_d), (masks_wide[:, 4 * P:], level_mask_d)):
                    sp.dma_start(o, i).then_inc(const_loaded, 16)
                sp.dma_start(z3[:, 0, 1:], zT[3 * RW:3 * RW + P, :]).then_inc(zl_loaded, 16)
                sp.dma_start(z3[:, 1, 1:], zT[3 * RW + P:3 * RW + 2 * P, :]).then_inc(zl_loaded, 16)
                sp.dma_start(z3[0:32, 2, 1:], zT[3 * RW + 2 * P:RWKV_IN, :]).then_inc(zl_loaded, 16)
                sp.wait_ge(lora_v, 8)
                sp.sem_inc(turn_over, 1)
                with sp.Fori(0, PAIRS) as turn:
                    start_turn(sp, turn)
                    for i in range(3):
                        sp.dma_start(z3[:, i, 1:], zT[bass.ds(turn * P + i * RW, P), :]).then_inc(pair_loaded.sem, 16)
                    cols = bass.ds(turn * P, P)
                    sp.dma_start(wa_w[0:64, :], w_up[:, cols]).then_inc(pair_loaded.sem, 16)
                    sp.dma_start(wa_w[64:128, :], a_up[:, cols]).then_inc(pair_loaded.sem, 16)
                    sp.dma_start(g1_w[:, :], g_up[0:P, cols]).then_inc(pair_loaded.sem, 16)
                    sp.dma_start(g2_w[:, :], g_up[P:RANK_G, cols]).then_inc(g2_loaded.sem, 16)
                    wait(sp, y_ready, turn, 2)
                    sp.dma_start(yT[cols, :], gT[:, :]).then_inc(y_stored, 16)
                    sp.wait_ge(y_stored, 16 * turn + 16)
                    sp.sem_inc(turn_over, 1)

            @block.gpsimd
            def _(pool):
                nc.gpsimd.memset(mh[:, :], -0.5).then_inc(mh_set, 1)
                pool.wait_ge(mh_set, 1)
                with pool.Fori(0, PAIRS) as turn:
                    wait(pool, norm_set, turn, 1)
                    nc.gpsimd.tensor_tensor(rn[:, :], nrm[:, :], mh[:, :], ALU.pow).then_inc(norm_pow.sem, 1)
                    wait(pool, var_set, turn, 1)
                    nc.gpsimd.tensor_tensor(rng_[:, :], var[:, :], mh[:, :], ALU.pow).then_inc(gn_pow.sem, 1)

            @block.scalar
            def _(act):
                act.wait_ge(const_loaded, 16 * 7)
                act.wait_ge(zl_loaded, 48)
                act.wait_ge(lora_v, 1)
                for i, (o, n) in enumerate(((wa_act, P), (g1_act, P), (g2_act, 32))):
                    nc.scalar.activation(o[:, :], z3[0:n, i, 1:], ACT.Copy, scale=oml[0:n, i:i + 1]).then_inc(lora_a, 1)
                act.wait_ge(lora_v, 4)
                nc.scalar.activation(wa_act[0:64, :], wa_act[0:64, :], ACT.Tanh).then_inc(lora_a, 1)
                nc.scalar.activation(g1_act[:, :], g1_act[:, :], ACT.Tanh, scale=0.5).then_inc(lora_a, 1)
                nc.scalar.activation(g2_act[:, :], g2_act[:, :], ACT.Tanh, scale=0.5).then_inc(lora_a, 1)
                act.wait_ge(lora_a, 6)
                act.sem_inc(turn_over, 1)
                with act.Fori(0, PAIRS) as turn:
                    start_turn(act, turn)
                    wait(act, pair_loaded, turn, 96)
                    wait(act, par_set, turn, 3)
                    for i in range(3):
                        nc.scalar.activation(mix[:, i, :], z3[:, i, 1:], ACT.Copy, scale=par[:, OMU_R + i:OMU_R + i + 1]).then_inc(scaled.sem, 1)
                    for i in range(4):
                        wait(act, lora_done, turn, i + 1)
                        o, b = ((lw, W0_H), (ac, A0_H))[i // 2]
                        nc.scalar.activation(o[:, half(i % 2)], ps[i][:, :], ACT.Tanh, bias=par[:, b:b + 1], scale=0.5).then_inc(tanhed.sem, 1)
                    for i in range(2):
                        wait(act, lora_done, turn, 5 + i)
                        nc.scalar.activation(gT[:, half(i)], ps[4 + i][:, :], ACT.Copy).then_inc(gated.sem, 1)
                    wait(act, kk_raw, turn, 1)
                    nc.scalar.activation(sq[:, :], kk[:, :], ACT.Square).then_inc(squared.sem, 1)
                    wait(act, cum_set, turn, 2)
                    nc.scalar.activation(ER[:, :], Lc[:, :], ACT.Exp).then_inc(exped.sem, 1)
                    nc.scalar.activation(dec[:, 0:TT - 1], m_sum[:, 0:TT - 1], ACT.Exp).then_inc(exped.sem, 1)
                    wait(act, cum_set, turn, 3)
                    nc.scalar.activation(La[:, :], La[:, :], ACT.Exp).then_inc(exped.sem, 1)
                    wait(act, exped, turn, 1)
                    nc.scalar.activation(Lc[:, :], Lc[:, :], ACT.Exp, scale=-1.0).then_inc(exped.sem, 1)
                    for j in range(TT):
                        wait(act, nat_done, turn, j + 1)
                        nc.scalar.activation(nat[:, j, :, :].rearrange("p a c -> p (a c)"), ps[2 + j % 2][:, 0:3 * P], ACT.Copy).then_inc(nat_set.sem, 1)
                    for lev in range(LEVELS):
                        for g in range(GROUPS):
                            n = lev * GROUPS + g
                            units = slice(4 * g, 4 * g + 4)
                            if lev == 0:
                                wait(act, t_set, turn, n + 1)
                                src = T1[:, 0, g % 2, :]
                            else:
                                wait(act, y_done, turn, n - GROUPS + 1)
                                src = ps[2 + g % 2][:, :]
                            nc.scalar.activation(Y[:, units, :].rearrange("p u c -> p (u c)"), src, ACT.Copy).then_inc(y_set.sem, 1)
                        if lev < LEVELS - 1:
                            for g in range(GROUPS):
                                wait(act, x_done, turn, lev * GROUPS + g + 1)
                                nc.scalar.activation(X[:, 4 * g:4 * g + 4, :].rearrange("p u c -> p (u c)"), ps[4 + g % 2][:, :], ACT.Copy).then_inc(x_set.sem, 1)
                    def copy_out(j):
                        wait(act, out_done, turn, j + 1)
                        nc.scalar.activation(ynat[:, tile(j)], ps[j % 2][:, 0:P], ACT.Copy).then_inc(out_set.sem, 1)
                    for j in range(TT):
                        wait(act, rhs_done, turn, j + 1)
                        nc.scalar.activation(RU[:, :], ps[6][:, 0:P], ACT.Copy).then_inc(rhs_set.sem, 1)
                        wait(act, u_done, turn, j + 1)
                        nc.scalar.activation(Un[:, :], ps[7][:, 0:P], ACT.Copy).then_inc(u_set.sem, 1)
                        copy_out(j)
                    for i in range(2):
                        wait(act, flipped, turn, i + 1)
                        nc.scalar.activation(ER[:, half(i)], ps[4 + i][:, :], ACT.Identity, bias=par[:, LNX_B:LNX_B + 1],
                                             scale=par[:, LNX_G:LNX_G + 1]).then_inc(affine.sem, 1)
                    wait(act, affine, turn, 2)
                    act.sem_inc(turn_over, 1)

            @block.vector
            def _(dve):
                for i in range(3):
                    nc.vector.memset(z3[:, i, 0:1], 0.0).then_inc(zeros_set, 1)
                dve.wait_ge(const_loaded, 16 * 7)
                nc.vector.tensor_copy(score_mask[:, :], masks_wide[:, 0:4 * P]).then_inc(masks_set, 1)
                nc.vector.tensor_copy(level_mask[...].rearrange("p l u c -> p (l u c)"), masks_wide[:, 4 * P:]).then_inc(masks_set, 1)
                dve.wait_ge(masks_set, 2)
                nc.vector.memset(SC[...].rearrange("p u a c -> p (u a c)"), 0.0).then_inc(zeros_set, 1)
                for lev in range(LEVELS):
                    for b in range(2):
                        for u in range(4):
                            nc.vector.tensor_copy(T1[:, lev, b, tile(u)], ident[:, :]).then_inc(zeros_set, 1)
                dve.wait_ge(zeros_set, 4 + LEVELS * 8)
                nc.vector.tensor_scalar(oml[:, :], mul[:, 0:3], -1.0, 1.0, ALU.mult, ALU.add).then_inc(lora_v, 1)
                dve.wait_ge(zl_loaded, 48)
                for i, (o, n) in enumerate(((wa_act, P), (g1_act, P), (g2_act, 32))):
                    dve.wait_ge(lora_a, i + 1)
                    nc.vector.scalar_tensor_tensor(o[:, :], z3[0:n, i, 0:SEQ], mul[0:n, i:i + 1], o[:, :], ALU.mult, ALU.add).then_inc(lora_v, 1)
                for i, (o, n) in enumerate(((g1_act, P), (g2_act, 32))):
                    dve.wait_ge(lora_a, 5 + i)
                    nc.vector.tensor_scalar(o[:, :], o[:, :], 0.5, 0.5, ALU.mult, ALU.add).then_inc(lora_v, 1)
                nc.vector.memset(Ss[:, 0, :], 0.0).then_inc(lora_v, 1)
                dve.wait_ge(lora_a, 6)
                dve.wait_ge(lora_v, 7)
                nc.vector.memset(m_half[:, :], 0.0).then_inc(lora_v, 1)
                dve.wait_ge(lora_v, 8)
                dve.sem_inc(turn_over, 1)
                with dve.Fori(0, PAIRS) as turn:
                    start_turn(dve, turn)
                    steps = [0]

                    def link(ins):
                        steps[0] += 1
                        ins.then_inc(dve_step.sem, 1)
                        wait(dve, dve_step, turn, steps[0])

                    here = par_all[:, bass.ds(turn, 1), :].rearrange("p a c -> p (a c)")
                    nc.vector.tensor_copy(par[:, 0:3], here[:, 0:3]).then_inc(par_set.sem, 1)
                    nc.vector.tensor_scalar(par[:, OMU_R:OMU_R + 3], here[:, 0:3], -1.0, 1.0, ALU.mult, ALU.add).then_inc(par_set.sem, 1)
                    link(nc.vector.tensor_scalar(par[:, W0_H:W0_H + 2], here[:, 3:5], 0.5, None, ALU.mult))
                    link(nc.vector.tensor_copy(par[:, K_K:K_A + 1], here[:, 5:7]))
                    link(nc.vector.tensor_scalar(par[:, ONE_M_KA:ONE_M_KA + 1], here[:, 6:7], -1.0, 1.0, ALU.mult, ALU.add))
                    nc.vector.tensor_copy(par[:, R_K:R_K + 3], here[:, 7:10]).then_inc(par_set.sem, 1)
                    wait(dve, par_set, turn, 3)
                    for i in range(3):
                        wait(dve, scaled, turn, i + 1)
                        nc.vector.scalar_tensor_tensor(mix[:, i, :], z3[:, i, 0:SEQ], par[:, i:i + 1], mix[:, i, :], ALU.mult, ALU.add).then_inc(mixed.sem, 1)
                    wait(dve, mixed, turn, 3)
                    nc.vector.tensor_scalar(kk[:, :], mix[:, 1, :], par[:, K_K:K_K + 1], None, ALU.mult).then_inc(kk_raw.sem, 1)
                    wait(dve, tanhed, turn, 2)
                    link(nc.vector.tensor_scalar(lw[:, :], lw[:, :], C0, C0, ALU.mult, ALU.add))
                    for j in range(TT):
                        ins = nc.vector.tensor_tensor_scan(Lc[:, tile(j)], lw[:, tile(j)], lw[:, tile(j)], 0.0, ALU.add, ALU.bypass)
                        link(ins)
                    Lv = Lc[:, :].rearrange("p (j c) -> p j c", c=P)
                    link(nc.vector.tensor_scalar(m_half[:, :], Lv[:, :, P - 1:P].rearrange("p j c -> p (j c)"), 0.5, None, ALU.mult))
                    nc.vector.tensor_tensor(m_sum[:, 0:TT - 1], m_half[:, 0:TT - 1], m_half[:, 1:TT], ALU.add).then_inc(cum_set.sem, 1)
                    nc.vector.tensor_tensor(Lv, Lv, m_half[:, :].unsqueeze(2).broadcast_to([P, TT, P]), ALU.subtract).then_inc(cum_set.sem, 1)
                    wait(dve, cum_set, turn, 2)
                    nc.vector.tensor_tensor(La[:, :], Lc[:, :], lw[:, :], ALU.subtract).then_inc(cum_set.sem, 1)
                    wait(dve, tanhed, turn, 4)
                    link(nc.vector.tensor_scalar(ac[:, :], ac[:, :], 0.5, 0.5, ALU.mult, ALU.add))
                    link(nc.vector.tensor_scalar(qk[:, :], ac[:, :], par[:, K_A:K_A + 1], par[:, ONE_M_KA:ONE_M_KA + 1], ALU.mult, ALU.add))
                    link(nc.vector.tensor_tensor(k2[:, :], mix[:, 1, :], qk[:, :], ALU.mult))
                    wait(dve, cum_set, turn, 3)
                    nc.vector.scalar_tensor_tensor(rrk[:, :], mix[:, 0, :], par[:, R_K:R_K + 1], k2[:, :], ALU.mult, ALU.mult).then_inc(bonus_in.sem, 1)
                    wait(dve, summed, turn, 1)
                    nc.vector.tensor_scalar(nrm[:, :], ps[6][:, 0:UNITS], 1e-24, None, ALU.max).then_inc(norm_set.sem, 1)
                    wait(dve, norm_pow, turn, 1)
                    nc.vector.tensor_copy(bv[:, :].rearrange("p (u c) -> p u c", c=HEAD),
                                          rn[:, :].unsqueeze(2).broadcast_to([P, UNITS, HEAD])).then_inc(norm_rep.sem, 1)
                    for i in range(2):
                        wait(dve, norm_wide, turn, i + 1)
                        nc.vector.tensor_tensor(kk[:, half(i)], kk[:, half(i)], ps[6 + i][:, :], ALU.mult).then_inc(kk_set.sem, 1)
                    wait(dve, kk_set, turn, 2)
                    link(nc.vector.tensor_tensor(ac[:, :], ac[:, :], kk[:, :], ALU.mult))
                    wait(dve, exped, turn, 4)
                    t3 = lambda x: x[:, :].rearrange("p (j c) -> p j c", c=P)
                    nc.vector.tensor_tensor(BT[:, :], ac[:, :], Lc[:, :], ALU.mult).then_inc(ops_set.sem, 1)
                    nc.vector.tensor_tensor(KTt[:, :], k2[:, :], Lc[:, :], ALU.mult).then_inc(ops_set.sem, 1)
                    nc.vector.scalar_tensor_tensor(AR[:, :, 0, :], t3(kk), -1.0, t3(La), ALU.mult, ALU.mult).then_inc(ops_set.sem, 1)
                    nc.vector.tensor_tensor(AR[:, :, 1, :], t3(mix[:, 0, :]), t3(ER), ALU.mult).then_inc(ops_set.sem, 1)
                    for i in range(2):
                        wait(dve, bonus_done, turn, i + 1)
                        ins = nc.vector.tensor_tensor(bv[:, half(i)], ps[i][:, :], mix[:, 2, half(i)], ALU.mult)
                        link(ins)
                    for u in range(UNITS):
                        wait(dve, scored, turn, u + 1)
                        dve.sem_inc(seen, 1)
                        nc.vector.copy_predicated(SC[:, u, :, :].rearrange("p a c -> p (a c)"), score_mask[:, :], ps[4 + u % 4][:, :]).then_inc(score_set.sem, 1)
                    for lev in range(LEVELS):
                        for g in range(GROUPS):
                            n = lev * GROUPS + g
                            wait(dve, t_done, turn, n + 1)
                            if g >= 2:
                                if lev:
                                    wait(dve, y_done, turn, n - GROUPS - 1)
                                else:
                                    wait(dve, y_set, turn, n - 1)
                                    wait(dve, x_done, turn, n - 1)
                            dve.sem_inc(seen, 1)
                            nc.vector.copy_predicated(T1[:, lev, g % 2, :], level_mask[:, lev, :, :].rearrange("p u c -> p (u c)"),
                                                      ps[g % 2][:, :]).then_inc(t_set.sem, 1)
                    nc.vector.memset(Ss[:, 0, :], 0.0).then_inc(s_set.sem, 1)
                    def stats(j):
                        wait(dve, out_set, turn, j + 1)
                        for h in range(2):
                            u = 2 * j + h
                            ins = nc.vector.bn_stats(st[:, u, :], ynat[:, j * P + h * HEAD:j * P + (h + 1) * HEAD])
                        ins.then_inc(stat_set.sem, 1)
                        wait(dve, stat_set, turn, j + 1)
                        dve.sem_inc(seen, 1)
                        for h in range(2):
                            u = 2 * j + h
                            ins = nc.vector.bn_aggr(ag[:, u, :], st[:, u, :])
                        ins.then_inc(aggr_set.sem, 1)
                    for j in range(TT):
                        if j < TT - 1:
                            wait(dve, s_done, turn, j + 1)
                            wait(dve, s_set, turn, j + 1)
                            nc.vector.tensor_tensor(Ss[:, (j + 1) % 2, :], Ss[:, j % 2, :], ps[2 + j % 2][:, 0:P], ALU.add)\
                                .then_inc(s_sum.sem, 1)
                            wait(dve, s_sum, turn, j + 1)
                            nc.vector.scalar_tensor_tensor(Ss[:, (j + 1) % 2, :], Ss[:, (j + 1) % 2, :], dec[:, j:j + 1], ones[:, :], ALU.mult, ALU.mult)\
                                .then_inc(s_set.sem, 1)
                        if j:
                            stats(j - 1)
                    stats(TT - 1)
                    wait(dve, aggr_set, turn, TT)
                    nc.vector.tensor_scalar(var[:, :], ag[:, :, 1:2].rearrange("p u c -> p (u c)"), GN_EPS, None, ALU.add).then_inc(var_set.sem, 1)
                    wait(dve, gn_pow, turn, 1)
                    for j in range(TT):
                        for h in range(2):
                            u = 2 * j + h
                            yv = ynat[:, j * P + h * HEAD:j * P + (h + 1) * HEAD]
                            ins = nc.vector.tensor_scalar(yv, yv, ag[:, u, 0:1], rng_[:, u:u + 1], ALU.subtract, ALU.mult)
                        ins.then_inc(gn_set.sem, 1)
                    for i in range(2):
                        wait(dve, affine, turn, i + 1)
                        nc.vector.tensor_tensor(ER[:, half(i)], ER[:, half(i)], bv[:, half(i)], ALU.add).then_inc(plus_bonus.sem, 1)
                        wait(dve, plus_bonus, turn, i + 1)
                        nc.vector.tensor_tensor(gT[:, half(i)], ER[:, half(i)], gT[:, half(i)], ALU.mult).then_inc(y_ready.sem, 1)
                    wait(dve, y_ready, turn, 2)
                    assert steps[0] == dve_step.per_turn, steps[0]
                    dve.sem_inc(turn_over, 1)

            @block.tensor
            def _(pe):
                pe.wait_ge(const_loaded, 16 * 7)
                pe.wait_ge(lora_a, 6)
                pe.wait_ge(lora_v, 8)
                pe.sem_inc(turn_over, 1)
                mm = nc.tensor.matmul
                with pe.Fori(0, PAIRS) as turn:
                    start_turn(pe, turn)
                    wait(pe, pair_loaded, turn, 96)
                    pe.wait_ge(g2_loaded.sem, 16 * turn + 16)
                    for i in range(2):
                        mm(ps[i][:, :], wa_w[0:64, :], wa_act[0:64, half(i)], start=True, stop=True).then_inc(lora_done.sem, 1)
                    for i in range(2):
                        mm(ps[2 + i][:, :], wa_w[64:128, :], wa_act[64:128, half(i)], start=True, stop=True).then_inc(lora_done.sem, 1)
                    for i in range(2):
                        mm(ps[4 + i][:, :], g1_w[:, :], g1_act[:, half(i)], start=True, stop=False)
                        mm(ps[4 + i][:, :], g2_w[:, :], g2_act[:, half(i)], start=False, stop=True).then_inc(lora_done.sem, 1)
                    wait(pe, squared, turn, 1)
                    for j in range(TT):
                        ins = mm(ps[6][:, 2 * j:2 * j + 2], sq[:, tile(j)], sel[:, :], start=True, stop=True)
                    ins.then_inc(summed.sem, 1)
                    wait(pe, bonus_in, turn, 1)
                    wait(pe, tanhed, turn, 2)
                    for i in range(2):
                        mm(ps[i][:, :], ones[:, :], rrk[:, half(i)], start=True, stop=True).then_inc(bonus_done.sem, 1)
                    wait(pe, norm_rep, turn, 1)
                    for i in range(2):
                        for jj in range(4):
                            u = 2 * (4 * i + jj)
                            ins = mm(ps[6 + i][:, tile(jj)], bv[:, u * HEAD:(u + 2) * HEAD], ident[:, :], start=True, stop=True)
                        ins.then_inc(norm_wide.sem, 1)
                    wait(pe, ops_set, turn, 2)
                    wait(pe, tanhed, turn, 4)
                    for j in range(TT):
                        if j >= 2:
                            wait(pe, nat_set, turn, j - 1)
                        for i, src in enumerate((BT[:, tile(j)], KTt[:, tile(j)], mix[:, 2, tile(j)])):
                            ins = nc.tensor.transpose(ps[2 + j % 2][:, tile(i)], src, ident[:, :])
                        ins.then_inc(nat_done.sem, 1)
                    wait(pe, ops_set, turn, 4)
                    wait(pe, gated, turn, 2)
                    wait(pe, kk_set, turn, 2)
                    for j in range(TT):
                        for h in range(2):
                            u = 2 * j + h
                            rows = slice(h * HEAD, (h + 1) * HEAD)
                            bank = ps[4 + u % 4]
                            if u >= 4:
                                wait(pe, score_set, turn, u - 3)
                            mm(bank[:, 0:P], AR[rows, j, 0, :], BT[rows, tile(j)], start=True, stop=True)
                            mm(bank[:, P:2 * P], BT[rows, tile(j)], AR[rows, j, 1, :], start=True, stop=True)
                            mm(bank[:, 2 * P:], KTt[rows, tile(j)], AR[rows, j, :, :].rearrange("p a c -> p (a c)"),
                               start=True, stop=True).then_inc(scored.sem, 1)
                    wait(pe, bonus_done, turn, 2)
                    wait(pe, dve_step, turn, 11 + TT)
                    wait(pe, score_set, turn, UNITS)
                    for lev in range(LEVELS):
                        for g in range(GROUPS):
                            n = lev * GROUPS + g
                            if n >= 2:
                                wait(pe, t_set, turn, n - 1)
                            if lev:
                                wait(pe, y_set, turn, n - GROUPS + 1)
                            for i in range(4):
                                u = 4 * g + i
                                if lev == 0:
                                    ins = nc.tensor.transpose(ps[g % 2][:, tile(i)], SC[:, u, 0, :], ident[:, :])
                                else:
                                    ins = mm(ps[g % 2][:, tile(i)], SC[:, u, 0, :], Y[:, u, :], start=True, stop=True)
                            ins.then_inc(t_done.sem, 1)
                        if lev:
                            for g in range(GROUPS):
                                n = lev * GROUPS + g
                                wait(pe, t_set, turn, n + 1)
                                wait(pe, x_set, turn, n - GROUPS + 1)
                                if g >= 2:
                                    wait(pe, y_set, turn, n - 1)
                                else:
                                    wait(pe, y_set, turn, n - GROUPS + 3)
                                for i in range(4):
                                    u = 4 * g + i
                                    ins = mm(ps[2 + g % 2][:, tile(i)], X[:, u, :], T1[:, lev, g % 2, tile(i)], start=True, stop=True)
                                ins.then_inc(y_done.sem, 1)
                        if lev < LEVELS - 1:
                            for g in range(GROUPS):
                                n = lev * GROUPS + g
                                wait(pe, y_set, turn, n + 1)
                                if n >= 2:
                                    wait(pe, x_set, turn, n - 1)
                                for i in range(4):
                                    u = 4 * g + i
                                    src = T1[:, 0, g % 2, tile(i)] if lev == 0 else Y[:, u, :]
                                    ins = nc.tensor.transpose(ps[4 + g % 2][:, tile(i)], src, ident[:, :])
                                ins.then_inc(x_done.sem, 1)
                    wait(pe, y_set, turn, LEVELS * GROUPS)
                    wait(pe, nat_set, turn, TT)
                    hs = lambda h: slice(h * HEAD, (h + 1) * HEAD)

                    def output(j):
                        if j >= 2:
                            wait(pe, out_set, turn, j - 1)
                        mm(ps[j % 2][:, 0:P], AR[:, j, 1, :], Ss[:, j % 2, :], start=True, stop=False)
                        for h in range(2):
                            u = 2 * j + h
                            o = ps[j % 2][:, hs(h)]
                            mm(o, SC[:, u, 1, :], Un[:, hs(h)], start=False, stop=False)
                            ins = mm(o, SC[:, u, 3, :], nat[:, j, 2, hs(h)], start=False, stop=h == 1)
                        ins.then_inc(out_done.sem, 1)
                    for j in range(TT):
                        wait(pe, s_set, turn, j + 1)
                        mm(ps[6][:, 0:P], AR[:, j, 0, :], Ss[:, j % 2, :], start=True, stop=False)
                        for h in range(2):
                            u = 2 * j + h
                            ins = mm(ps[6][:, hs(h)], SC[:, u, 2, :], nat[:, j, 2, hs(h)], start=False, stop=h == 1)
                        ins.then_inc(rhs_done.sem, 1)
                        wait(pe, rhs_set, turn, j + 1)
                        for h in range(2):
                            ins = mm(ps[7][:, hs(h)], Y[:, 2 * j + h, :], RU[:, hs(h)], start=True, stop=True)
                        ins.then_inc(u_done.sem, 1)
                        wait(pe, u_set, turn, j + 1)
                        if j < TT - 1:
                            mm(ps[2 + j % 2][:, 0:P], nat[:, j, 0, :], Un[:, :], start=True, stop=False)
                            mm(ps[2 + j % 2][:, 0:P], nat[:, j, 1, :], nat[:, j, 2, :], start=False, stop=True).then_inc(s_done.sem, 1)
                        output(j)
                    for i in range(2):
                        wait(pe, gn_set, turn, 4 * i + 4)
                        for jj in range(4):
                            ins = nc.tensor.transpose(ps[4 + i][:, tile(jj)], ynat[:, tile(4 * i + jj)], ident[:, :])
                        ins.then_inc(flipped.sem, 1)
                    wait(pe, affine, turn, 2)
                    pe.sem_inc(turn_over, 1)


KW = 192
Q0 = RWKV_IN
K0, V0 = Q0 + AW, Q0 + AW + KVW
GROUP_PAIRS = 4
SCALE = HEAD ** -0.5
NEVER = -1e30


def attention(nc, zT, sinks_b, bias_tab, ident_d, yT):
    with ExitStack() as ctx:
        sb = lambda n, s, d=F32: ctx.enter_context(nc.sbuf_tensor(n, s, d))
        sem = semaphores(nc, ctx)
        cnt = lambda n, k: Count(sem(n), k)
        ident = sb("ident_c", [P, P])
        sinks = sb("sinks", [P, 2 * PAIRS])
        sink_now = sb("sink_now", [P, 2])
        k2 = [sb(f"kT{g}", [P, HEAD + SEQ]) for g in range(2)]
        vT = sb("vT", [P, HEAD + SEQ])
        v_main, v_prev = sb("v_main", [P, TT, P]), sb("v_prev", [HEAD, TT, P])
        qT = sb("qT", [P, 2, SEQ])
        bias = sb("bias", [P, 2, 2 * KW])
        S = sb("S", [P, 2, 2, KW])
        E = sb("E", [P, 2, 2, KW])
        p_main, p_prev = sb("p_main", [P, 2, 2 * P]), sb("p_prev", [HEAD, 2, 2 * P])
        mx, nmx, es, rs, den, rden = (sb(n, [P, 2, 2]) for n in ("mx", "nmx", "es", "rs", "den", "rden"))
        o_nat = sb("o_nat", [P, 2, P])
        oT = sb("oT", [P, 2, SEQ])
        ps_s = [ctx.enter_context(nc.psum_tensor(f"ps_s{i}", [P, 2, HALF], F32)) for i in range(2)]
        ps_p = [ctx.enter_context(nc.psum_tensor(f"ps_p{i}", [P, HALF], F32)) for i in range(2)]
        ps_o, ps_f = (ctx.enter_context(nc.psum_tensor(n, [P, HALF], F32)) for n in ("ps_o", "ps_f"))
        const_loaded, kv_loaded, pads_set = sem("const_loaded_c"), sem("kv_loaded"), sem("pads_set")
        v_done, v_set = sem("v_done"), sem("v_set")
        q_loaded = [cnt(f"q_loaded{b}", 32) for b in range(2)]
        scored, biased, maxed, neg_set, exped, den_set, rden_set = (
            cnt(n, TT) for n in ("scored_c", "biased", "maxed", "neg_set", "exped_c", "den_set", "rden_set"))
        first_masked, sink_set, sink_max = cnt("first_masked", 1), cnt("sink_set", 1), cnt("sink_max", TT)
        p_done, p_set, o_done, o_set = (cnt(n, TT) for n in ("p_done", "p_set", "o_done", "o_set"))
        f_done, f_set = cnt("f_done", TT), cnt("f_set", 2)
        o_stored = sem("o_stored")
        half = lambda h: slice(h * HALF, (h + 1) * HALF)
        tile = lambda j: slice(j * P, (j + 1) * P)
        hs = lambda h: slice(h * HEAD, (h + 1) * HEAD)

        def wait(eng, c, turn, n):
            eng.wait_ge(c.sem, c.at(turn, n))

        with nc.Block() as block:
            @block.sync
            def _(sp):
                sp.dma_start(ident[:, :], ident_d).then_inc(const_loaded, 16)
                sp.dma_start(sinks[:, :], sinks_b).then_inc(const_loaded, 16)
                for g in range(2):
                    for h in range(2):
                        sp.dma_start(k2[g][hs(h), HEAD:], zT[K0 + g * HEAD:K0 + (g + 1) * HEAD, :]).then_inc(kv_loaded, 16)
                sp.dma_start(vT[:, HEAD:], zT[V0:V0 + KVW, :]).then_inc(kv_loaded, 16)

                def load(pair, b):
                    sp.dma_start(qT[:, b, :], zT[bass.ds(Q0 + pair * P, P), :]).then_inc(q_loaded[b].sem, 16)
                    sp.dma_start(bias[:, b, :], bias_tab[:, bass.ds(pair * 2 * KW, 2 * KW)]).then_inc(q_loaded[b].sem, 16)
                for b in range(2):
                    load(b, b)

                def store(it, b):
                    wait(sp, f_set, 2 * it + b, 2)
                    sp.dma_start(yT[bass.ds(RW + (2 * it + b) * P, P), :], oT[:, b, :]).then_inc(o_stored, 16)
                    sp.wait_ge(o_stored, (2 * it + b + 1) * 16)
                with sp.Fori(0, PAIRS // 2 - 1) as it:
                    for b in range(2):
                        store(it, b)
                        load(2 * it + 2 + b, b)
                for b in range(2):
                    store(PAIRS // 2 - 1, b)

            @block.vector
            def _(dve):
                for t in (*k2, vT):
                    nc.vector.memset(t[:, 0:HEAD], 0.0).then_inc(pads_set, 1)
                nc.vector.memset(oT[:, 0, 0:1], 0.0).then_inc(pads_set, 1)
                dve.wait_ge(const_loaded, 32)
                dve.wait_ge(pads_set, 4)
                with dve.Fori(0, PAIRS // 2) as it:
                    for b in range(2):
                        turn = 2 * it + b
                        wait(dve, q_loaded[b], it, 32)
                        nc.vector.tensor_copy(sink_now[:, :], sinks[:, bass.ds(turn * 2, 2)]).then_inc(sink_set.sem, 1)
                        wait(dve, sink_set, turn, 1)

                        def soften(j):
                            c = j % 2
                            wait(dve, scored, turn, j + 1)
                            if j >= 2:
                                wait(dve, exped, turn, j - 1)
                            nc.vector.scalar_tensor_tensor(S[:, c, :, :], ps_s[c][:, :, 0:KW], SCALE,
                                                           bias[:, b, :].rearrange("p (h k) -> p h k", h=2),
                                                           ALU.mult, ALU.add).then_inc(biased.sem, 1)
                            wait(dve, biased, turn, j + 1)
                            if j == 0:
                                nc.vector.memset(S[0:HEAD, c, :, 0:HEAD], NEVER).then_inc(first_masked.sem, 1)
                                wait(dve, first_masked, turn, 1)
                            nc.vector.tensor_reduce(mx[:, c, :], S[:, c, :, :], AXX, ALU.max).then_inc(maxed.sem, 1)
                            wait(dve, maxed, turn, j + 1)
                            nc.vector.tensor_tensor(mx[:, c, :], mx[:, c, :], sink_now[:, :], ALU.max).then_inc(sink_max.sem, 1)
                            wait(dve, sink_max, turn, j + 1)
                            nc.vector.tensor_scalar(nmx[:, c, :], mx[:, c, :], -1.0, None, ALU.mult).then_inc(neg_set.sem, 1)

                        def finish(j):
                            c = j % 2
                            wait(dve, exped, turn, j + 1)
                            nc.vector.tensor_tensor(den[:, c, :], rs[:, c, :], es[:, c, :], ALU.add).then_inc(den_set.sem, 1)
                            wait(dve, den_set, turn, j + 1)
                            nc.vector.reciprocal(rden[:, c, :], den[:, c, :]).then_inc(rden_set.sem, 1)
                            wait(dve, rden_set, turn, j + 1)
                            wait(dve, o_done, turn, j + 1)
                            if j >= 2:
                                wait(dve, f_done, turn, j - 1)
                            for h in range(2):
                                ins = nc.vector.tensor_scalar(o_nat[:, c, hs(h)], ps_o[:, hs(h)], rden[:, c, h:h + 1], None, ALU.mult)
                            ins.then_inc(o_set.sem, 1)
                        for j in range(TT):
                            soften(j)
                            if j:
                                finish(j - 1)
                        finish(TT - 1)
                        wait(dve, o_set, turn, TT)

            @block.scalar
            def _(act):
                act.wait_ge(const_loaded, 32)
                for j in range(TT):
                    act.wait_ge(v_done, j + 1)
                    nc.scalar.activation(v_main[:, j, :], ps_p[j % 2][:, 0:P], ACT.Copy)
                    nc.scalar.activation(v_prev[:, j, :], ps_p[j % 2][0:HEAD, P:2 * P], ACT.Copy).then_inc(v_set, 1)
                with act.Fori(0, PAIRS // 2) as it:
                    for b in range(2):
                        turn = 2 * it + b

                        def exps(j):
                            c = j % 2
                            wait(act, neg_set, turn, j + 1)
                            if j >= 2:
                                wait(act, p_done, turn, j - 1)
                            for h in range(2):
                                nc.scalar.activation(es[:, c, h:h + 1], sink_now[:, h:h + 1], ACT.Exp, bias=nmx[:, c, h:h + 1])
                                ins = nc.scalar.activation(E[:, c, h, :], S[:, c, h, :], ACT.Exp, bias=nmx[:, c, h:h + 1],
                                                           accum_out=rs[:, c, h:h + 1])
                            ins.then_inc(exped.sem, 1)

                        def copy_p(j):
                            c = j % 2
                            wait(act, p_done, turn, j + 1)
                            if j >= 2:
                                wait(act, o_done, turn, j - 1)
                            nc.scalar.activation(p_main[:, c, :], ps_p[c][:, 0:2 * P], ACT.Copy)
                            nc.scalar.activation(p_prev[:, c, :], ps_p[c][0:HEAD, 2 * P:], ACT.Copy).then_inc(p_set.sem, 1)
                        def copy_out(i):
                            wait(act, f_done, turn, 4 * i + 4)
                            nc.scalar.activation(oT[:, b, half(i)], ps_f[:, :], ACT.Copy).then_inc(f_set.sem, 1)
                        exps(0)
                        for j in range(1, TT):
                            exps(j)
                            copy_p(j - 1)
                            if j == 6:
                                copy_out(0)
                        copy_p(TT - 1)
                        copy_out(1)

            @block.tensor
            def _(pe):
                mm = nc.tensor.matmul
                pe.wait_ge(const_loaded, 32)
                pe.wait_ge(kv_loaded, 16 * 5)
                pe.wait_ge(pads_set, 4)
                for j in range(TT):
                    if j >= 2:
                        pe.wait_ge(v_set, j - 1)
                    nc.tensor.transpose(ps_p[j % 2][:, 0:P], vT[:, HEAD + j * P:HEAD + (j + 1) * P], ident[:, :])
                    nc.tensor.transpose(ps_p[j % 2][0:HEAD, P:2 * P], vT[:, j * P:j * P + HEAD], ident[:, :]).then_inc(v_done, 1)
                pe.wait_ge(v_set, TT)
                for g in range(2):
                    with pe.Fori(g * PAIRS // 4, (g + 1) * PAIRS // 4) as it:
                        for b in range(2):
                            turn = 2 * it + b
                            wait(pe, q_loaded[b], it, 32)

                            def score(j):
                                if j >= 2:
                                    wait(pe, biased, turn, j - 1)
                                for h in range(2):
                                    ins = mm(ps_s[j % 2][:, h, 0:KW], qT[hs(h), b, tile(j)],
                                             k2[g][hs(h), j * P:j * P + KW], start=True, stop=True)
                                ins.then_inc(scored.sem, 1)

                            def flip_p(j):
                                c = j % 2
                                wait(pe, exped, turn, j + 1)
                                if j >= 2:
                                    wait(pe, p_set, turn, j - 1)
                                for h in range(2):
                                    nc.tensor.transpose(ps_p[c][:, tile(h)], E[:, c, h, HEAD:], ident[:, :])
                                for h in range(2):
                                    ins = nc.tensor.transpose(ps_p[c][0:HEAD, tile(2 + h)], E[:, c, h, 0:HEAD], ident[:, :])
                                ins.then_inc(p_done.sem, 1)

                            def weigh(j):
                                c = j % 2
                                wait(pe, p_set, turn, j + 1)
                                if j:
                                    wait(pe, o_set, turn, j)
                                for h in range(2):
                                    mm(ps_o[:, hs(h)], p_main[:, c, tile(h)], v_main[:, j, hs(g)], start=True, stop=False)
                                    ins = mm(ps_o[:, hs(h)], p_prev[:, c, tile(h)], v_prev[:, j, hs(g)], start=False, stop=True)
                                ins.then_inc(o_done.sem, 1)

                            def flip_o(j):
                                wait(pe, o_set, turn, j + 1)
                                if j == 4:
                                    wait(pe, f_set, turn, 1)
                                nc.tensor.transpose(ps_f[:, tile(j % 4)], o_nat[:, j % 2, :], ident[:, :]).then_inc(f_done.sem, 1)
                            score(0)
                            for j in range(TT):
                                if j + 1 < TT:
                                    score(j + 1)
                                flip_p(j)
                                if j:
                                    flip_o(j - 1)
                                weigh(j)
                            flip_o(TT - 1)
                            wait(pe, f_set, turn, 2)


NG, EPG = 4, 8
NE = NG * EPG
TOPK = 2
HID = D // 4
NR = NG + NE
MAX_OVER = SEQ * TOPK // P - 1
BLOCKS = NE + MAX_OVER
NOWHERE = 1 << 14
BIG = 1e30
KQ = 4
CHUNKS = KT // KQ


def project_out(nc, yT, w_out, x, h_all):
    yv = yT.rearrange("(p k) t -> p k t", p=P)
    wv = w_out.rearrange("(p k) n -> p k n", p=P)
    xv = x.rearrange("(t p) d -> p t d", p=P)
    NC = D // HALF
    with ExitStack() as ctx:
        sb = lambda n, s, d=F32: ctx.enter_context(nc.sbuf_tensor(n, s, d))
        sem = semaphores(nc, ctx)
        y_raw = sb("y_raw", [P, 2, KQ, HALF])
        y_hi, y_lo = sb("y_hi", [P, KT, HALF], F32R), sb("y_lo", [P, KT, HALF], F32R)
        raw = sb("wo_raw", [P, 2, KQ, HALF])
        hi, lo = sb("wo_hi", [P, 2, KQ, HALF], F32R), sb("wo_lo", [P, 2, KQ, HALF], F32R)
        ps = [ctx.enter_context(nc.psum_tensor(f"psD{i}", [P, HALF], F32)) for i in range(8)]
        x_loaded = sem("x_loaded_d")
        y_loaded = [sem(f"y_loaded{i}") for i in range(2)]
        w_loaded = [sem(f"wo_loaded{i}") for i in range(2)]
        y_hi_set, y_lo_set = sem("y_hi_set"), sem("y_lo_set")
        hi_set, lo_set, used, added = (sem(n) for n in ("wo_hi_set", "wo_lo_set", "wo_used", "wo_added"))
        TURN = 2 * CHUNKS

        with nc.Block() as block:
            @block.sync
            def _(sp):
                def load_w(it, i):
                    n0 = (2 * it + i // CHUNKS) * HALF
                    k = i % CHUNKS
                    sp.dma_start(raw[:, i % 2, :, :], wv[:, k * KQ:(k + 1) * KQ, bass.ds(n0, HALF)]).then_inc(w_loaded[i % 2], 16)
                for s in range(NH):
                    for c in range(CHUNKS):
                        if s or c >= 2:
                            sp.wait_ge(y_lo_set, s * CHUNKS + c - 1)
                        sp.dma_start(y_raw[:, c % 2, :, :], yv[:, c * KQ:(c + 1) * KQ, s * HALF:(s + 1) * HALF]).then_inc(y_loaded[c % 2], 16)
                    if s == 0:
                        load_w(0, 0)
                        load_w(0, 1)
                        for t in range(TT):
                            sp.dma_start(h_all[:, t, :], xv[:, t, :]).then_inc(x_loaded, 16)
                        first = 2
                    else:
                        first = 0
                    for i in range(first, TURN):
                        sp.wait_ge(lo_set, s * 2 * TURN + i - 1)
                        load_w(0, i)
                    with sp.Fori(1, NC // 2) as it:
                        for i in range(TURN):
                            sp.wait_ge(lo_set, (s * (NC // 2) + it) * TURN + i - 1)
                            load_w(it, i)

            @block.scalar
            def _(act):
                for s in range(NH):
                    for c in range(CHUNKS):
                        n = s * CHUNKS + c
                        act.wait_ge(y_loaded[c % 2], 16 * (n // 2 + 1))
                        if s:
                            act.wait_ge(used, 2 + CHUNKS * NC * s)
                        nc.scalar.activation(y_hi[:, c * KQ:(c + 1) * KQ, :], y_raw[:, c % 2, :, :], ACT.Copy).then_inc(y_hi_set, 1)
                    with act.Fori(0, NC // 2) as it:
                        for i in range(TURN):
                            n = (s * (NC // 2) + it) * TURN + i
                            act.wait_ge(w_loaded[i % 2], ((s * (NC // 2) + it) * (TURN // 2) + i // 2 + 1) * 16)
                            act.wait_ge(used, n + 1)
                            nc.scalar.activation(hi[:, i % 2, :, :], raw[:, i % 2, :, :], ACT.Copy).then_inc(hi_set, 1)

            def residual(dve, s, it, b):
                m = s * NC + 2 * it + b
                dve.wait_ge(x_loaded, 16 * TT)
                dve.wait_ge(used, 2 + CHUNKS * (m + 1))
                for t in range(4):
                    o = h_all[:, 4 * s + t, bass.ds((2 * it + b) * HALF, HALF)]
                    ins = nc.vector.tensor_tensor(o, ps[4 * b + t][:, :], o, ALU.add)
                ins.then_inc(added, 1)

            @block.vector
            def _(dve):
                nc.vector.sem_inc(used, 2)
                nc.vector.sem_inc(added, 2)
                for s in range(NH):
                    for c in range(CHUNKS):
                        n = s * CHUNKS + c
                        dve.wait_ge(y_hi_set, n + 1)
                        ks = slice(c * KQ, (c + 1) * KQ)
                        nc.vector.tensor_tensor(y_lo[:, ks, :], y_raw[:, c % 2, :, :], y_hi[:, ks, :].bitcast(F32), ALU.subtract).then_inc(y_lo_set, 1)
                    with dve.Fori(0, NC // 2) as it:
                        for i in range(TURN):
                            n = (s * (NC // 2) + it) * TURN + i
                            dve.wait_ge(used, n + 1)
                            dve.wait_ge(hi_set, n + 1)
                            nc.vector.tensor_tensor(lo[:, i % 2, :, :], raw[:, i % 2, :, :], hi[:, i % 2, :, :].bitcast(F32), ALU.subtract).then_inc(lo_set, 1)
                            if i % CHUNKS == 0 and i:
                                residual(dve, s, it, 0)
                        residual(dve, s, it, 1)

            @block.tensor
            def _(pe):
                mm = nc.tensor.matmul
                for s in range(NH):
                    pe.wait_ge(y_lo_set, CHUNKS * (s + 1))
                    with pe.Fori(0, NC // 2) as it:
                        for i in range(TURN):
                            b = i // CHUNKS
                            n = (s * (NC // 2) + it) * TURN + i
                            pe.wait_ge(lo_set, n + 1)
                            if i % CHUNKS == 0:
                                pe.wait_ge(added, s * NC + 2 * it + b + 1)
                            for k in range(KQ):
                                kk = (i % CHUNKS) * KQ + k
                                for t in range(4):
                                    ts = slice(t * P, (t + 1) * P)
                                    o = ps[4 * b + t][:, :]
                                    mm(o, y_hi[:, kk, ts], hi[:, i % 2, k, :], start=kk == 0, stop=False)
                                    mm(o, y_hi[:, kk, ts], lo[:, i % 2, k, :], start=False, stop=False)
                                    ins = mm(o, y_lo[:, kk, ts], hi[:, i % 2, k, :], start=False, stop=kk == KT - 1)
                            ins.then_inc(used, 1)


def route(nc, h_all, norm_g, router_w, router_b, consts, xn, table, info):
    ident_d, idx_d, before_d = consts
    with ExitStack() as ctx:
        sb = lambda n, s, d=F32: ctx.enter_context(nc.sbuf_tensor(n, s, d))
        sem = semaphores(nc, ctx)
        ident, before, ones = sb("ident_r", [P, P]), sb("before", [P, P]), sb("ones_r", [P, P])
        idx = sb("idx", [P, 4 + 3 * NE + 2 * MAX_OVER])
        g4, e32, eno = idx[:, 0:4], idx[:, 4:4 + NE], idx[:, 4 + NE:4 + 2 * NE]
        thr = idx[:, 4 + 2 * NE:4 + 2 * NE + MAX_OVER]
        blk = idx[:, 4 + 2 * NE + MAX_OVER:4 + 2 * NE + 2 * MAX_OVER]
        tok = sb("tok", [P, TT, TOPK])
        gb = sb("gb", [P, D])
        rw = sb("rw", [P, KT, NR])
        rb = sb("rb", [P, NR])
        junk = sb("junk_r", [P, D])
        xt = sb("xt_r", [P, 2, D])
        xT = sb("xT_r", [P, 2, KT, P])
        ss, rstd, mh = sb("ss_r", [P, TT]), sb("rstd_r", [P, TT]), sb("mh_r", [P, TT])
        L = sb("L", [P, TT, NR])
        ps_t = [ctx.enter_context(nc.psum_tensor(f"ps_t{i}", [P, HALF], F32)) for i in range(4)]
        ps_l = ctx.enter_context(nc.psum_tensor("ps_l", [P, TT, NR], F32))
        ps_r, ps_c = ctx.enter_context(nc.psum_tensor("ps_r", [P, TT, NE], F32)), ctx.enter_context(nc.psum_tensor("ps_c", [P, NE], F32))
        loaded, squared, mean_set, rstd_set, xn_set = (sem(n) for n in ("loaded_r", "squared_r", "mean_r", "rstd_set_r", "xn_set"))
        stored = [sem(f"xn_stored{i}") for i in range(2)]
        flipped, copied, logits, ones_set = sem("flipped_r"), sem("copied_r"), sem("logits_r"), sem("ones_set_r")
        chain, exp_in, exp_out = sem("route_step"), sem("exp_in"), sem("exp_out")
        ranks_in, ranks_out, slots_set = sem("ranks_in"), sem("ranks_out"), sem("slots_set")
        filled, scattered, info_stored = sem("table_filled"), sem("scattered"), sem("info_stored")
        fill_set = sem("fill_set")
        slot_i = sb("slot_i", [P, TT, TOPK], I32)
        entry = sb("entry", [P, TT, TOPK, 3], I32)
        empty = sb("empty", [P, BLOCKS, 3], I32)
        info_i = sb("info_i", [P, MAX_OVER + 1], I32)
        a4 = lambda n: sb(n, [P, TT, NG])
        a32 = lambda n: sb(n, [P, TT, NG, EPG])
        gm, es_, pg, v1, v2, m1, ev, w1, w2 = (sb(n, [P, TT]) for n in ("gm", "es_r", "pg", "v1", "v2", "m1", "ev", "w1", "w2"))
        gsub, goh = a4("gsub"), a4("goh")
        el, oh1, oh2, tmp, O, Opre = (a32(n) for n in ("el", "oh1", "oh2", "tmp_r", "O", "Opre"))
        cnt_e, over_e, cum, over_start = (sb(n, [P, NE]) for n in ("cnt_e", "over_e", "cum_e", "over_start"))
        th = sb("th", [P, NE, MAX_OVER])
        rank = sb("rank", [P, TT, NE])
        rk, en, ov, slot = (sb(n, [P, TT, TOPK]) for n in ("rk", "en", "ov", "slot_f"))
        info_f = sb("info_f", [P, MAX_OVER + 1])
        bh = sb("bh", [P, MAX_OVER, NE])

        with nc.Block() as block:
            @block.sync
            def _(sp):
                for o, i in ((ident[:, :], ident_d), (idx[:, :], idx_d), (before[:, :], before_d), (gb[:, :], norm_g),
                             (rw[:, :, :], router_w), (rb[:, :], router_b)):
                    sp.dma_start(o, i).then_inc(loaded, 16)
                sp.wait_ge(fill_set, 3)
                sp.dma_start(table.rearrange("(b p) c -> p b c", p=P), empty[:, :, :]).then_inc(filled, 16)
                for t in range(TT):
                    sp.wait_ge(xn_set, t + 1)
                    sp.dma_start(xn[t * P:(t + 1) * P, :], xt[:, t % 2, :]).then_inc(stored[t % 2], 16)
                for i in range(2):
                    sp.wait_ge(stored[i], 16 * (TT // 2))
                sp.wait_ge(slots_set, 4)
                sp.dma_start(info, info_i[0:1, :]).then_inc(info_stored, 16)
                sp.wait_ge(info_stored, 16)

            @block.gpsimd
            def _(pool):
                nc.gpsimd.memset(ones[:, :], 1.0).then_inc(ones_set, 1)
                nc.gpsimd.memset(mh[:, :], -0.5).then_inc(ones_set, 1)
                nc.gpsimd.memset(empty[:, :, 0:2], NOWHERE).then_inc(fill_set, 1)
                nc.gpsimd.memset(empty[:, :, 2:3], 0).then_inc(fill_set, 1)
                nc.gpsimd.iota(tok[:, :, :], [[P, TT], [0, TOPK]], base=0, channel_multiplier=1,
                               allow_small_or_imprecise_dtypes=True).then_inc(fill_set, 1)
                pool.wait_ge(ones_set, 2)
                for t in range(TT):
                    pool.wait_ge(mean_set, t + 1)
                    nc.gpsimd.tensor_tensor(rstd[:, t:t + 1], ss[:, t:t + 1], mh[:, t:t + 1], ALU.pow).then_inc(rstd_set, 1)
                pool.wait_ge(slots_set, 4)
                pool.wait_ge(filled, 16)
                for t in range(TT):
                    for c in range(TOPK):
                        pool.indirect_dma_start(table[:, :], bass.IndirectOffsetOnAxis(ap=slot_i[:, t, c:c + 1].bitcast(U32), axis=0),
                                                entry[:, t, c, :], None).then_inc(scattered, 16)
                pool.wait_ge(scattered, 16 * TT * TOPK)

            def copies(act, t):
                for q in range(4):
                    act.wait_ge(flipped, 4 * t + q + 1)
                    if t >= 2:
                        act.wait_ge(logits, t - 1)
                    nc.scalar.activation(xT[:, t % 2, 4 * q:4 * q + 4, :].rearrange("p k c -> p (k c)"), ps_t[q][:, :], ACT.Copy).then_inc(copied, 1)

            @block.scalar
            def _(act):
                for t in range(TT):
                    if t:
                        act.wait_ge(squared, t)
                    nc.scalar.activation(junk[:, :], h_all[:, t, :], ACT.Square, accum_out=ss[:, t:t + 1]).then_inc(squared, 1)
                    if t:
                        copies(act, t - 1)
                copies(act, TT - 1)
                for i, (o, n) in enumerate(((gsub, None), (ev, None))):
                    act.wait_ge(exp_in, i + 1)
                    nc.scalar.activation(o[...], o[...], ACT.Exp).then_inc(exp_out, 1)

            @block.tensor
            def _(pe):
                pe.wait_ge(loaded, 96)
                for t in range(TT):
                    pe.wait_ge(xn_set, t + 1)
                    for q in range(4):
                        if t:
                            pe.wait_ge(copied, 4 * (t - 1) + q + 1)
                        for i in range(4):
                            k = 4 * q + i
                            ins = nc.tensor.transpose(ps_t[q][:, i * P:(i + 1) * P], xt[:, t % 2, k * P:(k + 1) * P], ident[:, :])
                        ins.then_inc(flipped, 1)
                    pe.wait_ge(copied, 4 * t + 4)
                    for k in range(KT):
                        ins = nc.tensor.matmul(ps_l[:, t, :], xT[:, t % 2, k, :], rw[:, k, :], start=k == 0, stop=k == KT - 1)
                    ins.then_inc(logits, 1)
                pe.wait_ge(ranks_in, 2)
                pe.wait_ge(ones_set, 2)
                fl = lambda a: a[...].rearrange("p t g e -> p (t g e)")
                psr = ps_r[...].rearrange("p t e -> p (t e)")
                nc.tensor.matmul(psr, before[:, :], fl(O), start=True, stop=False)
                nc.tensor.matmul(psr, ones[:, :], fl(Opre), start=False, stop=True).then_inc(ranks_out, 1)
                nc.tensor.matmul(ps_c[:, :], ones[:, :], Opre[:, TT - 1, :, :].rearrange("p g e -> p (g e)"), start=True, stop=False)
                nc.tensor.matmul(ps_c[:, :], ones[:, :], O[:, TT - 1, :, :].rearrange("p g e -> p (g e)"), start=False, stop=True).then_inc(ranks_out, 1)

            @block.vector
            def _(dve):
                v = nc.vector
                n = [0]

                def link(ins):
                    n[0] += 1
                    ins.then_inc(chain, 1)
                    dve.wait_ge(chain, n[0])
                dve.wait_ge(loaded, 96)
                for t in range(TT):
                    dve.wait_ge(squared, t + 1)
                    v.tensor_scalar(ss[:, t:t + 1], ss[:, t:t + 1], 1.0 / D, RMS_EPS, ALU.mult, ALU.add).then_inc(mean_set, 1)
                    dve.wait_ge(rstd_set, t + 1)
                    if t >= 2:
                        dve.wait_ge(stored[t % 2], 16 * (t // 2))
                        dve.wait_ge(flipped, 4 * (t - 1))
                    v.scalar_tensor_tensor(xt[:, t % 2, :], h_all[:, t, :], rstd[:, t:t + 1], gb[:, :], ALU.mult, ALU.mult).then_inc(xn_set, 1)
                dve.wait_ge(logits, TT)
                b3 = lambda a, k: a.unsqueeze(2).broadcast_to([P, TT, k])
                link(v.tensor_tensor(L[:, :, :], ps_l[:, :, :], rb[:, :].unsqueeze(1).broadcast_to([P, TT, NR]), ALU.add))
                gl = L[:, :, 0:NG]
                link(v.tensor_reduce(gm[:, :], gl, AXX, ALU.max))
                v.tensor_tensor(gsub[:, :, :], gl, b3(gm[:, :], NG), ALU.subtract).then_inc(exp_in, 1)
                link(v.tensor_tensor(goh[:, :, :], gl, b3(gm[:, :], NG), ALU.is_ge))
                link(v.tensor_tensor(goh[:, :, :], goh[:, :, :], g4.unsqueeze(1).broadcast_to([P, TT, NG]), ALU.mult))
                link(v.tensor_reduce(m1[:, :], goh[:, :, :], AXX, ALU.max))
                link(v.tensor_tensor(goh[:, :, :], goh[:, :, :], b3(m1[:, :], NG), ALU.is_equal))
                dve.wait_ge(exp_out, 1)
                link(v.tensor_reduce(es_[:, :], gsub[:, :, :], AXX, ALU.add))
                link(v.reciprocal(pg[:, :], es_[:, :]))
                link(v.tensor_scalar(goh[:, :, :], goh[:, :, :], BIG, -BIG, ALU.mult, ALU.add))
                f = lambda a: a[...].rearrange("p t g e -> p t (g e)")
                link(v.tensor_copy(el[...].rearrange("p t g e -> p (t g) e"), goh[...].rearrange("p t g -> p (t g)").unsqueeze(2).broadcast_to([P, TT * NG, EPG])))
                link(v.tensor_tensor(f(el), f(el), L[:, :, NG:], ALU.add))

                def first_of_largest(oh, top):
                    link(v.tensor_reduce(top[:, :], f(el), AXX, ALU.max))
                    link(v.tensor_tensor(f(oh), f(el), b3(top[:, :], NE), ALU.is_ge))
                    link(v.tensor_tensor(f(oh), f(oh), e32.unsqueeze(1).broadcast_to([P, TT, NE]), ALU.mult))
                    link(v.tensor_reduce(m1[:, :], f(oh), AXX, ALU.max))
                    link(v.tensor_tensor(f(oh), f(oh), b3(m1[:, :], NE), ALU.is_equal))
                first_of_largest(oh1, v1)
                link(v.scalar_tensor_tensor(f(el), f(oh1), -10.0 * BIG, f(el), ALU.mult, ALU.add))
                first_of_largest(oh2, v2)
                v.tensor_tensor(ev[:, :], v2[:, :], v1[:, :], ALU.subtract).then_inc(exp_in, 1)
                link(v.tensor_tensor(f(O), f(oh1), f(oh2), ALU.add))
                link(v.memset(Opre[:, 0, :, :], 0.0))
                for t in range(1, TT):
                    link(v.tensor_tensor(Opre[:, t, :, :], Opre[:, t - 1, :, :], O[:, t - 1, :, :], ALU.add))
                v.sem_inc(ranks_in, 2)
                dve.wait_ge(exp_out, 2)
                link(v.tensor_scalar(w2[:, :], ev[:, :], 1.0, None, ALU.add))
                link(v.reciprocal(w1[:, :], w2[:, :]))
                link(v.tensor_tensor(w1[:, :], w1[:, :], pg[:, :], ALU.mult))
                link(v.tensor_tensor(w2[:, :], w1[:, :], ev[:, :], ALU.mult))
                dve.wait_ge(ranks_out, 2)
                link(v.tensor_copy(cnt_e[:, :], ps_c[:, :]))
                link(v.tensor_copy(rank[:, :, :], ps_r[:, :, :]))
                link(v.tensor_tensor(th[:, :, :], cnt_e[:, :].unsqueeze(2).broadcast_to([P, NE, MAX_OVER]),
                                     thr.unsqueeze(1).broadcast_to([P, NE, MAX_OVER]), ALU.is_gt))
                link(v.tensor_reduce(over_e[:, :], th[:, :, :], AXX, ALU.add))
                link(v.tensor_tensor_scan(cum[:, :], over_e[:, :], over_e[:, :], 0.0, ALU.add, ALU.bypass))
                link(v.tensor_tensor(over_start[:, :], cum[:, :], over_e[:, :], ALU.subtract))
                link(v.tensor_tensor(bh[:, :, :], cum[:, :].unsqueeze(1).broadcast_to([P, MAX_OVER, NE]),
                                     blk.unsqueeze(2).broadcast_to([P, MAX_OVER, NE]), ALU.is_le))
                link(v.tensor_reduce(info_f[:, 0:MAX_OVER], bh[:, :, :], AXX, ALU.add))
                link(v.tensor_scalar(info_f[:, 0:MAX_OVER], info_f[:, 0:MAX_OVER], float(NE - 1), None, ALU.min))
                link(v.tensor_copy(info_f[:, MAX_OVER:], cum[:, NE - 1:NE]))
                v.tensor_copy(info_i[:, :], info_f[:, :]).then_inc(slots_set, 1)
                for c, oh in enumerate((oh1, oh2)):
                    for o, col in ((rk, None), (en, eno), (ov, over_start[:, :])):
                        other = rank[:, :, :] if col is None else col.unsqueeze(1).broadcast_to([P, TT, NE])
                        link(v.tensor_tensor(f(tmp), f(oh), other, ALU.mult))
                        link(v.tensor_reduce(o[:, :, c:c + 1], f(tmp), AXX, ALU.add))
                fl = lambda a: a[...].rearrange("p t c -> p (t c)")
                link(v.tensor_tensor(fl(ov), fl(ov), fl(en), ALU.subtract))
                link(v.tensor_scalar(fl(ov), fl(ov), float(P), float(P * NE - P), ALU.mult, ALU.add))
                link(v.scalar_tensor_tensor(fl(ov), fl(rk), float(P), fl(ov), ALU.is_ge, ALU.mult))
                link(v.scalar_tensor_tensor(fl(slot), fl(en), float(P), fl(rk), ALU.mult, ALU.add))
                link(v.tensor_tensor(fl(slot), fl(slot), fl(ov), ALU.add))
                v.tensor_copy(slot_i[:, :, :], slot[:, :, :]).then_inc(slots_set, 1)
                dve.wait_ge(fill_set, 3)
                link(v.tensor_copy(entry[:, :, :, 0], tok[:, :, :]))
                link(v.tensor_scalar(rk[:, :, :], tok[:, :, :], 2.0, None, ALU.mult))
                link(v.tensor_scalar(rk[:, :, 1:2], rk[:, :, 1:2], 1.0, None, ALU.add))
                v.tensor_copy(entry[:, :, :, 1], rk[:, :, :]).then_inc(slots_set, 1)
                link(v.tensor_copy(entry[:, :, 0, 2].bitcast(F32), w1[:, :]))
                v.tensor_copy(entry[:, :, 1, 2].bitcast(F32), w2[:, :]).then_inc(slots_set, 1)


RAWS, SPLITS = 4, 3
GC, DC = CHUNKS, HID // P
PER = 2 * GC + DC
NB = D // HALF
XR = KT // KQ


def experts(nc, xn, table, w_gate, w_up, w_down, ident_d, yk):
    gv = w_gate.rearrange("e (p k) h -> e p k h", p=P)
    uv = w_up.rearrange("e (p k) h -> e p k h", p=P)
    dv = w_down.rearrange("e (p k) n -> e p k n", p=P)
    with ExitStack() as ctx:
        sb = lambda n, s, d=F32: ctx.enter_context(nc.sbuf_tensor(n, s, d))
        sem = semaphores(nc, ctx)
        ident = sb("ident_e", [P, P])
        slots = sb("slots", [P, BLOCKS, 3], I32)
        raw = sb("raw", [P, RAWS, 4 * HALF])
        hi, lo = sb("w_hi_e", [P, SPLITS, 4 * HALF], F32R), sb("w_lo_e", [P, SPLITS, 4 * HALF], F32R)
        xg = sb("xg", [P, D])
        xT_hi, xT_lo = sb("xT_hi", [P, KT, P], F32R), sb("xT_lo", [P, KT, P], F32R)
        gidx, sidx, sw = sb("gidx", [P, 1], I32), sb("sidx", [P, 1], I32), sb("sw", [P, 1], I32)
        th, hid = sb("th_e", [P, HID]), sb("hid", [P, HID])
        hT_hi, hT_lo = sb("hT_hi", [P, DC, P], F32R), sb("hT_lo", [P, DC, P], F32R)
        y_sb = sb("y_sb", [P, D])
        ps_g, ps_u = (ctx.enter_context(nc.psum_tensor(n, [P, HALF], F32)) for n in ("ps_g", "ps_u"))
        ps_x = [ctx.enter_context(nc.psum_tensor(f"ps_x{i}", [P, HALF], F32)) for i in range(2)]
        ps_y = [ctx.enter_context(nc.psum_tensor(f"ps_y{i}", [P, HALF], F32)) for i in range(NB)]

        const_loaded, slots_loaded, cleared = sem("const_loaded_e"), sem("slots_loaded"), sem("cleared")
        w_loaded = [sem(f"w_loaded_e{i}") for i in range(RAWS)]
        seen = sem("seen_e")
        hi_set, lo_set, used = sem("hi_set_e"), sem("lo_set_e"), sem("used_e")
        gidx_set, sidx_set, gathered, scattered = sem("gidx_set"), sem("sidx_set"), sem("gathered"), sem("scattered_e")
        x_flip, x_hi, x_lo = sem("x_flip"), sem("x_hi"), sem("x_lo")
        tanh_set, act_set, hid_set = sem("tanh_set"), sem("act_set"), sem("hid_set")
        h_flip, h_hi, h_lo = sem("h_flip"), sem("h_hi"), sem("h_lo")
        y_set = sem("y_set_e")
        chunk = lambda e, i: 2 * GC + PER * (e - 1) + i
        TAIL = chunk(NE, 0)
        y_done = lambda e: chunk(e + 2, 0)
        raw_slot = lambda i: i % RAWS
        split_slot = lambda i: (i + 2 * GC) % SPLITS
        fills = lambda e, i: 2 * GC // RAWS + PER // RAWS * (e - 1) + i // RAWS + 1
        flat = lambda a: a.rearrange("p k c -> p (k c)")
        assert 2 * GC % RAWS == 0 and PER % RAWS == 0 and PER % SPLITS == 0

        with nc.Block() as block:
            @block.sync
            def _(sp):
                sp.dma_start(ident[:, :], ident_d).then_inc(const_loaded, 16)
                sp.dma_start(slots[:, :, :], table.rearrange("(b p) c -> p b c", p=P)).then_inc(slots_loaded, 16)

                def load(e, i, n, s, free):
                    if free:
                        sp.wait_ge(lo_set, n - RAWS + 1)
                    if i < 2 * GC:
                        v = (gv, uv)[i // GC]
                        src = v[bass.ds(e, 1), :, (i % GC) * KQ:(i % GC + 1) * KQ, :].rearrange("a p k h -> (a p) (k h)")
                    else:
                        src = dv[bass.ds(e, 1), :, i - 2 * GC, :].rearrange("a p n -> (a p) n")
                    sp.dma_start(raw[:, s, :], src).then_inc(w_loaded[s], 16)
                for i in range(2 * GC):
                    load(0, i, i, raw_slot(i), i >= RAWS)
                with sp.Fori(1, NE) as e:
                    for i in range(PER):
                        load(e if i < 2 * GC else e - 1, i, chunk(e, i), raw_slot(i), True)
                for i in range(DC):
                    load(NE - 1, 2 * GC + i, TAIL + i, raw_slot(i), True)

            @block.gpsimd
            def _(pool):
                def gather(e, free):
                    if free:
                        pool.wait_ge(x_flip, XR * e)
                        pool.wait_ge(gathered, 16 * e)
                    nc.gpsimd.tensor_copy(gidx[:, :], slots[:, bass.ds(e, 1), 0]).then_inc(gidx_set, 1)
                    pool.wait_ge(gidx_set, e + 1)
                    pool.sem_inc(seen, 1)
                    pool.indirect_dma_start(xg[:, :], None, xn[:, :], bass.IndirectOffsetOnAxis(ap=gidx[:, :].bitcast(U32), axis=0),
                                            bounds_check=SEQ - 1, oob_is_err=False).then_inc(gathered, 16)

                def scatter(e, free):
                    if free:
                        pool.wait_ge(scattered, 16 * e)
                        pool.wait_ge(y_set, NB * e)
                    nc.gpsimd.tensor_copy(sidx[:, :], slots[:, bass.ds(e, 1), 1])
                    nc.gpsimd.tensor_copy(sw[:, :], slots[:, bass.ds(e, 1), 2]).then_inc(sidx_set, 1)
                    pool.wait_ge(sidx_set, e + 1)
                    pool.wait_ge(y_set, NB * (e + 1))
                    pool.sem_inc(seen, 1)
                    pool.indirect_dma_start(yk[:, :], bass.IndirectOffsetOnAxis(ap=sidx[:, :].bitcast(U32), axis=0), y_sb[:, :], None,
                                            bounds_check=TOPK * SEQ - 1, oob_is_err=False).then_inc(scattered, 16)
                nc.gpsimd.memset(xg[:, :], 0.0).then_inc(cleared, 1)
                pool.wait_ge(cleared, 1)
                pool.wait_ge(slots_loaded, 16)
                gather(0, False)
                gather(1, True)
                gather(2, True)
                scatter(0, False)
                with pool.Fori(3, NE) as e:
                    gather(e, True)
                    scatter(e - 2, True)
                scatter(NE - 2, True)
                scatter(NE - 1, True)
                pool.wait_ge(scattered, 16 * NE)

            def split_hi(act, i, n, s, filled, free=True):
                act.wait_ge(w_loaded[i % RAWS], 16 * filled)
                if free:
                    act.wait_ge(used, n - SPLITS + 1)
                nc.scalar.activation(hi[:, s, :], raw[:, i % RAWS, :], ACT.Copy).then_inc(hi_set, 1)

            def x_to_hi(act, e, q):
                act.wait_ge(x_flip, XR * e + q + 1)
                nc.scalar.activation(flat(xT_hi[:, KQ * q:KQ * (q + 1), :]), ps_x[q % 2][:, :], ACT.Copy).then_inc(x_hi, 1)

            def h_to_hi(act, count):
                act.wait_ge(h_flip, count)
                nc.scalar.activation(flat(hT_hi[:, :, :]), ps_x[0][:, :], ACT.Copy).then_inc(h_hi, 1)

            def tanh(act, e, first=False):
                if not first:
                    act.wait_ge(hid_set, e)
                nc.scalar.activation(th[:, :], ps_g[:, :], ACT.Tanh, scale=0.5).then_inc(tanh_set, 1)

            def y_out(act, e, products):
                act.wait_ge(used, products)
                act.wait_ge(sidx_set, e + 1)
                for b in range(NB):
                    nc.scalar.activation(y_sb[:, b * HALF:(b + 1) * HALF], ps_y[b][:, :], ACT.Copy, scale=sw[:, :].bitcast(F32)).then_inc(y_set, 1)

            def scalar_turn(act, e, first=False, last=False):
                for i in range(PER):
                    split_hi(act, i, chunk(e, i), split_slot(i), fills(e, i))
                    if i in (0, 1):
                        x_to_hi(act, e, i + 2)
                    if i == 2 and not first:
                        y_out(act, e - 2, y_done(e - 2))
                    if i == GC + SPLITS - 1:
                        h_to_hi(act, e)
                    if i == 2 * GC - 1:
                        tanh(act, e)
                    if i in (PER - 2, PER - 1) and not last:
                        x_to_hi(act, e + 1, i - (PER - 2))

            @block.scalar
            def _(act):
                for i in range(2 * GC):
                    split_hi(act, i, i, i % SPLITS, i // RAWS + 1, i >= SPLITS)
                    if i == SPLITS - 1:
                        for q in range(XR):
                            x_to_hi(act, 0, q)
                    if i == GC + SPLITS - 1:
                        tanh(act, 0, first=True)
                for q in range(2):
                    x_to_hi(act, 1, q)
                scalar_turn(act, 1, first=True)
                with act.Fori(2, NE - 1) as e:
                    scalar_turn(act, e)
                scalar_turn(act, NE - 1, last=True)
                for i in range(DC):
                    split_hi(act, i, TAIL + i, split_slot(i), fills(NE, i))
                    if i == 0:
                        h_to_hi(act, NE)
                    if i == 2:
                        y_out(act, NE - 2, y_done(NE - 2))
                y_out(act, NE - 1, TAIL + DC)

            def split_lo(dve, i, n, s):
                dve.wait_ge(hi_set, n + 1)
                nc.vector.tensor_tensor(lo[:, s, :], raw[:, i % RAWS, :], hi[:, s, :].bitcast(F32), ALU.subtract).then_inc(lo_set, 1)

            def x_to_lo(dve, e, q):
                dve.wait_ge(x_hi, XR * e + q + 1)
                ks = slice(KQ * q, KQ * (q + 1))
                nc.vector.tensor_tensor(flat(xT_lo[:, ks, :]), ps_x[q % 2][:, :], flat(xT_hi[:, ks, :]).bitcast(F32), ALU.subtract).then_inc(x_lo, 1)

            def h_to_lo(dve, count):
                dve.wait_ge(h_hi, count)
                nc.vector.tensor_tensor(flat(hT_lo[:, :, :]), ps_x[0][:, :], flat(hT_hi[:, :, :]).bitcast(F32), ALU.subtract).then_inc(h_lo, 1)

            def swiglu(dve, e, products, first=False):
                dve.wait_ge(used, products)
                dve.wait_ge(tanh_set, e + 1)
                if not first:
                    dve.wait_ge(h_flip, e)
                nc.vector.scalar_tensor_tensor(hid[:, :], th[:, :], 1.0, ps_g[:, :], ALU.add, ALU.mult).then_inc(act_set, 1)
                dve.wait_ge(act_set, e + 1)
                nc.vector.scalar_tensor_tensor(hid[:, :], hid[:, :], 0.5, ps_u[:, :], ALU.mult, ALU.mult).then_inc(hid_set, 1)

            def vector_turn(dve, e, last=False):
                for i in range(PER):
                    split_lo(dve, i, chunk(e, i), split_slot(i))
                    if i in (0, 1):
                        x_to_lo(dve, e, i + 2)
                    if i == GC + SPLITS - 1:
                        h_to_lo(dve, e)
                    if i in (PER - 2, PER - 1) and not last:
                        x_to_lo(dve, e + 1, i - (PER - 2))
                    if i == PER - 2:
                        swiglu(dve, e, chunk(e, 2 * GC))

            @block.vector
            def _(dve):
                for i in range(2 * GC):
                    split_lo(dve, i, i, i % SPLITS)
                    if i == SPLITS - 1:
                        for q in range(XR):
                            x_to_lo(dve, 0, q)
                swiglu(dve, 0, 2 * GC, first=True)
                for q in range(2):
                    x_to_lo(dve, 1, q)
                with dve.Fori(1, NE - 1) as e:
                    vector_turn(dve, e)
                vector_turn(dve, NE - 1, last=True)
                for i in range(DC):
                    split_lo(dve, i, TAIL + i, split_slot(i))
                    if i == 0:
                        h_to_lo(dve, NE)

            def three(o, a_hi, a_lo, s, cols, start, stop):
                mm = nc.tensor.matmul
                mm(o, a_hi, hi[:, s, cols], start=start, stop=False)
                mm(o, a_hi, lo[:, s, cols], start=False, stop=False)
                return mm(o, a_lo, hi[:, s, cols], start=False, stop=stop)

            def flip_x(pe, e, q):
                if q == 0:
                    pe.wait_ge(gathered, 16 * (e + 1))
                if not (isinstance(e, int) and e == 0 and q < 2):
                    pe.wait_ge(x_lo, XR * e + q - 1)
                for j in range(KQ):
                    ins = nc.tensor.transpose(ps_x[q % 2][:, j * P:(j + 1) * P], xg[:, KQ * q + j::KT], ident[:, :])
                ins.then_inc(x_flip, 1)

            def flip_hid(pe, count):
                pe.wait_ge(hid_set, count)
                for j in range(DC):
                    ins = nc.tensor.transpose(ps_x[0][:, j * P:(j + 1) * P], hid[:, j::DC], ident[:, :])
                ins.then_inc(h_flip, 1)

            def gate_up(pe, e, i, n, s):
                if i < GC:
                    pe.wait_ge(x_lo, XR * e + i + 1)
                pe.wait_ge(lo_set, n + 1)
                o = (ps_g, ps_u)[i // GC][:, :]
                for j in range(KQ):
                    k = (i % GC) * KQ + j
                    ins = three(o, xT_hi[:, k, :], xT_lo[:, k, :], s, slice(j * HALF, (j + 1) * HALF), k == 0, k == KT - 1)
                ins.then_inc(used, 1)

            def down(pe, q, n, s):
                pe.wait_ge(lo_set, n + 1)
                for b in range(NB):
                    ins = three(ps_y[b][:, :], hT_hi[:, q, :], hT_lo[:, q, :], s, slice(b * HALF, (b + 1) * HALF), q == 0, q == DC - 1)
                ins.then_inc(used, 1)

            def tensor_turn(pe, e, first=False, last=False):
                pe.wait_ge(hid_set, e)
                for i in range(2 * GC):
                    gate_up(pe, e, i, chunk(e, i), split_slot(i))
                    if i == GC - 1:
                        flip_hid(pe, e)
                pe.wait_ge(h_lo, e)
                for q in range(DC):
                    if not last:
                        flip_x(pe, e + 1, q)
                    if q == 0 and not first:
                        pe.wait_ge(y_set, NB * (e - 1))
                    down(pe, q, chunk(e, 2 * GC + q), split_slot(2 * GC + q))

            @block.tensor
            def _(pe):
                pe.wait_ge(const_loaded, 16)
                pe.wait_ge(cleared, 1)
                for q in range(XR):
                    flip_x(pe, 0, q)
                for i in range(2 * GC):
                    gate_up(pe, 0, i, i, i % SPLITS)
                for q in range(XR):
                    flip_x(pe, 1, q)
                tensor_turn(pe, 1, first=True)
                with pe.Fori(2, NE - 1) as e:
                    tensor_turn(pe, e)
                tensor_turn(pe, NE - 1, last=True)
                flip_hid(pe, NE)
                pe.wait_ge(h_lo, NE)
                pe.wait_ge(y_set, NB * (NE - 1))
                for q in range(DC):
                    down(pe, q, TAIL + q, split_slot(q))


def experts_over(nc, xn, table, info, w_gate, w_up, w_down, ident_d, yk):
    gv = w_gate.rearrange("e (p k) h -> e p k h", p=P)
    uv = w_up.rearrange("e (p k) h -> e p k h", p=P)
    dv = w_down.rearrange("e (p k) n -> e p k n", p=P)
    with ExitStack() as ctx:
        sb = lambda n, s, d=F32: ctx.enter_context(nc.sbuf_tensor(n, s, d))
        sem = semaphores(nc, ctx)
        ident = sb("ident_o", [P, P])
        slots = sb("slots_o", [P, MAX_OVER, 3], I32)
        infos = sb("infos", [1, MAX_OVER + 1], I32)
        w = sb("w_o", [P, RAWS, 4 * HALF])
        xg, y_sb = sb("xg_o", [P, D]), sb("y_sb_o", [P, D])
        xT, hT = sb("xT_o", [P, KT, P]), sb("hT_o", [P, DC, P])
        th, hid = sb("th_o", [P, HID]), sb("hid_o", [P, HID])
        gidx, sidx, sw = sb("gidx_o", [P, 1], I32), sb("sidx_o", [P, 1], I32), sb("sw_o", [P, 1], I32)
        ps_g, ps_u, ps_h = (ctx.enter_context(nc.psum_tensor(n, [P, HALF], F32)) for n in ("ps_go", "ps_uo", "ps_ho"))
        ps_y = [ctx.enter_context(nc.psum_tensor(f"ps_yo{i}", [P, HALF], F32)) for i in range(NB)]
        loaded, slots_loaded, cleared = sem("loaded_o"), sem("slots_loaded_o"), sem("cleared_o")
        w_loaded = [sem(f"w_loaded_o{i}") for i in range(RAWS)]
        seen, blocks_done = sem("seen_o"), sem("blocks_done")
        picked, gathered, scattered, used = sem("picked_o"), sem("gathered_o"), sem("scattered_o"), sem("used_o")
        x_flip, x_set, h_flip, h_set = sem("x_flip_o"), sem("x_set_o"), sem("h_flip_o"), sem("h_set_o")
        tanh_set, act_set, hid_set, y_set = sem("tanh_o"), sem("act_o"), sem("hid_set_o"), sem("y_set_o")
        flat = lambda a: a.rearrange("p k c -> p (k c)")

        with nc.Block() as block:
            @block.sync
            def _(sp):
                sp.dma_start(infos[:, :], info).then_inc(loaded, 16)
                sp.dma_start(ident[:, :], ident_d).then_inc(loaded, 16)
                sp.dma_start(slots[:, :, :], table.rearrange("(b p) c -> p b c", p=P)[:, NE:, :]).then_inc(slots_loaded, 16)
                sp.wait_ge(loaded, 32)
                blocks = sp.value_load(infos[0:1, MAX_OVER:MAX_OVER + 1], min_val=0, max_val=MAX_OVER)
                with sp.Fori(0, MAX_OVER) as j:
                    with sp.If(j < blocks):
                        sp.wait_ge(blocks_done, j + 1)
                        e = sp.value_load(infos[0:1, bass.ds(j, 1)], min_val=0, max_val=NE - 1)
                        for i in range(PER):
                            if i >= RAWS:
                                sp.wait_ge(used, PER * j + i - RAWS + 1)
                            if i < 2 * GC:
                                v = (gv, uv)[i // GC]
                                src = v[bass.ds(e, 1), :, (i % GC) * KQ:(i % GC + 1) * KQ, :].rearrange("a p k h -> (a p) (k h)")
                            else:
                                src = dv[bass.ds(e, 1), :, i - 2 * GC, :].rearrange("a p n -> (a p) n")
                            sp.dma_start(w[:, i % RAWS, :], src).then_inc(w_loaded[i % RAWS], 16)

            @block.gpsimd
            def _(pool):
                pool.sem_inc(blocks_done, 1)
                nc.gpsimd.memset(xg[:, :], 0.0).then_inc(cleared, 1)
                pool.wait_ge(cleared, 1)
                pool.wait_ge(slots_loaded, 16)
                pool.wait_ge(loaded, 32)
                blocks = pool.value_load(infos[0:1, MAX_OVER:MAX_OVER + 1], min_val=0, max_val=MAX_OVER)
                with pool.Fori(0, MAX_OVER) as j:
                    with pool.If(j < blocks):
                        for c, o in enumerate((gidx, sidx, sw)):
                            nc.gpsimd.tensor_copy(o[:, :], slots[:, bass.ds(j, 1), c]).then_inc(picked, 1)
                        pool.wait_ge(picked, 3 * (j + 1))
                        pool.sem_inc(seen, 1)
                        pool.indirect_dma_start(xg[:, :], None, xn[:, :], bass.IndirectOffsetOnAxis(ap=gidx[:, :].bitcast(U32), axis=0),
                                                bounds_check=SEQ - 1, oob_is_err=False).then_inc(gathered, 16)
                        pool.wait_ge(y_set, NB * (j + 1))
                        pool.sem_inc(seen, 1)
                        pool.indirect_dma_start(yk[:, :], bass.IndirectOffsetOnAxis(ap=sidx[:, :].bitcast(U32), axis=0), y_sb[:, :], None,
                                                bounds_check=TOPK * SEQ - 1, oob_is_err=False).then_inc(scattered, 16)
                        pool.wait_ge(scattered, 16 * (j + 1))
                        pool.sem_inc(blocks_done, 1)

            @block.scalar
            def _(act):
                act.wait_ge(loaded, 32)
                blocks = act.value_load(infos[0:1, MAX_OVER:MAX_OVER + 1], min_val=0, max_val=MAX_OVER)
                with act.Fori(0, MAX_OVER) as j:
                    with act.If(j < blocks):
                        for q in range(XR):
                            act.wait_ge(x_flip, XR * j + q + 1)
                            nc.scalar.activation(flat(xT[:, KQ * q:KQ * (q + 1), :]), ps_y[q][:, :], ACT.Copy).then_inc(x_set, 1)
                        act.wait_ge(used, PER * j + GC)
                        nc.scalar.activation(th[:, :], ps_g[:, :], ACT.Tanh, scale=0.5).then_inc(tanh_set, 1)
                        act.wait_ge(h_flip, j + 1)
                        nc.scalar.activation(flat(hT[:, :, :]), ps_h[:, :], ACT.Copy).then_inc(h_set, 1)
                        act.wait_ge(used, PER * (j + 1))
                        act.wait_ge(picked, 3 * (j + 1))
                        act.wait_ge(blocks_done, j + 1)
                        for b in range(NB):
                            nc.scalar.activation(y_sb[:, b * HALF:(b + 1) * HALF], ps_y[b][:, :], ACT.Copy, scale=sw[:, :].bitcast(F32)).then_inc(y_set, 1)

            @block.vector
            def _(dve):
                dve.wait_ge(loaded, 32)
                blocks = dve.value_load(infos[0:1, MAX_OVER:MAX_OVER + 1], min_val=0, max_val=MAX_OVER)
                with dve.Fori(0, MAX_OVER) as j:
                    with dve.If(j < blocks):
                        dve.wait_ge(used, PER * j + 2 * GC)
                        dve.wait_ge(tanh_set, j + 1)
                        nc.vector.scalar_tensor_tensor(hid[:, :], th[:, :], 1.0, ps_g[:, :], ALU.add, ALU.mult).then_inc(act_set, 1)
                        dve.wait_ge(act_set, j + 1)
                        nc.vector.scalar_tensor_tensor(hid[:, :], hid[:, :], 0.5, ps_u[:, :], ALU.mult, ALU.mult).then_inc(hid_set, 1)

            @block.tensor
            def _(pe):
                pe.wait_ge(loaded, 32)
                pe.wait_ge(cleared, 1)
                blocks = pe.value_load(infos[0:1, MAX_OVER:MAX_OVER + 1], min_val=0, max_val=MAX_OVER)
                with pe.Fori(0, MAX_OVER) as j:
                    with pe.If(j < blocks):
                        pe.wait_ge(gathered, 16 * (j + 1))
                        pe.wait_ge(blocks_done, j + 1)
                        for q in range(XR):
                            for i in range(KQ):
                                ins = nc.tensor.transpose(ps_y[q][:, i * P:(i + 1) * P], xg[:, KQ * q + i::KT], ident[:, :])
                            ins.then_inc(x_flip, 1)
                        pe.wait_ge(x_set, XR * (j + 1))
                        for i in range(PER):
                            pe.wait_ge(w_loaded[i % RAWS], 16 * (PER // RAWS * j + i // RAWS + 1))
                            if i == 2 * GC:
                                pe.wait_ge(hid_set, j + 1)
                                for m in range(DC):
                                    ins = nc.tensor.transpose(ps_h[:, m * P:(m + 1) * P], hid[:, m::DC], ident[:, :])
                                ins.then_inc(h_flip, 1)
                                pe.wait_ge(h_set, j + 1)
                            for m in range(4):
                                k = (i % GC) * KQ + m
                                ws = w[:, i % RAWS, m * HALF:(m + 1) * HALF]
                                if i < 2 * GC:
                                    ins = nc.tensor.matmul((ps_g, ps_u)[i // GC][:, :], xT[:, k, :], ws, start=k == 0, stop=k == KT - 1)
                                else:
                                    q = i - 2 * GC
                                    ins = nc.tensor.matmul(ps_y[m][:, :], hT[:, q, :], ws, start=q == 0, stop=q == DC - 1)
                            ins.then_inc(used, 1)


def finish(nc, h_all, yk, norm_g, out):
    yv = yk.rearrange("(t p c) d -> p t c d", p=P, c=TOPK)
    ov = out.rearrange("(t p) d -> p t d", p=P)
    with ExitStack() as ctx:
        sb = lambda n, s, d=F32: ctx.enter_context(nc.sbuf_tensor(n, s, d))
        sem = semaphores(nc, ctx)
        gb, junk = sb("gb_f", [P, D]), sb("junk_f", [P, D])
        y2, o = sb("y2", [P, 2, TOPK, D]), sb("o_f", [P, 2, D])
        ss, rstd, mh = sb("ss_f", [P, TT]), sb("rstd_f", [P, TT]), sb("mh_f", [P, 1])
        loaded, mh_set, added = sem("loaded_f"), sem("mh_set_f"), sem("added_f")
        y_loaded = [sem(f"y2_loaded{i}") for i in range(2)]
        stored = [sem(f"stored_f{i}") for i in range(2)]
        squared, mean_set, rstd_set, out_set = sem("squared_f"), sem("mean_f"), sem("rstd_f_set"), sem("out_set_f")
        with nc.Block() as block:
            @block.sync
            def _(sp):
                sp.dma_start(gb[:, :], norm_g).then_inc(loaded, 16)
                for t in range(TT):
                    if t >= 2:
                        sp.wait_ge(added, 2 * (t - 1))
                    sp.dma_start(y2[:, t % 2, :, :], yv[:, t, :, :]).then_inc(y_loaded[t % 2], 16)
                    if t >= 2:
                        sp.wait_ge(out_set, t - 1)
                        sp.dma_start(ov[:, t - 2, :], o[:, t % 2, :]).then_inc(stored[t % 2], 16)
                for t in (TT - 2, TT - 1):
                    sp.wait_ge(out_set, t + 1)
                    sp.dma_start(ov[:, t, :], o[:, t % 2, :]).then_inc(stored[t % 2], 16)
                for i in range(2):
                    sp.wait_ge(stored[i], 16 * (TT // 2))

            @block.gpsimd
            def _(pool):
                nc.gpsimd.memset(mh[:, :], -0.5).then_inc(mh_set, 1)
                pool.wait_ge(mh_set, 1)
                for t in range(TT):
                    pool.wait_ge(mean_set, t + 1)
                    nc.gpsimd.tensor_tensor(rstd[:, t:t + 1], ss[:, t:t + 1], mh[:, :], ALU.pow).then_inc(rstd_set, 1)

            @block.scalar
            def _(act):
                for t in range(TT):
                    act.wait_ge(added, 2 * (t + 1))
                    if t:
                        act.wait_ge(squared, t)
                    nc.scalar.activation(junk[:, :], h_all[:, t, :], ACT.Square, accum_out=ss[:, t:t + 1]).then_inc(squared, 1)

            @block.vector
            def _(dve):
                v = nc.vector

                def scale(t):
                    dve.wait_ge(rstd_set, t + 1)
                    dve.wait_ge(loaded, 16)
                    if t >= 2:
                        dve.wait_ge(stored[t % 2], 16 * (t // 2))
                    v.scalar_tensor_tensor(o[:, t % 2, :], h_all[:, t, :], rstd[:, t:t + 1], gb[:, :], ALU.mult, ALU.mult).then_inc(out_set, 1)
                for t in range(TT):
                    dve.wait_ge(y_loaded[t % 2], 16 * (t // 2 + 1))
                    for c in range(TOPK):
                        v.tensor_tensor(h_all[:, t, :], h_all[:, t, :], y2[:, t % 2, c, :], ALU.add).then_inc(added, 1)
                        dve.wait_ge(added, 2 * t + c + 1)
                    if t:
                        scale(t - 1)
                    dve.wait_ge(squared, t + 1)
                    v.tensor_scalar(ss[:, t:t + 1], ss[:, t:t + 1], 1.0 / D, RMS_EPS, ALU.mult, ALU.add).then_inc(mean_set, 1)
                scale(TT - 1)


def mask_tables():
    r, c = np.arange(P)[:, None], np.arange(P)[None, :]
    ident = np.eye(P, dtype=np.float32)
    same_head = (r // HEAD == c // HEAD).astype(np.float32)
    head_of = np.stack([(np.arange(P) // HEAD == h) for h in range(2)], 1).astype(np.float32)
    before, upto = r < c, r <= c
    score_mask = np.concatenate([c < r, upto, before, upto], 1).astype(np.float32)
    level_mask = np.concatenate([np.tile(((r >> i) % 2 == 0) & (c >> i == (r >> i) + 1), (1, 4))
                                 for i in range(LEVELS)], 1).astype(np.float32)
    heads = AW // HEAD
    i, k = np.arange(P)[:, None], np.arange(KW)[None, :]
    dist = np.abs(i - (k - HEAD)).astype(np.float32)
    seen = (k // HEAD == i // HEAD) | (k // HEAD == i // HEAD + 1)
    slope = (2.0 ** (-8.0 * np.arange(1, heads + 1) / heads)).astype(np.float32)
    bias = np.where(seen[:, None, :], -slope[None, :, None] * dist[:, None, :], np.float32(NEVER)).astype(np.float32).reshape(P, -1)
    cols = np.zeros(NG + 3 * NE + 2 * MAX_OVER, np.float32)
    known = np.concatenate([NG - np.arange(NG), NE - np.arange(NE), np.arange(NE),
                            P * (1 + np.arange(MAX_OVER)), np.arange(MAX_OVER)])
    cols[:known.size] = known
    return dict(ident=ident, same_head=same_head, head_of=head_of, score_mask=score_mask, level_mask=level_mask,
                bias=bias, cols=np.tile(cols, (P, 1)), before=before.astype(np.float32))


def lay_out(inputs):
    a = {n: np.asarray(v) for n, v in inputs.items()}
    one = lambda n: a[n][0]
    per_channel = lambda v: v.reshape(-1, P).T
    across = lambda v: np.tile(v.reshape(1, -1), (P, 1))
    w = one("w_in")
    starts = [P * i for i in range(COLT)] + [IN_TOTAL - P]
    mu = one("shift_mu")
    mu_lora = np.zeros((P, 3), np.float32)
    for i in range(3):
        part = mu[3 * RW + i * P:min(3 * RW + (i + 1) * P, RWKV_IN)]
        mu_lora[:part.size, i] = part
    router_w = np.concatenate([one("router_group_w"), one("router_expert_w").transpose(1, 0, 2).reshape(D, NE)], 1)
    arrays = dict(
        x=a["x"][0],
        norm_mix_g=per_channel(one("norm_mix_g")),
        w_in=np.stack([w[:, s:s + P].reshape(KT, P, P).transpose(1, 0, 2) for s in starts]),
        rwkv_params=np.stack([per_channel(v) for v in (
            mu[0:RW], mu[RW:2 * RW], mu[2 * RW:3 * RW], one("w0"), one("a0"), one("k_k"), one("k_a"),
            one("r_k").reshape(-1), one("ln_x_g"), one("ln_x_b"))], 2),
        mu_lora=mu_lora,
        w_lora_up=one("w_lora_up"), a_lora_up=one("a_lora_up"), g_lora_up=one("g_lora_up"),
        sinks=across(one("attn_sinks")),
        w_out=one("w_out"),
        norm_ffn_g=across(one("norm_ffn_g")),
        router_w=router_w.reshape(KT, P, NR).transpose(1, 0, 2),
        router_b=across(np.concatenate([one("router_group_b"), one("router_expert_b").reshape(-1)])),
        w_gate=one("expert_w_gate"), w_up=one("expert_w_up"), w_down=one("expert_w_down"),
        norm_final_g=across(a["norm_final_g"]))
    arrays.update(mask_tables())
    return {f"in_{n}": np.ascontiguousarray(v) for n, v in arrays.items()}


def build(nc, t, out):
    scratch = lambda n, s, d=F32: nc.dram_tensor(n, s, d, kind="Internal").ap()
    zT, yT = scratch("zT", (IN_TOTAL, SEQ)), scratch("yT", (D, SEQ))
    xn, yk = scratch("xn", (SEQ, D)), scratch("yk", (TOPK * SEQ, D))
    table, info = scratch("table", (BLOCKS * P, 3), I32), scratch("info", (1, MAX_OVER + 1), I32)
    project_in(nc, t["x"], t["norm_mix_g"], t["w_in"], zT, t["ident"])
    rwkv(nc, zT, t["rwkv_params"], t["mu_lora"], t["w_lora_up"], t["a_lora_up"], t["g_lora_up"],
         [t[n] for n in ("ident", "same_head", "head_of", "score_mask", "level_mask")], yT)
    attention(nc, zT, t["sinks"], t["bias"], t["ident"], yT)
    with nc.sbuf_tensor("h_all", [P, TT, D], F32) as h_all:
        project_out(nc, yT, t["w_out"], t["x"], h_all)
        route(nc, h_all, t["norm_ffn_g"], t["router_w"], t["router_b"], (t["ident"], t["cols"], t["before"]), xn, table, info)
        experts(nc, xn, table, t["w_gate"], t["w_up"], t["w_down"], t["ident"], yk)
        experts_over(nc, xn, table, info, t["w_gate"], t["w_up"], t["w_down"], t["ident"], yk)
        finish(nc, h_all, yk, t["norm_final_g"], out)


def kernel(**inputs):
    import concourse.bacc as bacc
    from concourse.bass_utils import run_bass_kernel_spmd

    nc = bacc.Bacc("TRN2", target_bir_lowering=False, num_devices=1)
    arrays = lay_out(inputs)
    args = {n[3:]: nc.dram_tensor(n, v.shape, mybir.dt.from_np(v.dtype), kind="ExternalInput").ap() for n, v in arrays.items()}
    out = nc.dram_tensor("out", (SEQ, D), F32, kind="ExternalOutput").ap()
    build(nc, args, out)
    r = run_bass_kernel_spmd(nc, [arrays], core_ids=[0])
    return r.results[0]["out"].reshape(1, SEQ, D)
```

```python
import math
from contextlib import ExitStack

import numpy as np
import concourse.bass as bass
from concourse import mybir

F32 = mybir.dt.float32
F32R = mybir.dt.float32r
I32 = mybir.dt.int32
U32 = mybir.dt.uint32
U8 = mybir.dt.uint8
ALU = mybir.AluOpType
ACT = mybir.ActivationFunctionType
AXX = mybir.AxisListType.X

P = 128
SEQ = 1024
D = 2048
TT = SEQ // P
KT = D // P
HALF = 512
NH = SEQ // HALF
RMS_EPS = 1e-6

HEAD = 64
RW = 1024
RANK_W, RANK_A, RANK_G = 64, 64, 160
RWKV_IN = 3 * RW + RANK_W + RANK_A + RANK_G
AW = 1024
KVW = 128
IN_TOTAL = RWKV_IN + AW + 2 * KVW
PAIRS = RW // P
GN_EPS = 64e-5

COLT = IN_TOTAL // P
COL_TAIL = IN_TOTAL - COLT * P


def semaphores(nc, ctx):
    taken = []

    def give_back():
        nc.clear_and_free_semaphores(taken)
        nc.all_engine_barrier()
    ctx.callback(give_back)

    def take(name):
        taken.append(nc.alloc_semaphore(name))
        return taken[-1]
    return take


def project_in(nc, x, norm_g, w_in, zT, ident_d):
    xv = x.rearrange("(t p) d -> p t d", p=P)
    RAW = 3
    with ExitStack() as ctx:
        sb = lambda n, s, d=F32: ctx.enter_context(nc.sbuf_tensor(n, s, d))
        sem = semaphores(nc, ctx)
        hn_hi = sb("hn_hi", [P, KT, SEQ], F32R)
        hn_lo = sb("hn_lo", [P, KT, SEQ], F32R)
        ident = sb("ident_a", [P, P])
        g_col = sb("g_col", [P, KT])
        ss = sb("ss", [P, TT])
        rstd = sb("rstd", [P, TT])
        mhalf = sb("mhalf", [P, 1])
        ps = [ctx.enter_context(nc.psum_tensor(f"psA{i}", [P, HALF], F32)) for i in range(8)]
        x_loaded = [sem(f"x_loaded{t}") for t in range(TT)]
        c_loaded = sem("c_loaded")
        squared, mean_ready, rstd_ready, scaled = sem("squared"), sem("mean_ready"), sem("rstd_ready"), sem("scaled")
        transposed, hi_ready, lo_ready = sem("transposed"), sem("hi_ready"), sem("lo_ready")
        half_set = sem("half_set")
        wraw = [sb("wraw0", [P, KT, P])]
        w_loaded = [sem("w_loaded0"), sem("w_loaded1")]

        with ExitStack() as ctx2:
            xt = ctx2.enter_context(nc.sbuf_tensor("xt", [P, TT, D], F32))
            junk = hn_lo[:, 0:D // HALF, HALF:]
            with nc.Block() as block:
                @block.sync
                def _(sp):
                    sp.dma_start(ident[:, :], ident_d).then_inc(c_loaded, 16)
                    sp.dma_start(g_col[:, :], norm_g).then_inc(c_loaded, 16)
                    for t in range(TT):
                        sp.dma_start(xt[:, t, :], xv[:, t, :]).then_inc(x_loaded[t], 16)
                    sp.dma_start(wraw[0][:, :, :], w_in[0, :, :, :]).then_inc(w_loaded[0], 16)

                @block.gpsimd
                def _(pool):
                    nc.gpsimd.memset(mhalf[:, :], -0.5).then_inc(half_set, 1)
                    pool.wait_ge(half_set, 1)
                    for t in range(TT):
                        pool.wait_ge(mean_ready, t + 1)
                        nc.gpsimd.tensor_tensor(rstd[:, t:t + 1], ss[:, t:t + 1], mhalf[:, :], ALU.pow).then_inc(rstd_ready, 1)

                @block.scalar
                def _(act):
                    def evacuate(h):
                        for k in range(KT):
                            n = h * KT + k
                            act.wait_ge(transposed, n + 1)
                            nc.scalar.activation(hn_hi[:, k, h * HALF:(h + 1) * HALF], ps[n % 4][:, :], ACT.Copy,
                                                 scale=g_col[:, k:k + 1]).then_inc(hi_ready, 1)
                    act.wait_ge(c_loaded, 32)
                    for h in range(NH):
                        for t in range(4 * h, 4 * h + 4):
                            act.wait_ge(x_loaded[t], 16)
                            if t:
                                act.wait_ge(squared, t)
                            nc.scalar.activation(junk, xt[:, t, :].rearrange("p (k c) -> p k c", c=HALF), ACT.Square, accum_out=ss[:, t:t + 1]).then_inc(squared, 1)
                        evacuate(h)

                @block.vector
                def _(dve):
                    dve.wait_ge(c_loaded, 32)
                    for h in range(NH):
                        for i in range(4):
                            t = 4 * h + i
                            dve.wait_ge(squared, t + 1)
                            nc.vector.tensor_scalar(ss[:, t:t + 1], ss[:, t:t + 1], 1.0 / D, RMS_EPS, ALU.mult, ALU.add).then_inc(mean_ready, 1)
                            dve.wait_ge(rstd_ready, t + 1)
                            nc.vector.tensor_scalar(xt[:, t, :], xt[:, t, :], rstd[:, t:t + 1], None, ALU.mult).then_inc(scaled, 1)
                        for k in range(KT):
                            n = h * KT + k
                            dve.wait_ge(hi_ready, n + 1)
                            nc.vector.scalar_tensor_tensor(hn_lo[:, k, h * HALF:(h + 1) * HALF], ps[n % 4][:, :], g_col[:, k:k + 1],
                                                           hn_hi[:, k, h * HALF:(h + 1) * HALF].bitcast(F32), ALU.mult, ALU.subtract).then_inc(lo_ready, 1)

                @block.tensor
                def _(pe):
                    pe.wait_ge(c_loaded, 32)
                    for h in range(NH):
                        pe.wait_ge(scaled, 4 * (h + 1))
                        for k in range(KT):
                            n = h * KT + k
                            if n >= 4:
                                pe.wait_ge(lo_ready, n - 3)
                            for i in range(4):
                                last = nc.tensor.transpose(ps[n % 4][:, i * P:(i + 1) * P], xt[:, 4 * h + i, k * P:(k + 1) * P], ident[:, :])
                            last.then_inc(transposed, 1)

        wraw.append(sb("wraw1", [P, KT, P]))
        w_hi = sb("w_hi", [P, 2, KT, P], F32R)
        w_lo = sb("w_lo", [P, 2, KT, P], F32R)
        z_sb = sb("z_sb", [P, 2, SEQ])
        z_stored = [sem("z_stored0"), sem("z_stored1")]
        hi_split, lo_split = [sem("hi_split0"), sem("hi_split1")], [sem("lo_split0"), sem("lo_split1")]
        z_done, z_copied = [sem("z_done0"), sem("z_done1")], [sem("z_copied0"), sem("z_copied1")]
        TURNS = COLT // 2
        with nc.Block() as block:
            def load_w(sp, turn, b):
                sp.wait_ge(lo_split[b], turn)
                sp.dma_start(wraw[b][:, :, :], w_in[bass.ds(2 * turn + b, 1), :, :, :].rearrange("a p k n -> (a p) k n")).then_inc(w_loaded[b], 16)

            def store_z(sp, turn, b):
                sp.wait_ge(z_copied[b], 2 * turn + 2)
                sp.dma_start(zT[bass.ds((2 * turn + b) * P, P), :], z_sb[:, b, :]).then_inc(z_stored[b], 16)

            @block.sync
            def _(sp):
                sp.dma_start(wraw[1][:, :, :], w_in[1, :, :, :]).then_inc(w_loaded[1], 16)
                with sp.Fori(1, TURNS) as turn:
                    for b in range(2):
                        load_w(sp, turn, b)
                        store_z(sp, turn - 1, b)
                load_w(sp, TURNS, 0)
                for b in range(2):
                    store_z(sp, TURNS - 1, b)
                sp.wait_ge(z_copied[0], 2 * TURNS + 2)
                sp.dma_start(zT[COLT * P:, :], z_sb[P - COL_TAIL:, 0, :]).then_inc(z_stored[0], 16)
                sp.wait_ge(z_stored[0], 16 * (TURNS + 1))
                sp.wait_ge(z_stored[1], 16 * TURNS)

            def split_hi(act, turn, b, first):
                act.wait_ge(w_loaded[b], 16 * turn + 16)
                if not first:
                    act.wait_ge(z_done[b], 2 * turn)
                nc.scalar.activation(w_hi[:, b, :, :], wraw[b][:, :, :], ACT.Copy).then_inc(hi_split[b], 1)

            def copy_z(act, turn, b, first):
                if not first:
                    act.wait_ge(z_stored[b], 16 * turn)
                for h in range(NH):
                    act.wait_ge(z_done[b], 2 * turn + h + 1)
                    nc.scalar.activation(z_sb[:, b, h * HALF:(h + 1) * HALF], ps[2 * b + h][:, :], ACT.Copy).then_inc(z_copied[b], 1)

            @block.scalar
            def _(act):
                split_hi(act, 0, 0, True)
                split_hi(act, 0, 1, True)
                copy_z(act, 0, 0, True)
                split_hi(act, 1, 0, False)
                copy_z(act, 0, 1, True)
                with act.Fori(1, TURNS) as turn:
                    split_hi(act, turn, 1, False)
                    copy_z(act, turn, 0, False)
                    split_hi(act, turn + 1, 0, False)
                    copy_z(act, turn, 1, False)
                copy_z(act, TURNS, 0, False)

            def split_lo(dve, turn, b):
                dve.wait_ge(hi_split[b], turn + 1)
                nc.vector.tensor_tensor(w_lo[:, b, :, :], wraw[b][:, :, :], w_hi[:, b, :, :].bitcast(F32), ALU.subtract).then_inc(lo_split[b], 1)

            @block.vector
            def _(dve):
                with dve.Fori(0, TURNS) as turn:
                    for b in range(2):
                        split_lo(dve, turn, b)
                split_lo(dve, TURNS, 0)

            def multiply(pe, turn, b, first):
                pe.wait_ge(lo_split[b], turn + 1)
                for h in range(NH):
                    if not first:
                        pe.wait_ge(z_copied[b], 2 * turn - 1 + h)
                    cols = slice(h * HALF, (h + 1) * HALF)
                    for k in range(KT):
                        nc.tensor.matmul(ps[2 * b + h][:, :], w_hi[:, b, k, :], hn_hi[:, k, cols], start=k == 0, stop=False)
                        nc.tensor.matmul(ps[2 * b + h][:, :], w_hi[:, b, k, :], hn_lo[:, k, cols], start=False, stop=False)
                        last = nc.tensor.matmul(ps[2 * b + h][:, :], w_lo[:, b, k, :], hn_hi[:, k, cols], start=False, stop=k == KT - 1)
                    last.then_inc(z_done[b], 1)

            @block.tensor
            def _(pe):
                for b in range(2):
                    multiply(pe, 0, b, True)
                with pe.Fori(1, TURNS) as turn:
                    for b in range(2):
                        multiply(pe, turn, b, False)
                multiply(pe, TURNS, 0, False)


C0 = -0.5 * math.exp(-0.5)
UNITS = TT * 2
LEVELS = 7
GROUPS = UNITS // 4
PACKS = UNITS // 8
(MU_R, MU_K, MU_V, OMU_R, OMU_K, OMU_V, W0_H, A0_H, K_K, KA_H, ONE_M_KA, R_K, LNX_G, LNX_B) = range(14)
GIVEN = 10

KW = 192
Q0 = RWKV_IN
K0, V0 = Q0 + AW, Q0 + AW + KVW
GROUP_PAIRS = 4
SCALE = HEAD ** -0.5
NEVER = -1e30


class Count:

    def __init__(self, sem, per_turn):
        self.sem, self.per_turn = sem, per_turn

    def at(self, turn, n):
        return turn * self.per_turn + n


def mix_heads(nc, zT, params, mu_lora, w_up, a_up, g_up, sinks_b, bias_tab, consts, yT):
    ident_d, ones_d, sel_d, score_mask_d, level_mask_d = consts
    with ExitStack() as ctx:
        sb = lambda n, s, d=F32: ctx.enter_context(nc.sbuf_tensor(n, s, d))
        sem = semaphores(nc, ctx)
        cnt = lambda n, k: Count(sem(n), k)
        ident, ones = sb("ident_b", [P, P]), sb("ones_b", [P, P])
        sel = sb("sel_b", [P, 2])
        score_mask = sb("score_mask", [P, 4 * P], U8)
        level_mask = sb("level_mask", [P, LEVELS, 4, P], U8)
        par_all = sb("par_all", [P, PAIRS, GIVEN])
        par = sb("par", [P, 14])
        mul, oml = sb("mul", [P, 3]), sb("oml", [P, 3])
        z3 = sb("z3", [P, 3, SEQ + 1])
        mix = sb("mix", [P, 3, SEQ])
        wa_act, g1_act, g2_act = sb("wa_act", [P, SEQ]), sb("g1_act", [P, SEQ]), sb("g2_act", [32, SEQ])
        wa_w = sb("wa_w", [P, P])
        g1_w, g2_w = sb("g1_w", [P, P]), sb("g2_w", [32, P])
        lw, ac, ER = (sb(n, [P, SEQ]) for n in ("lw", "ac", "ER"))
        L2 = sb("L2", [P, 2, SEQ])
        Lc, La = L2[:, 0, :], L2[:, 1, :]
        X = mix[:, 0:2, :].rearrange("p a (u c) -> p (a u) c", c=P)
        Y = L2[:, :, :].rearrange("p a (u c) -> p (a u) c", c=P)
        kk, sq, k2, bv, gT = (sb(n, [P, SEQ]) for n in ("kkn", "sq", "k2", "bv", "gT"))
        BT, KTt = ac, k2
        AR = sb("AR", [P, TT, 2, P])
        nat = sb("nat", [P, TT, 3, P])
        SC = sb("SC", [P, UNITS, 4, P])
        masks_wide = SC[...].rearrange("p u a c -> p (u a c)")[:, 0:(LEVELS + 1) * 4 * P]
        T1 = sb("T1", [P, LEVELS, 2, 4 * P])
        m_half, m_sum, dec = sb("m_half", [P, TT]), sb("m_sum", [P, TT]), sb("dec", [P, TT])
        nrm, rn, mh = sb("nrm", [P, UNITS]), sb("rn", [P, UNITS]), sb("mh", [P, UNITS])
        RU, Un = sb("RU", [P, P]), sb("Un", [P, P])
        Ss = sb("Ss", [P, 2, P])
        st, ag = sb("st", [P, UNITS, 6]), sb("ag", [P, UNITS, 2])
        var = sb("var", [P, UNITS])
        rng_ = sb("rng_", [P, UNITS])
        ynat = sq
        rrk, qk = lw, bv
        ps = [ctx.enter_context(nc.psum_tensor(f"psB{i}", [P, HALF], F32)) for i in range(5)]
        T_BANK, Y_BANK, X_BANK, X_FIRST_BANK = (0, 1), (2, 3), (2, 4, 3, 4), (4, 2, 4, 2)
        SCORE_BANK = (4, 2, 3, 0)
        kT = sb("kT", [P, HEAD + SEQ])
        vT = sq
        v_main, v_prev = sb("v_main", [P, TT, P]), sb("v_prev", [HEAD, TT, P])
        sinks, sink_now = sb("sinks", [P, 2 * PAIRS]), sb("sink_now", [P, 2])
        qT, oT = sb("qT", [P, SEQ]), sb("oT", [P, SEQ])
        bias = sb("bias", [P, 2, KW])
        S, E = sb("S", [P, 2, 2, KW]), sb("E", [P, 2, 2, KW])
        p_main, p_prev = sb("p_main", [P, 2, 2 * P]), sb("p_prev", [HEAD, 2, 2 * P])
        mx, nmx, den, rden = (sb(n, [P, 2, 2]) for n in ("mx", "nmx", "den", "rden"))
        es, rs = sb("es", [P, 4, 2]), sb("rs", [P, 4, 2])
        o_nat = sb("o_nat", [P, 2, P])
        psC = ctx.enter_context(nc.psum_tensor("psC", [P, 3, HALF], F32))
        ps_s = psC[:, 0:2, 0:KW]
        ps_o, ps_f = psC[:, 0, 2 * P:3 * P], psC[:, 1, 2 * P:3 * P]
        ps_main, ps_prev = psC[:, 2, 0:2 * P], psC[0:HEAD, 2, 2 * P:]

        const_loaded = sem("const_loaded")
        zl_loaded = sem("zl_loaded")
        masks_set, zeros_set = sem("masks_set"), sem("zeros_set")
        lora_a, lora_v = sem("lora_a"), sem("lora_v")
        turn_over, seen = sem("turn_over"), sem("seen_b")
        out_free = sem("out_free")
        pair_loaded = cnt("pair_loaded", 16 * 6)
        v_loaded, pads_set, v_done, v_set = sem("v_loaded"), sem("pads_set"), sem("v_done"), sem("v_set")
        q_loaded = cnt("q_loaded", 64)
        biased, maxed, neg_set, softened, den_set, rden_set, sink_max = (
            cnt(n, TT) for n in ("biased", "maxed", "neg_set", "softened", "den_set", "rden_set", "sink_max"))
        slot_filled, slot_read = cnt("slot_filled", TT + 4), cnt("slot_read", TT + 4)
        first_masked, sink_set = cnt("first_masked", 1), cnt("sink_set", 1)
        p_done, p_set, o_set, f_set = (cnt(n, TT) for n in ("p_done", "p_set", "o_set", "f_set"))
        o_stored = sem("o_stored")
        par_set = cnt("par_set", 3)
        scaled, mixed = cnt("scaled_b", 3), cnt("mixed", 3)
        lora_done, tanhed, gated = cnt("lora_done", 6), cnt("tanhed", 4), cnt("gated", 2)
        kk_raw, squared, summed, norm_set, norm_pow, norm_wide, kk_set = (
            cnt("kk_raw", 1), cnt("squared_b", 1), cnt("summed", 1), cnt("norm_set", 1), cnt("norm_pow", 1),
            cnt("norm_wide", 2), cnt("kk_set", 2))
        dve_step = cnt("dve_step", 10 + TT)
        cum_set, exped = cnt("cum_set", 3), cnt("exped", 4)
        bonus_in, bonus_done = cnt("bonus_in", 1), cnt("bonus_done", 2)
        ops_set = cnt("ops_set", 4)
        nat_done, nat_set = cnt("nat_done", TT), cnt("nat_set", TT)
        scored, score_set = cnt("scored", UNITS), cnt("score_set", UNITS)
        later = LEVELS - 1
        t_done, t_set, y_set = (cnt(n, GROUPS + later * PACKS) for n in ("t_done", "t_set", "y_set"))
        y_done = cnt("y_done", later * PACKS)
        x_done, x_set = cnt("x_done", later * GROUPS), cnt("x_set", later * GROUPS)
        rhs_done, rhs_set, u_done, u_set = (cnt(n, TT) for n in ("rhs_done", "rhs_set", "u_done", "u_set"))
        s_done, s_set, out_done, out_set = cnt("s_done", TT - 1), cnt("s_set", TT), cnt("out_done", TT), cnt("out_set", TT)
        stat_set, aggr_set, var_set, gn_pow, gn_set = (cnt("stat_set", TT), cnt("aggr_set", TT), cnt("var_set", 2),
                                                       cnt("gn_pow", 2), cnt("gn_set", TT))
        flipped, affine, plus_bonus, y_ready = cnt("flipped", 2), cnt("affine", 2), cnt("plus_bonus", 2), cnt("y_ready", 2)
        y_stored = sem("y_stored")
        mh_set = sem("mh_set")
        g2_loaded = cnt("g2_loaded", 16)
        norm_rep = cnt("norm_rep", 1)
        half = lambda h: slice(h * HALF, (h + 1) * HALF)
        tile = lambda j: slice(j * P, (j + 1) * P)

        def through(lev, n):
            return GROUPS + (lev - 1) * PACKS + n if lev else n

        def odd_blocks(a, lev):
            return a.rearrange("p (m two b) -> p m two b", two=2, b=1 << lev)[:, :, 1, :]
        ENG = 3

        def wait(eng, c, turn, n):
            eng.wait_ge(c.sem, c.at(turn, n))

        def start_turn(eng, turn):
            eng.wait_ge(turn_over, (turn + 1) * ENG)

        hs = lambda h: slice(h * HEAD, (h + 1) * HEAD)
        SLOTS = TT + 4

        def attend_pe(pe, turn, k):
            mm = nc.tensor.matmul
            if 0 <= k - 2 < TT:
                j = k - 2
                c = j % 2
                wait(pe, softened, turn, j + 1)
                if j:
                    wait(pe, p_set, turn, j)
                for h in range(2):
                    nc.tensor.transpose(ps_main[:, tile(h)], E[:, c, h, HEAD:], ident[:, :])
                for h in range(2):
                    ins = nc.tensor.transpose(ps_prev[:, tile(h)], E[:, c, h, 0:HEAD], ident[:, :])
                ins.then_inc(p_done.sem, 1)
            if k:
                wait(pe, slot_read, turn, k)
            ins = None
            if 0 <= k - 3 < TT:
                j = k - 3
                c = j % 2
                wait(pe, p_set, turn, j + 1)
                for h in range(2):
                    cols = bass.ds(turn // GROUP_PAIRS * HEAD, HEAD)
                    mm(ps_o[:, hs(h)], p_main[:, c, tile(h)], v_main[:, j, cols], start=True, stop=False)
                    ins = mm(ps_o[:, hs(h)], p_prev[:, c, tile(h)], v_prev[:, j, cols], start=False, stop=True)
            if 0 <= k - 4 < TT:
                j = k - 4
                wait(pe, o_set, turn, j + 1)
                ins = nc.tensor.transpose(ps_f, o_nat[:, j % 2, :], ident[:, :])
            if k < TT:
                if k == 0:
                    wait(pe, q_loaded, turn, 64)
                for h in range(2):
                    ins = mm(psC[:, h, 0:KW], qT[hs(h), tile(k)], kT[hs(h), k * P:k * P + KW], start=True, stop=True)
            ins.then_inc(slot_filled.sem, 1)

        def attend_act(act, turn, k):
            if 0 <= k - 2 < TT:
                j = k - 2
                c = j % 2
                wait(act, p_done, turn, j + 1)
                if j >= 2:
                    wait(act, slot_filled, turn, k - 1)
                nc.scalar.activation(p_main[:, c, :], ps_main, ACT.Copy)
                nc.scalar.activation(p_prev[:, c, :], ps_prev, ACT.Copy).then_inc(p_set.sem, 1)
            if 0 <= k - 1 < TT:
                j = k - 1
                c = j % 2
                wait(act, neg_set, turn, j + 1)
                if j >= 2:
                    wait(act, p_done, turn, j - 1)
                for h in range(2):
                    nc.scalar.activation(es[:, j % 4, h:h + 1], sink_now[:, h:h + 1], ACT.Exp, bias=nmx[:, c, h:h + 1])
                    ins = nc.scalar.activation(E[:, c, h, :], S[:, c, h, :], ACT.Exp, bias=nmx[:, c, h:h + 1],
                                               accum_out=rs[:, j % 4, h:h + 1])
                ins.then_inc(softened.sem, 1)

        def attend_dve(dve, turn, k):
            ins = None
            if 0 <= k - 3 < TT:
                j = k - 3
                c = j % 2
                wait(dve, softened, turn, j + 1)
                nc.vector.tensor_tensor(den[:, c, :], rs[:, j % 4, :], es[:, j % 4, :], ALU.add).then_inc(den_set.sem, 1)
                wait(dve, den_set, turn, j + 1)
                nc.vector.reciprocal(rden[:, c, :], den[:, c, :]).then_inc(rden_set.sem, 1)
                wait(dve, rden_set, turn, j + 1)
            if k == 0:
                nc.vector.tensor_copy(sink_now[:, :], sinks[:, bass.ds(turn * 2, 2)]).then_inc(sink_set.sem, 1)
                wait(dve, sink_set, turn, 1)
            wait(dve, slot_filled, turn, k + 1)
            if k < TT:
                c = k % 2
                if k >= 2:
                    wait(dve, softened, turn, k - 1)
                nc.vector.scalar_tensor_tensor(S[:, c, :, :], ps_s, SCALE, bias[:, :, :], ALU.mult, ALU.add).then_inc(biased.sem, 1)
            if 0 <= k - 3 < TT:
                j = k - 3
                for h in range(2):
                    ins = nc.vector.tensor_scalar(o_nat[:, j % 2, hs(h)], ps_o[:, hs(h)], rden[:, j % 2, h:h + 1], None, ALU.mult)
                ins.then_inc(o_set.sem, 1)
            if 0 <= k - 4 < TT:
                j = k - 4
                if j == 0:
                    dve.wait_ge(out_free, turn + 1)
                nc.vector.tensor_copy(oT[:, tile(j)], ps_f).then_inc(f_set.sem, 1)
            if k < TT:
                wait(dve, biased, turn, k + 1)
            if 0 <= k - 3 < TT:
                wait(dve, o_set, turn, k - 2)
            if 0 <= k - 4 < TT:
                wait(dve, f_set, turn, k - 3)
            dve.sem_inc(slot_read.sem, 1)
            if k < TT:
                if k == 0:
                    nc.vector.memset(S[0:HEAD, c, :, 0:HEAD], NEVER).then_inc(first_masked.sem, 1)
                    wait(dve, first_masked, turn, 1)
                nc.vector.tensor_reduce(mx[:, c, :], S[:, c, :, :], AXX, ALU.max).then_inc(maxed.sem, 1)
                wait(dve, maxed, turn, k + 1)
                nc.vector.tensor_tensor(mx[:, c, :], mx[:, c, :], sink_now[:, :], ALU.max).then_inc(sink_max.sem, 1)
                wait(dve, sink_max, turn, k + 1)
                nc.vector.tensor_scalar(nmx[:, c, :], mx[:, c, :], -1.0, None, ALU.mult).then_inc(neg_set.sem, 1)

        PLACES = {"norm": (0,), "level 0": (1,), "level 1": (2,), "level 3": (3,), "level 4": (4,), "chunk 0": (5,),
                  "chunk 1": (6,), "chunk 2": (7,), "chunk 3": (8,), "chunk 5": (9,), "chunk 6": (10,), "chunk 7": (11,)}
        assert sorted(k for ks in PLACES.values() for k in ks) == list(range(SLOTS))

        def attend(step, engine, turn, place):
            for k in PLACES.get(place, ()):
                step(engine, turn, k)

        with nc.Block() as block:
            @block.sync
            def _(sp):
                for o, i in ((ident[...], ident_d), (ones[...], ones_d), (sel[...], sel_d), (par_all[...], params), (mul[...], mu_lora),
                             (masks_wide[:, 0:4 * P], score_mask_d), (masks_wide[:, 4 * P:], level_mask_d)):
                    sp.dma_start(o, i).then_inc(const_loaded, 16)
                sp.dma_start(z3[:, 0, 1:], zT[3 * RW:3 * RW + P, :]).then_inc(zl_loaded, 16)
                sp.dma_start(z3[:, 1, 1:], zT[3 * RW + P:3 * RW + 2 * P, :]).then_inc(zl_loaded, 16)
                sp.dma_start(z3[0:32, 2, 1:], zT[3 * RW + 2 * P:RWKV_IN, :]).then_inc(zl_loaded, 16)
                sp.dma_start(vT[:, :], zT[V0:V0 + KVW, :]).then_inc(v_loaded, 16)
                sp.dma_start(sinks[:, :], sinks_b).then_inc(v_loaded, 16)
                sp.sem_inc(out_free, 1)

                def load_z(turn):
                    for i in range(3):
                        sp.dma_start(z3[:, i, 1:], zT[bass.ds(turn * P + i * RW, P), :]).then_inc(pair_loaded.sem, 16)

                def load_lora(turn):
                    cols = bass.ds(turn * P, P)
                    sp.dma_start(wa_w[0:64, :], w_up[:, cols]).then_inc(pair_loaded.sem, 16)
                    sp.dma_start(wa_w[64:128, :], a_up[:, cols]).then_inc(pair_loaded.sem, 16)
                    sp.dma_start(g1_w[:, :], g_up[0:P, cols]).then_inc(pair_loaded.sem, 16)
                    sp.dma_start(g2_w[:, :], g_up[P:RANK_G, cols]).then_inc(g2_loaded.sem, 16)

                def load_q(turn):
                    sp.dma_start(qT[:, :], zT[bass.ds(Q0 + turn * P, P), :]).then_inc(q_loaded.sem, 16)
                    for h in range(2):
                        sp.dma_start(kT[hs(h), HEAD:], zT[bass.ds(K0 + turn // GROUP_PAIRS * HEAD, HEAD), :]).then_inc(q_loaded.sem, 16)
                    sp.dma_start(bias[:, :, :].rearrange("p h k -> p (h k)"), bias_tab[:, bass.ds(turn * 2 * KW, 2 * KW)]).then_inc(q_loaded.sem, 16)

                def store(turn):
                    wait(sp, f_set, turn, TT)
                    sp.dma_start(yT[bass.ds(RW + turn * P, P), :], oT[:, :]).then_inc(o_stored, 16)
                    wait(sp, y_ready, turn, 2)
                    sp.dma_start(yT[bass.ds(turn * P, P), :], gT[:, :]).then_inc(y_stored, 16)
                    sp.wait_ge(o_stored, 16 * turn + 16)
                    sp.wait_ge(y_stored, 16 * turn + 16)
                load_lora(0)
                load_q(0)
                sp.wait_ge(lora_v, 8)
                sp.wait_ge(lora_a, 6)
                load_z(0)
                with sp.Fori(0, PAIRS - 1) as turn:
                    wait(sp, lora_done, turn, 6)
                    load_lora(turn + 1)
                    wait(sp, scaled, turn, 3)
                    wait(sp, mixed, turn, 3)
                    load_z(turn + 1)
                    wait(sp, slot_filled, turn, TT)
                    wait(sp, biased, turn, TT)
                    load_q(turn + 1)
                    store(turn)
                    sp.sem_inc(out_free, 1)
                store(PAIRS - 1)

            @block.gpsimd
            def _(pool):
                nc.gpsimd.memset(mh[:, :], -0.5).then_inc(mh_set, 1)
                pool.wait_ge(mh_set, 1)
                with pool.Fori(0, PAIRS) as turn:
                    wait(pool, norm_set, turn, 1)
                    nc.gpsimd.tensor_tensor(rn[:, :], nrm[:, :], mh[:, :], ALU.pow).then_inc(norm_pow.sem, 1)
                    for i in range(2):
                        us = slice(i * UNITS // 2, (i + 1) * UNITS // 2)
                        wait(pool, var_set, turn, i + 1)
                        nc.gpsimd.tensor_tensor(rng_[:, us], var[:, us], mh[:, us], ALU.pow).then_inc(gn_pow.sem, 1)

            @block.scalar
            def _(act):
                act.wait_ge(const_loaded, 16 * 7)
                act.wait_ge(zl_loaded, 48)
                act.wait_ge(lora_v, 1)
                for i, (o, n) in enumerate(((wa_act, P), (g1_act, P), (g2_act, 32))):
                    nc.scalar.activation(o[:, :], z3[0:n, i, 1:], ACT.Copy, scale=oml[0:n, i:i + 1]).then_inc(lora_a, 1)
                act.wait_ge(lora_v, 4)
                nc.scalar.activation(wa_act[0:64, :], wa_act[0:64, :], ACT.Tanh).then_inc(lora_a, 1)
                nc.scalar.activation(g1_act[:, :], g1_act[:, :], ACT.Tanh, scale=0.5).then_inc(lora_a, 1)
                nc.scalar.activation(g2_act[:, :], g2_act[:, :], ACT.Tanh, scale=0.5).then_inc(lora_a, 1)
                for j in range(TT):
                    act.wait_ge(v_done, j + 1)
                    nc.scalar.activation(v_main[:, j, :], ps[2 + j % 2][:, 0:P], ACT.Copy).then_inc(v_set, 1)
                    if j:
                        nc.scalar.activation(v_prev[:, j, :], ps[2 + j % 2][0:HEAD, P:2 * P], ACT.Copy).then_inc(v_set, 1)
                act.wait_ge(lora_a, 6)
                act.wait_ge(v_set, 2 * TT - 1)
                act.sem_inc(turn_over, 1)
                with act.Fori(0, PAIRS) as turn:
                    start_turn(act, turn)
                    wait(act, pair_loaded, turn, 96)
                    wait(act, par_set, turn, 3)
                    for i in range(3):
                        nc.scalar.activation(mix[:, i, :], z3[:, i, 1:], ACT.Copy, scale=par[:, OMU_R + i:OMU_R + i + 1]).then_inc(scaled.sem, 1)
                    for i in range(4):
                        wait(act, lora_done, turn, i + 1)
                        o, b = ((lw, W0_H), (ac, A0_H))[i // 2]
                        nc.scalar.activation(o[:, half(i % 2)], ps[i][:, :], ACT.Tanh, bias=par[:, b:b + 1], scale=0.5).then_inc(tanhed.sem, 1)
                    act.wait_ge(out_free, turn + 1)
                    for i in range(2):
                        wait(act, lora_done, turn, 5 + i)
                        nc.scalar.activation(gT[:, half(i)], ps[(4, 0)[i]][:, :], ACT.Copy).then_inc(gated.sem, 1)
                    attend(attend_act, act, turn, "lora")
                    wait(act, kk_raw, turn, 1)
                    nc.scalar.activation(sq[:, :], kk[:, :], ACT.Square).then_inc(squared.sem, 1)
                    wait(act, cum_set, turn, 2)
                    nc.scalar.activation(ER[:, :], Lc[:, :], ACT.Exp).then_inc(exped.sem, 1)
                    nc.scalar.activation(dec[:, 0:TT - 1], m_sum[:, 0:TT - 1], ACT.Exp).then_inc(exped.sem, 1)
                    wait(act, cum_set, turn, 3)
                    nc.scalar.activation(La[:, :], La[:, :], ACT.Exp).then_inc(exped.sem, 1)
                    wait(act, exped, turn, 1)
                    nc.scalar.activation(Lc[:, :], Lc[:, :], ACT.Exp, scale=-1.0).then_inc(exped.sem, 1)
                    attend(attend_act, act, turn, "norm")
                    for j in range(TT):
                        wait(act, nat_done, turn, j + 1)
                        nc.scalar.activation(nat[:, j, :, :].rearrange("p a c -> p (a c)"), ps[2 + j % 2][:, 0:3 * P], ACT.Copy).then_inc(nat_set.sem, 1)
                    for lev in range(LEVELS):
                        attend(attend_act, act, turn, f"level {lev}")
                        if lev == 0:
                            for g in range(GROUPS):
                                wait(act, t_set, turn, g + 1)
                                nc.scalar.activation(Y[:, 4 * g:4 * g + 4, :].rearrange("p u c -> p (u c)"), T1[:, 0, g % 2, :],
                                                     ACT.Copy).then_inc(y_set.sem, 1)
                        else:
                            for g in range(PACKS):
                                wait(act, y_done, turn, (lev - 1) * PACKS + g + 1)
                                nc.scalar.activation(odd_blocks(Y[:, 8 * g:8 * g + 8, :].rearrange("p u c -> p (u c)"), lev),
                                                     ps[Y_BANK[g]][:, :].rearrange("p (m b) -> p m b", b=1 << lev), ACT.Copy).then_inc(y_set.sem, 1)
                        if lev < LEVELS - 1:
                            for g in range(GROUPS):
                                bank = (X_BANK if lev else X_FIRST_BANK)[g]
                                wait(act, x_done, turn, lev * GROUPS + g + 1)
                                nc.scalar.activation(X[:, 4 * g:4 * g + 4, :].rearrange("p u c -> p (u c)"), ps[bank][:, :], ACT.Copy).then_inc(x_set.sem, 1)
                    def copy_out(j):
                        wait(act, out_done, turn, j + 1)
                        nc.scalar.activation(ynat[:, tile(j)], ps[j % 2][:, 0:P], ACT.Copy).then_inc(out_set.sem, 1)
                    for j in range(TT):
                        wait(act, rhs_done, turn, j + 1)
                        nc.scalar.activation(RU[:, :], ps[4][:, 0:P], ACT.Copy).then_inc(rhs_set.sem, 1)
                        wait(act, u_done, turn, j + 1)
                        nc.scalar.activation(Un[:, :], ps[3][:, 0:P], ACT.Copy).then_inc(u_set.sem, 1)
                        copy_out(j)
                        attend(attend_act, act, turn, f"chunk {j}")
                    for i in range(2):
                        wait(act, flipped, turn, i + 1)
                        nc.scalar.activation(ER[:, half(i)], ps[(4, 3)[i]][:, :], ACT.Identity, bias=par[:, LNX_B:LNX_B + 1],
                                             scale=par[:, LNX_G:LNX_G + 1]).then_inc(affine.sem, 1)
                    attend(attend_act, act, turn, "flip")
                    wait(act, affine, turn, 2)
                    act.sem_inc(turn_over, 1)

            @block.vector
            def _(dve):
                nc.vector.memset(kT[:, 0:HEAD], 0.0).then_inc(pads_set, 1)
                nc.vector.memset(v_prev[:, 0, :], 0.0).then_inc(pads_set, 1)
                for i in range(3):
                    nc.vector.memset(z3[:, i, 0:1], 0.0).then_inc(zeros_set, 1)
                dve.wait_ge(const_loaded, 16 * 7)
                nc.vector.tensor_copy(score_mask[:, :], masks_wide[:, 0:4 * P]).then_inc(masks_set, 1)
                nc.vector.tensor_copy(level_mask[...].rearrange("p l u c -> p (l u c)"), masks_wide[:, 4 * P:]).then_inc(masks_set, 1)
                dve.wait_ge(masks_set, 2)
                nc.vector.memset(SC[...].rearrange("p u a c -> p (u a c)"), 0.0).then_inc(zeros_set, 1)
                for b in range(2):
                    for u in range(4):
                        nc.vector.tensor_copy(T1[:, 0, b, tile(u)], ident[:, :]).then_inc(zeros_set, 1)
                    for lev in range(1, LEVELS):
                        for u in range(8):
                            nc.vector.tensor_copy(T1[:, lev, b, u * HEAD:(u + 1) * HEAD].rearrange("p (m b) -> p m b", b=1 << lev),
                                                  odd_blocks(ident[:, :], lev)).then_inc(zeros_set, 1)
                dve.wait_ge(zeros_set, 4 + 8 + later * 16)
                nc.vector.tensor_scalar(oml[:, :], mul[:, 0:3], -1.0, 1.0, ALU.mult, ALU.add).then_inc(lora_v, 1)
                dve.wait_ge(zl_loaded, 48)
                for i, (o, n) in enumerate(((wa_act, P), (g1_act, P), (g2_act, 32))):
                    dve.wait_ge(lora_a, i + 1)
                    nc.vector.scalar_tensor_tensor(o[:, :], z3[0:n, i, 0:SEQ], mul[0:n, i:i + 1], o[:, :], ALU.mult, ALU.add).then_inc(lora_v, 1)
                for i, (o, n) in enumerate(((g1_act, P), (g2_act, 32))):
                    dve.wait_ge(lora_a, 5 + i)
                    nc.vector.tensor_scalar(o[:, :], o[:, :], 0.5, 0.5, ALU.mult, ALU.add).then_inc(lora_v, 1)
                nc.vector.memset(Ss[:, 0, :], 0.0).then_inc(lora_v, 1)
                dve.wait_ge(lora_a, 6)
                dve.wait_ge(lora_v, 7)
                nc.vector.memset(m_half[:, :], 0.0).then_inc(lora_v, 1)
                dve.wait_ge(lora_v, 8)
                dve.wait_ge(v_loaded, 32)
                dve.sem_inc(turn_over, 1)
                with dve.Fori(0, PAIRS) as turn:
                    start_turn(dve, turn)
                    steps = [0]

                    def link(ins):
                        steps[0] += 1
                        ins.then_inc(dve_step.sem, 1)
                        wait(dve, dve_step, turn, steps[0])

                    here = par_all[:, bass.ds(turn, 1), :].rearrange("p a c -> p (a c)")
                    nc.vector.tensor_copy(par[:, 0:3], here[:, 0:3]).then_inc(par_set.sem, 1)
                    nc.vector.tensor_scalar(par[:, OMU_R:OMU_R + 3], here[:, 0:3], -1.0, 1.0, ALU.mult, ALU.add).then_inc(par_set.sem, 1)
                    link(nc.vector.tensor_scalar(par[:, W0_H:W0_H + 2], here[:, 3:5], 0.5, None, ALU.mult))
                    nc.vector.tensor_scalar(par[:, KA_H:KA_H + 1], here[:, 6:7], 0.5, None, ALU.mult)
                    link(nc.vector.tensor_copy(par[:, K_K:K_K + 1], here[:, 5:6]))
                    link(nc.vector.tensor_scalar(par[:, ONE_M_KA:ONE_M_KA + 1], here[:, 6:7], -0.5, 1.0, ALU.mult, ALU.add))
                    nc.vector.tensor_copy(par[:, R_K:R_K + 3], here[:, 7:10]).then_inc(par_set.sem, 1)
                    wait(dve, par_set, turn, 3)
                    for i in range(3):
                        wait(dve, scaled, turn, i + 1)
                        nc.vector.scalar_tensor_tensor(mix[:, i, :], z3[:, i, 0:SEQ], par[:, i:i + 1], mix[:, i, :], ALU.mult, ALU.add).then_inc(mixed.sem, 1)
                    wait(dve, mixed, turn, 3)
                    nc.vector.tensor_scalar(kk[:, :], mix[:, 1, :], par[:, K_K:K_K + 1], None, ALU.mult).then_inc(kk_raw.sem, 1)
                    attend(attend_dve, dve, turn, "lora")
                    wait(dve, tanhed, turn, 2)
                    link(nc.vector.tensor_scalar(lw[:, :], lw[:, :], C0, C0, ALU.mult, ALU.add))
                    for j in range(TT):
                        ins = nc.vector.tensor_tensor_scan(Lc[:, tile(j)], lw[:, tile(j)], lw[:, tile(j)], 0.0, ALU.add, ALU.bypass)
                        link(ins)
                    Lv = Lc[:, :].rearrange("p (j c) -> p j c", c=P)
                    link(nc.vector.tensor_scalar(m_half[:, :], Lv[:, :, P - 1:P].rearrange("p j c -> p (j c)"), 0.5, None, ALU.mult))
                    nc.vector.tensor_tensor(m_sum[:, 0:TT - 1], m_half[:, 0:TT - 1], m_half[:, 1:TT], ALU.add).then_inc(cum_set.sem, 1)
                    nc.vector.tensor_tensor(Lv, Lv, m_half[:, :].unsqueeze(2).broadcast_to([P, TT, P]), ALU.subtract).then_inc(cum_set.sem, 1)
                    wait(dve, cum_set, turn, 2)
                    nc.vector.tensor_tensor(La[:, :], Lc[:, :], lw[:, :], ALU.subtract).then_inc(cum_set.sem, 1)
                    wait(dve, tanhed, turn, 4)
                    link(nc.vector.tensor_scalar(qk[:, :], ac[:, :], par[:, KA_H:KA_H + 1], par[:, ONE_M_KA:ONE_M_KA + 1], ALU.mult, ALU.add))
                    link(nc.vector.tensor_tensor(k2[:, :], mix[:, 1, :], qk[:, :], ALU.mult))
                    wait(dve, cum_set, turn, 3)
                    nc.vector.scalar_tensor_tensor(rrk[:, :], mix[:, 0, :], par[:, R_K:R_K + 1], k2[:, :], ALU.mult, ALU.mult).then_inc(bonus_in.sem, 1)
                    wait(dve, summed, turn, 1)
                    nc.vector.tensor_scalar(nrm[:, :], ps[1][:, 0:UNITS], 1e-24, None, ALU.max).then_inc(norm_set.sem, 1)
                    wait(dve, norm_pow, turn, 1)
                    nc.vector.tensor_copy(bv[:, :].rearrange("p (u c) -> p u c", c=HEAD),
                                          rn[:, :].unsqueeze(2).broadcast_to([P, UNITS, HEAD])).then_inc(norm_rep.sem, 1)
                    for i in range(2):
                        wait(dve, norm_wide, turn, i + 1)
                        nc.vector.tensor_tensor(kk[:, half(i)], kk[:, half(i)], ps[3 + i][:, :], ALU.mult).then_inc(kk_set.sem, 1)
                    attend(attend_dve, dve, turn, "norm")
                    wait(dve, kk_set, turn, 2)
                    link(nc.vector.scalar_tensor_tensor(ac[:, :], ac[:, :], 1.0, kk[:, :], ALU.add, ALU.mult))
                    wait(dve, exped, turn, 4)
                    t3 = lambda x: x[:, :].rearrange("p (j c) -> p j c", c=P)
                    nc.vector.scalar_tensor_tensor(BT[:, :], ac[:, :], 0.5, Lc[:, :], ALU.mult, ALU.mult).then_inc(ops_set.sem, 1)
                    nc.vector.tensor_tensor(KTt[:, :], k2[:, :], Lc[:, :], ALU.mult).then_inc(ops_set.sem, 1)
                    nc.vector.scalar_tensor_tensor(AR[:, :, 0, :], t3(kk), -1.0, t3(La), ALU.mult, ALU.mult).then_inc(ops_set.sem, 1)
                    nc.vector.tensor_tensor(AR[:, :, 1, :], t3(mix[:, 0, :]), t3(ER), ALU.mult).then_inc(ops_set.sem, 1)
                    for i in range(2):
                        wait(dve, bonus_done, turn, i + 1)
                        ins = nc.vector.tensor_tensor(bv[:, half(i)], ps[i][:, :], mix[:, 2, half(i)], ALU.mult)
                        link(ins)
                    for u in range(UNITS):
                        wait(dve, scored, turn, u + 1)
                        dve.sem_inc(seen, 1)
                        nc.vector.copy_predicated(SC[:, u, :, :].rearrange("p a c -> p (a c)"), score_mask[:, :], ps[SCORE_BANK[u % 4]][:, :]).then_inc(score_set.sem, 1)
                    for lev in range(LEVELS):
                        for g in range(PACKS if lev else GROUPS):
                            wait(dve, t_done, turn, through(lev, g + 1))
                            if lev == 0 and g >= 2:
                                wait(dve, y_set, turn, g - 1)
                                wait(dve, x_done, turn, g - 1)
                            dve.sem_inc(seen, 1)
                            nc.vector.copy_predicated(T1[:, lev, g % 2, :], level_mask[:, lev, :, :].rearrange("p u c -> p (u c)"),
                                                      ps[T_BANK[g % 2]][:, :]).then_inc(t_set.sem, 1)
                        attend(attend_dve, dve, turn, f"level {lev}")
                    nc.vector.memset(Ss[:, 0, :], 0.0).then_inc(s_set.sem, 1)
                    def stats(j):
                        wait(dve, out_set, turn, j + 1)
                        for h in range(2):
                            u = 2 * j + h
                            ins = nc.vector.bn_stats(st[:, u, :], ynat[:, j * P + h * HEAD:j * P + (h + 1) * HEAD])
                        ins.then_inc(stat_set.sem, 1)
                        wait(dve, stat_set, turn, j + 1)
                        dve.sem_inc(seen, 1)
                        for h in range(2):
                            u = 2 * j + h
                            ins = nc.vector.bn_aggr(ag[:, u, :], st[:, u, :])
                        ins.then_inc(aggr_set.sem, 1)

                    def variance(i):
                        us = slice(i * UNITS // 2, (i + 1) * UNITS // 2)
                        wait(dve, aggr_set, turn, (i + 1) * TT // 2)
                        nc.vector.tensor_scalar(var[:, us], ag[:, us, 1:2].rearrange("p u c -> p (u c)"), GN_EPS, None, ALU.add).then_inc(var_set.sem, 1)

                    def normalise(i):
                        wait(dve, gn_pow, turn, i + 1)
                        for j in range(i * TT // 2, (i + 1) * TT // 2):
                            for h in range(2):
                                u = 2 * j + h
                                yv = ynat[:, j * P + h * HEAD:j * P + (h + 1) * HEAD]
                                ins = nc.vector.tensor_scalar(yv, yv, ag[:, u, 0:1], rng_[:, u:u + 1], ALU.subtract, ALU.mult)
                            ins.then_inc(gn_set.sem, 1)
                    for j in range(TT):
                        if j < TT - 1:
                            wait(dve, s_done, turn, j + 1)
                            wait(dve, s_set, turn, j + 1)
                            nc.vector.scalar_tensor_tensor(Ss[:, (j + 1) % 2, :], ps[2][:, 0:P], dec[:, j:j + 1], ones[:, :], ALU.mult, ALU.mult)\
                                .then_inc(s_set.sem, 1)
                        if j:
                            stats(j - 1)
                        attend(attend_dve, dve, turn, f"chunk {j}")
                        if j == 4:
                            variance(0)
                        if j == 6:
                            normalise(0)
                    stats(TT - 1)
                    variance(1)
                    normalise(1)
                    attend(attend_dve, dve, turn, "flip")
                    wait(dve, gn_set, turn, TT)
                    dve.sem_inc(turn_over, 1)
                    for i in range(2):
                        wait(dve, affine, turn, i + 1)
                        nc.vector.tensor_tensor(ER[:, half(i)], ER[:, half(i)], bv[:, half(i)], ALU.add).then_inc(plus_bonus.sem, 1)
                        wait(dve, plus_bonus, turn, i + 1)
                        nc.vector.tensor_tensor(gT[:, half(i)], ER[:, half(i)], gT[:, half(i)], ALU.mult).then_inc(y_ready.sem, 1)
                    wait(dve, y_ready, turn, 2)
                    assert steps[0] == dve_step.per_turn, steps[0]

            @block.tensor
            def _(pe):
                pe.wait_ge(const_loaded, 16 * 7)
                pe.wait_ge(lora_a, 6)
                pe.wait_ge(lora_v, 8)
                pe.wait_ge(v_loaded, 32)
                pe.wait_ge(pads_set, 2)
                for j in range(TT):
                    if j >= 2:
                        pe.wait_ge(v_set, 2 * (j - 1) - 1)
                    ins = nc.tensor.transpose(ps[2 + j % 2][:, 0:P], vT[:, tile(j)], ident[:, :])
                    if j:
                        ins = nc.tensor.transpose(ps[2 + j % 2][0:HEAD, P:2 * P], vT[:, j * P - HEAD:j * P], ident[:, :])
                    ins.then_inc(v_done, 1)
                pe.wait_ge(v_set, 2 * TT - 1)
                pe.sem_inc(turn_over, 1)
                mm = nc.tensor.matmul
                with pe.Fori(0, PAIRS) as turn:
                    start_turn(pe, turn)
                    wait(pe, pair_loaded, turn, 96)
                    pe.wait_ge(g2_loaded.sem, 16 * turn + 16)
                    for i in range(2):
                        mm(ps[i][:, :], wa_w[0:64, :], wa_act[0:64, half(i)], start=True, stop=True).then_inc(lora_done.sem, 1)
                    for i in range(2):
                        mm(ps[2 + i][:, :], wa_w[64:128, :], wa_act[64:128, half(i)], start=True, stop=True).then_inc(lora_done.sem, 1)
                    for i in range(2):
                        if i:
                            wait(pe, tanhed, turn, 1)
                        bank = ps[(4, 0)[i]][:, :]
                        mm(bank, g1_w[:, :], g1_act[:, half(i)], start=True, stop=False)
                        mm(bank, g2_w[:, :], g2_act[:, half(i)], start=False, stop=True).then_inc(lora_done.sem, 1)
                    attend(attend_pe, pe, turn, "lora")
                    wait(pe, squared, turn, 1)
                    wait(pe, tanhed, turn, 2)
                    for j in range(TT):
                        ins = mm(ps[1][:, 2 * j:2 * j + 2], sq[:, tile(j)], sel[:, :], start=True, stop=True)
                    ins.then_inc(summed.sem, 1)
                    wait(pe, bonus_in, turn, 1)
                    wait(pe, gated, turn, 2)
                    wait(pe, norm_set, turn, 1)
                    for i in range(2):
                        mm(ps[i][:, :], ones[:, :], rrk[:, half(i)], start=True, stop=True).then_inc(bonus_done.sem, 1)
                    wait(pe, norm_rep, turn, 1)
                    wait(pe, tanhed, turn, 4)
                    for i in range(2):
                        for jj in range(4):
                            u = 2 * (4 * i + jj)
                            ins = mm(ps[3 + i][:, tile(jj)], bv[:, u * HEAD:(u + 2) * HEAD], ident[:, :], start=True, stop=True)
                        ins.then_inc(norm_wide.sem, 1)
                    attend(attend_pe, pe, turn, "norm")
                    wait(pe, ops_set, turn, 2)
                    wait(pe, tanhed, turn, 4)
                    for j in range(TT):
                        if j >= 2:
                            wait(pe, nat_set, turn, j - 1)
                        for i, src in enumerate((BT[:, tile(j)], KTt[:, tile(j)], mix[:, 2, tile(j)])):
                            ins = nc.tensor.transpose(ps[2 + j % 2][:, tile(i)], src, ident[:, :])
                        ins.then_inc(nat_done.sem, 1)
                    wait(pe, ops_set, turn, 4)
                    wait(pe, gated, turn, 2)
                    wait(pe, kk_set, turn, 2)
                    for j in range(TT):
                        for h in range(2):
                            u = 2 * j + h
                            rows = slice(h * HEAD, (h + 1) * HEAD)
                            bank = ps[SCORE_BANK[u % 4]]
                            if u == 1:
                                wait(pe, nat_set, turn, TT)
                            if u == 3:
                                wait(pe, dve_step, turn, 10 + TT)
                            if u >= 4:
                                wait(pe, score_set, turn, u - 3)
                            mm(bank[:, 0:P], AR[rows, j, 0, :], BT[rows, tile(j)], start=True, stop=True)
                            mm(bank[:, P:2 * P], BT[rows, tile(j)], AR[rows, j, 1, :], start=True, stop=True)
                            mm(bank[:, 2 * P:], KTt[rows, tile(j)], AR[rows, j, :, :].rearrange("p a c -> p (a c)"),
                               start=True, stop=True).then_inc(scored.sem, 1)
                    wait(pe, bonus_done, turn, 2)
                    wait(pe, dve_step, turn, 10 + TT)
                    wait(pe, score_set, turn, UNITS)
                    def products_t(lev, g):
                        wait(pe, y_set, turn, 2 * (g + 1) if lev == 1 else through(lev - 1, g + 1))
                        for i in range(8):
                            u = 8 * g + i
                            o = ps[T_BANK[g]][:, i * HEAD:(i + 1) * HEAD].rearrange("p (m b) -> p m b", b=1 << lev)
                            ins = mm(o, SC[:, u, 0, :], odd_blocks(Y[:, u, :], lev), start=True, stop=True)
                        ins.then_inc(t_done.sem, 1)

                    def products_y(lev, g):
                        wait(pe, t_set, turn, through(lev, g + 1))
                        wait(pe, x_set, turn, lev * GROUPS if lev == 1 else (lev - 1) * GROUPS + 2 * (g + 1))
                        for i in range(8):
                            ins = mm(ps[Y_BANK[g]][:, i * HEAD:(i + 1) * HEAD], X[:, 8 * g + i, :],
                                     T1[:, lev, g, i * HEAD:(i + 1) * HEAD], start=True, stop=True)
                        ins.then_inc(y_done.sem, 1)

                    def flip_y(lev, g):
                        wait(pe, y_set, turn, through(lev, g // 2 + 1) if lev else g + 1)
                        if lev == 0 and g >= 2 or lev and g == 3:
                            wait(pe, x_set, turn, lev * GROUPS + g - 1)
                        if lev and g == 1:
                            wait(pe, x_set, turn, lev * GROUPS)
                        for i in range(4):
                            src = Y[:, 4 * g + i, :] if lev else T1[:, 0, g % 2, tile(i)]
                            ins = nc.tensor.transpose(ps[(X_BANK if lev else X_FIRST_BANK)[g]][:, tile(i)], src, ident[:, :])
                        ins.then_inc(x_done.sem, 1)
                    for g in range(GROUPS):
                        if g >= 2:
                            wait(pe, t_set, turn, g - 1)
                        for i in range(4):
                            ins = nc.tensor.transpose(ps[T_BANK[g % 2]][:, tile(i)], SC[:, 4 * g + i, 0, :], ident[:, :])
                        ins.then_inc(t_done.sem, 1)
                    attend(attend_pe, pe, turn, "level 0")
                    for lev in range(1, LEVELS):
                        for g in range(PACKS):
                            flip_y(lev - 1, 2 * g)
                            flip_y(lev - 1, 2 * g + 1)
                            if lev > 1:
                                products_t(lev, g)
                        if lev == 1:
                            for g in range(PACKS):
                                products_t(lev, g)
                        attend(attend_pe, pe, turn, f"level {lev}")
                        for g in range(PACKS):
                            products_y(lev, g)
                    wait(pe, y_set, turn, through(LEVELS - 1, PACKS))
                    wait(pe, nat_set, turn, TT)

                    def rhs_values(j):
                        for h in range(2):
                            mm(ps[4][:, hs(h)], SC[:, 2 * j + h, 2, :], nat[:, j, 2, hs(h)], start=h == 0, stop=False)
                    rhs_values(0)
                    for j in range(TT):
                        wait(pe, s_set, turn, j + 1)
                        mm(ps[4][:, 0:P], AR[:, j, 0, :], Ss[:, j % 2, :], start=False, stop=True).then_inc(rhs_done.sem, 1)
                        if j >= 2:
                            wait(pe, out_set, turn, j - 1)
                        mm(ps[j % 2][:, 0:P], AR[:, j, 1, :], Ss[:, j % 2, :], start=True, stop=False)
                        for h in range(2):
                            mm(ps[j % 2][:, hs(h)], SC[:, 2 * j + h, 3, :], nat[:, j, 2, hs(h)], start=False, stop=False)
                        wait(pe, rhs_set, turn, j + 1)
                        for h in range(2):
                            ins = mm(ps[3][:, hs(h)], Y[:, 2 * j + h, :], RU[:, hs(h)], start=True, stop=True)
                        ins.then_inc(u_done.sem, 1)
                        if j < TT - 1:
                            mm(ps[2][:, 0:P], ident[:, :], Ss[:, j % 2, :], start=True, stop=False)
                            mm(ps[2][:, 0:P], nat[:, j, 1, :], nat[:, j, 2, :], start=False, stop=False)
                            rhs_values(j + 1)
                            wait(pe, u_set, turn, j + 1)
                            mm(ps[2][:, 0:P], nat[:, j, 0, :], Un[:, :], start=False, stop=True).then_inc(s_done.sem, 1)
                        else:
                            wait(pe, u_set, turn, j + 1)
                        for h in range(2):
                            ins = mm(ps[j % 2][:, hs(h)], SC[:, 2 * j + h, 1, :], Un[:, hs(h)], start=False, stop=h == 1)
                        ins.then_inc(out_done.sem, 1)
                        attend(attend_pe, pe, turn, f"chunk {j}")
                    for i in range(2):
                        wait(pe, gn_set, turn, 4 * i + 4)
                        for jj in range(4):
                            ins = nc.tensor.transpose(ps[(4, 3)[i]][:, tile(jj)], ynat[:, tile(4 * i + jj)], ident[:, :])
                        ins.then_inc(flipped.sem, 1)
                    attend(attend_pe, pe, turn, "flip")
                    wait(pe, affine, turn, 2)
                    pe.sem_inc(turn_over, 1)


NG, EPG = 4, 8
NE = NG * EPG
TOPK = 2
HID = D // 4
NR = NG + NE
MAX_OVER = SEQ * TOPK // P - 1
BLOCKS = NE + MAX_OVER
NOWHERE = 1 << 14
BIG = 1e30
KQ = 4
CHUNKS = KT // KQ


def project_out(nc, yT, w_out, x, h_all):
    yv = yT.rearrange("(p k) t -> p k t", p=P)
    wv = w_out.rearrange("(p k) n -> p k n", p=P)
    xv = x.rearrange("(t p) d -> p t d", p=P)
    NC = D // HALF
    with ExitStack() as ctx:
        sb = lambda n, s, d=F32: ctx.enter_context(nc.sbuf_tensor(n, s, d))
        sem = semaphores(nc, ctx)
        y_raw = sb("y_raw", [P, 2, KQ, HALF])
        y_hi, y_lo = sb("y_hi", [P, KT, HALF], F32R), sb("y_lo", [P, KT, HALF], F32R)
        raw = sb("wo_raw", [P, 2, KQ, HALF])
        hi, lo = sb("wo_hi", [P, 2, KQ, HALF], F32R), sb("wo_lo", [P, 2, KQ, HALF], F32R)
        ps = [ctx.enter_context(nc.psum_tensor(f"psD{i}", [P, HALF], F32)) for i in range(8)]
        x_loaded = sem("x_loaded_d")
        y_loaded = [sem(f"y_loaded{i}") for i in range(2)]
        w_loaded = [sem(f"wo_loaded{i}") for i in range(2)]
        y_hi_set, y_lo_set = sem("y_hi_set"), sem("y_lo_set")
        hi_set, lo_set, used, added = (sem(n) for n in ("wo_hi_set", "wo_lo_set", "wo_used", "wo_added"))
        TURN = 2 * CHUNKS

        with nc.Block() as block:
            @block.sync
            def _(sp):
                def load_w(it, i):
                    n0 = (2 * it + i // CHUNKS) * HALF
                    k = i % CHUNKS
                    sp.dma_start(raw[:, i % 2, :, :], wv[:, k * KQ:(k + 1) * KQ, bass.ds(n0, HALF)]).then_inc(w_loaded[i % 2], 16)
                for s in range(NH):
                    for c in range(CHUNKS):
                        if c == 2:
                            for i in range(2):
                                if s:
                                    sp.wait_ge(lo_set, s * 2 * TURN + i - 1)
                                load_w(0, i)
                        if s or c >= 2:
                            sp.wait_ge(y_lo_set, s * CHUNKS + c - 1)
                        sp.dma_start(y_raw[:, c % 2, :, :], yv[:, c * KQ:(c + 1) * KQ, s * HALF:(s + 1) * HALF]).then_inc(y_loaded[c % 2], 16)
                    if s == 0:
                        for t in range(TT):
                            sp.dma_start(h_all[:, t, :], xv[:, t, :]).then_inc(x_loaded, 16)
                    for i in range(2, TURN):
                        sp.wait_ge(lo_set, s * 2 * TURN + i - 1)
                        load_w(0, i)
                    with sp.Fori(1, NC // 2) as it:
                        for i in range(TURN):
                            sp.wait_ge(lo_set, (s * (NC // 2) + it) * TURN + i - 1)
                            load_w(it, i)

            @block.scalar
            def _(act):
                for s in range(NH):
                    for c in range(CHUNKS):
                        n = s * CHUNKS + c
                        act.wait_ge(y_loaded[c % 2], 16 * (n // 2 + 1))
                        if s:
                            act.wait_ge(used, 2 + CHUNKS * (NC * s - 1) + c + 1)
                        nc.scalar.activation(y_hi[:, c * KQ:(c + 1) * KQ, :], y_raw[:, c % 2, :, :], ACT.Copy).then_inc(y_hi_set, 1)
                    with act.Fori(0, NC // 2) as it:
                        for i in range(TURN):
                            n = (s * (NC // 2) + it) * TURN + i
                            act.wait_ge(w_loaded[i % 2], ((s * (NC // 2) + it) * (TURN // 2) + i // 2 + 1) * 16)
                            act.wait_ge(used, n + 1)
                            nc.scalar.activation(hi[:, i % 2, :, :], raw[:, i % 2, :, :], ACT.Copy).then_inc(hi_set, 1)

            def residual(dve, s, it, b):
                m = s * NC + 2 * it + b
                dve.wait_ge(x_loaded, 16 * TT)
                dve.wait_ge(used, 2 + CHUNKS * (m + 1))
                for t in range(4):
                    o = h_all[:, 4 * s + t, bass.ds((2 * it + b) * HALF, HALF)]
                    ins = nc.vector.tensor_tensor(o, ps[4 * b + t][:, :], o, ALU.add)
                ins.then_inc(added, 1)

            @block.vector
            def _(dve):
                nc.vector.sem_inc(used, 2)
                nc.vector.sem_inc(added, 2)
                for s in range(NH):
                    for c in range(CHUNKS):
                        n = s * CHUNKS + c
                        dve.wait_ge(y_hi_set, n + 1)
                        ks = slice(c * KQ, (c + 1) * KQ)
                        nc.vector.tensor_tensor(y_lo[:, ks, :], y_raw[:, c % 2, :, :], y_hi[:, ks, :].bitcast(F32), ALU.subtract).then_inc(y_lo_set, 1)
                    if s:
                        residual(dve, s - 1, NC // 2 - 1, 1)

                    def turn(it, first=False):
                        for i in range(TURN):
                            n = (s * (NC // 2) + it) * TURN + i
                            dve.wait_ge(used, n + 1)
                            dve.wait_ge(hi_set, n + 1)
                            nc.vector.tensor_tensor(lo[:, i % 2, :, :], raw[:, i % 2, :, :], hi[:, i % 2, :, :].bitcast(F32), ALU.subtract).then_inc(lo_set, 1)
                            if i == 1 and not first:
                                residual(dve, s, it - 1, 1)
                            if i == CHUNKS + 1:
                                residual(dve, s, it, 0)
                    turn(0, first=True)
                    with dve.Fori(1, NC // 2) as it:
                        turn(it)
                residual(dve, NH - 1, NC // 2 - 1, 1)

            @block.tensor
            def _(pe):
                mm = nc.tensor.matmul
                for s in range(NH):
                    with pe.Fori(0, NC // 2) as it:
                        for i in range(TURN):
                            b = i // CHUNKS
                            n = (s * (NC // 2) + it) * TURN + i
                            if i < CHUNKS:
                                pe.wait_ge(y_lo_set, CHUNKS * s + i + 1)
                            pe.wait_ge(lo_set, n + 1)
                            if i % CHUNKS == 0:
                                pe.wait_ge(added, s * NC + 2 * it + b + 1)
                            for k in range(KQ):
                                kk = (i % CHUNKS) * KQ + k
                                for t in range(4):
                                    ts = slice(t * P, (t + 1) * P)
                                    o = ps[4 * b + t][:, :]
                                    mm(o, y_hi[:, kk, ts], hi[:, i % 2, k, :], start=kk == 0, stop=False)
                                    mm(o, y_hi[:, kk, ts], lo[:, i % 2, k, :], start=False, stop=False)
                                    ins = mm(o, y_lo[:, kk, ts], hi[:, i % 2, k, :], start=False, stop=kk == KT - 1)
                            ins.then_inc(used, 1)


def route(nc, h_all, norm_g, router_w, router_b, consts, xn, table, info, ahead):
    ident_d, idx_d, before_d = consts
    with ExitStack() as ctx:
        sb = lambda n, s, d=F32: ctx.enter_context(nc.sbuf_tensor(n, s, d))
        sem = semaphores(nc, ctx)
        ident, before, ones = sb("ident_r", [P, P]), sb("before", [P, P]), sb("ones_r", [P, P])
        idx = sb("idx", [P, 4 + 3 * NE + 2 * MAX_OVER])
        g4, e32, eno = idx[:, 0:4], idx[:, 4:4 + NE], idx[:, 4 + NE:4 + 2 * NE]
        thr = idx[:, 4 + 2 * NE:4 + 2 * NE + MAX_OVER]
        blk = idx[:, 4 + 2 * NE + MAX_OVER:4 + 2 * NE + 2 * MAX_OVER]
        tok = sb("tok", [P, TT, TOPK])
        gb = sb("gb", [P, D])
        rw = sb("rw", [P, KT, NR])
        rb = sb("rb", [P, NR])
        junk = sb("junk_r", [P, D])
        xt = sb("xt_r", [P, 2, D])
        xT = sb("xT_r", [P, 2, KT, P])
        ss, rstd, mh = sb("ss_r", [P, TT]), sb("rstd_r", [P, TT]), sb("mh_r", [P, TT])
        L = sb("L", [P, TT, NR])
        ps_t = [ctx.enter_context(nc.psum_tensor(f"ps_t{i}", [P, HALF], F32)) for i in range(4)]
        ps_l = ctx.enter_context(nc.psum_tensor("ps_l", [P, TT, NR], F32))
        ps_r, ps_c = ctx.enter_context(nc.psum_tensor("ps_r", [P, TT, NE], F32)), ctx.enter_context(nc.psum_tensor("ps_c", [P, NE], F32))
        loaded, squared, mean_set, rstd_set, xn_set = (sem(n) for n in ("loaded_r", "squared_r", "mean_r", "rstd_set_r", "xn_set"))
        stored = [sem(f"xn_stored{i}") for i in range(2)]
        flipped, copied, logits, ones_set = sem("flipped_r"), sem("copied_r"), sem("logits_r"), sem("ones_set_r")
        chain, exp_in, exp_out = sem("route_step"), sem("exp_in"), sem("exp_out")
        ranks_in, ranks_out, slots_set = sem("ranks_in"), sem("ranks_out"), sem("slots_set")
        filled, scattered, info_stored = sem("table_filled"), sem("scattered"), sem("info_stored")
        fill_set = sem("fill_set")
        slot_i = sb("slot_i", [P, TT, TOPK], I32)
        entry = sb("entry", [P, TT, TOPK, 3], I32)
        empty = sb("empty", [P, BLOCKS, 3], I32)
        info_i = sb("info_i", [P, MAX_OVER + 1], I32)
        a4 = lambda n: sb(n, [P, TT, NG])
        a32 = lambda n: sb(n, [P, TT, NG, EPG])
        gm, es_, pg, v1, v2, m1, ev, w1, w2 = (sb(n, [P, TT]) for n in ("gm", "es_r", "pg", "v1", "v2", "m1", "ev", "w1", "w2"))
        gsub, goh = a4("gsub"), a4("goh")
        el, oh1, oh2, tmp, O, Opre = (a32(n) for n in ("el", "oh1", "oh2", "tmp_r", "O", "Opre"))
        cnt_e, over_e, cum, over_start = (sb(n, [P, NE]) for n in ("cnt_e", "over_e", "cum_e", "over_start"))
        th = sb("th", [P, NE, MAX_OVER])
        rank = sb("rank", [P, TT, NE])
        rk, en, ov, slot = (sb(n, [P, TT, TOPK]) for n in ("rk", "en", "ov", "slot_f"))
        info_f = sb("info_f", [P, MAX_OVER + 1])
        bh = sb("bh", [P, MAX_OVER, NE])

        with nc.Block() as block:
            @block.sync
            def _(sp):
                for o, i in ((ident[:, :], ident_d), (idx[:, :], idx_d), (before[:, :], before_d), (gb[:, :], norm_g),
                             (rw[:, :, :], router_w), (rb[:, :], router_b)):
                    sp.dma_start(o, i).then_inc(loaded, 16)
                sp.wait_ge(fill_set, 3)
                sp.dma_start(table.rearrange("(b p) c -> p b c", p=P), empty[:, :, :]).then_inc(filled, 16)
                for to, source, arrived in ahead:
                    sp.dma_start(to, source).then_inc(arrived, 16)
                for t in range(TT):
                    sp.wait_ge(xn_set, t + 1)
                    sp.dma_start(xn[t * P:(t + 1) * P, :], xt[:, t % 2, :]).then_inc(stored[t % 2], 16)
                for i in range(2):
                    sp.wait_ge(stored[i], 16 * (TT // 2))
                sp.wait_ge(slots_set, 4)
                sp.dma_start(info, info_i[0:1, :]).then_inc(info_stored, 16)
                sp.wait_ge(info_stored, 16)

            @block.gpsimd
            def _(pool):
                nc.gpsimd.memset(ones[:, :], 1.0).then_inc(ones_set, 1)
                nc.gpsimd.memset(mh[:, :], -0.5).then_inc(ones_set, 1)
                nc.gpsimd.memset(empty[:, :, 0:2], NOWHERE).then_inc(fill_set, 1)
                nc.gpsimd.memset(empty[:, :, 2:3], 0).then_inc(fill_set, 1)
                nc.gpsimd.iota(tok[:, :, :], [[P, TT], [0, TOPK]], base=0, channel_multiplier=1,
                               allow_small_or_imprecise_dtypes=True).then_inc(fill_set, 1)
                pool.wait_ge(ones_set, 2)
                for t in range(TT):
                    pool.wait_ge(mean_set, t + 1)
                    nc.gpsimd.tensor_tensor(rstd[:, t:t + 1], ss[:, t:t + 1], mh[:, t:t + 1], ALU.pow).then_inc(rstd_set, 1)
                pool.wait_ge(slots_set, 4)
                pool.wait_ge(filled, 16)
                for t in range(TT):
                    for c in range(TOPK):
                        pool.indirect_dma_start(table[:, :], bass.IndirectOffsetOnAxis(ap=slot_i[:, t, c:c + 1].bitcast(U32), axis=0),
                                                entry[:, t, c, :], None).then_inc(scattered, 16)
                pool.wait_ge(scattered, 16 * TT * TOPK)

            def copies(act, t):
                for q in range(4):
                    act.wait_ge(flipped, 4 * t + q + 1)
                    if t >= 2:
                        act.wait_ge(logits, t - 1)
                    nc.scalar.activation(xT[:, t % 2, 4 * q:4 * q + 4, :].rearrange("p k c -> p (k c)"), ps_t[q][:, :], ACT.Copy).then_inc(copied, 1)

            @block.scalar
            def _(act):
                def square(t):
                    if t:
                        act.wait_ge(squared, t)
                    nc.scalar.activation(junk[:, :], h_all[:, t, :], ACT.Square, accum_out=ss[:, t:t + 1]).then_inc(squared, 1)
                square(0)
                square(1)
                for t in range(TT):
                    if t + 2 < TT:
                        square(t + 2)
                    copies(act, t)
                for i, (o, n) in enumerate(((gsub, None), (ev, None))):
                    act.wait_ge(exp_in, i + 1)
                    nc.scalar.activation(o[...], o[...], ACT.Exp).then_inc(exp_out, 1)

            @block.tensor
            def _(pe):
                pe.wait_ge(loaded, 96)
                def quarter(t, q):
                    if q == 0:
                        pe.wait_ge(copied, 4 * t + 4)
                    for k in range(4 * q, 4 * q + 4):
                        ins = nc.tensor.matmul(ps_l[:, t, :], xT[:, t % 2, k, :], rw[:, k, :], start=k == 0, stop=k == KT - 1)
                    if q == 3:
                        ins.then_inc(logits, 1)
                for t in range(TT):
                    pe.wait_ge(xn_set, t + 1)
                    for q in range(4):
                        if t:
                            pe.wait_ge(copied, 4 * (t - 1) + q + 1)
                        for i in range(4):
                            k = 4 * q + i
                            ins = nc.tensor.transpose(ps_t[q][:, i * P:(i + 1) * P], xt[:, t % 2, k * P:(k + 1) * P], ident[:, :])
                        ins.then_inc(flipped, 1)
                    for q in range(4):
                        if t:
                            quarter(t - 1, q)
                for q in range(4):
                    quarter(TT - 1, q)
                pe.wait_ge(ranks_in, 2)
                pe.wait_ge(ones_set, 2)
                fl = lambda a: a[...].rearrange("p t g e -> p (t g e)")
                psr = ps_r[...].rearrange("p t e -> p (t e)")
                nc.tensor.matmul(psr, before[:, :], fl(O), start=True, stop=False)
                nc.tensor.matmul(psr, ones[:, :], fl(Opre), start=False, stop=True).then_inc(ranks_out, 1)
                nc.tensor.matmul(ps_c[:, :], ones[:, :], Opre[:, TT - 1, :, :].rearrange("p g e -> p (g e)"), start=True, stop=False)
                nc.tensor.matmul(ps_c[:, :], ones[:, :], O[:, TT - 1, :, :].rearrange("p g e -> p (g e)"), start=False, stop=True).then_inc(ranks_out, 1)

            @block.vector
            def _(dve):
                v = nc.vector
                n = [0]

                def link(ins):
                    n[0] += 1
                    ins.then_inc(chain, 1)
                    dve.wait_ge(chain, n[0])
                dve.wait_ge(loaded, 96)
                def mean(t):
                    dve.wait_ge(squared, t + 1)
                    v.tensor_scalar(ss[:, t:t + 1], ss[:, t:t + 1], 1.0 / D, RMS_EPS, ALU.mult, ALU.add).then_inc(mean_set, 1)
                mean(0)
                for t in range(TT):
                    if t + 1 < TT:
                        mean(t + 1)
                    dve.wait_ge(rstd_set, t + 1)
                    if t >= 2:
                        dve.wait_ge(stored[t % 2], 16 * (t // 2))
                        dve.wait_ge(flipped, 4 * (t - 1))
                    v.scalar_tensor_tensor(xt[:, t % 2, :], h_all[:, t, :], rstd[:, t:t + 1], gb[:, :], ALU.mult, ALU.mult).then_inc(xn_set, 1)
                dve.wait_ge(logits, TT)
                b3 = lambda a, k: a.unsqueeze(2).broadcast_to([P, TT, k])
                link(v.tensor_tensor(L[:, :, :], ps_l[:, :, :], rb[:, :].unsqueeze(1).broadcast_to([P, TT, NR]), ALU.add))
                gl = L[:, :, 0:NG]
                link(v.tensor_reduce(gm[:, :], gl, AXX, ALU.max))
                v.tensor_tensor(gsub[:, :, :], gl, b3(gm[:, :], NG), ALU.subtract).then_inc(exp_in, 1)
                link(v.tensor_tensor(goh[:, :, :], gl, b3(gm[:, :], NG), ALU.is_ge))
                link(v.tensor_tensor(goh[:, :, :], goh[:, :, :], g4.unsqueeze(1).broadcast_to([P, TT, NG]), ALU.mult))
                link(v.tensor_reduce(m1[:, :], goh[:, :, :], AXX, ALU.max))
                link(v.tensor_tensor(goh[:, :, :], goh[:, :, :], b3(m1[:, :], NG), ALU.is_equal))
                dve.wait_ge(exp_out, 1)
                link(v.tensor_reduce(es_[:, :], gsub[:, :, :], AXX, ALU.add))
                link(v.reciprocal(pg[:, :], es_[:, :]))
                link(v.tensor_scalar(goh[:, :, :], goh[:, :, :], BIG, -BIG, ALU.mult, ALU.add))
                f = lambda a: a[...].rearrange("p t g e -> p t (g e)")
                link(v.tensor_copy(el[...].rearrange("p t g e -> p (t g) e"), goh[...].rearrange("p t g -> p (t g)").unsqueeze(2).broadcast_to([P, TT * NG, EPG])))
                link(v.tensor_tensor(f(el), f(el), L[:, :, NG:], ALU.add))

                def first_of_largest(oh, top):
                    link(v.tensor_reduce(top[:, :], f(el), AXX, ALU.max))
                    link(v.tensor_tensor(f(oh), f(el), b3(top[:, :], NE), ALU.is_ge))
                    link(v.tensor_tensor(f(oh), f(oh), e32.unsqueeze(1).broadcast_to([P, TT, NE]), ALU.mult))
                    link(v.tensor_reduce(m1[:, :], f(oh), AXX, ALU.max))
                    link(v.tensor_tensor(f(oh), f(oh), b3(m1[:, :], NE), ALU.is_equal))
                first_of_largest(oh1, v1)
                link(v.scalar_tensor_tensor(f(el), f(oh1), -10.0 * BIG, f(el), ALU.mult, ALU.add))
                first_of_largest(oh2, v2)
                v.tensor_tensor(ev[:, :], v2[:, :], v1[:, :], ALU.subtract).then_inc(exp_in, 1)
                link(v.tensor_tensor(f(O), f(oh1), f(oh2), ALU.add))
                link(v.memset(Opre[:, 0, :, :], 0.0))
                for t in range(1, TT):
                    link(v.tensor_tensor(Opre[:, t, :, :], Opre[:, t - 1, :, :], O[:, t - 1, :, :], ALU.add))
                v.sem_inc(ranks_in, 2)
                dve.wait_ge(exp_out, 2)
                link(v.tensor_scalar(w2[:, :], ev[:, :], 1.0, None, ALU.add))
                link(v.reciprocal(w1[:, :], w2[:, :]))
                link(v.tensor_tensor(w1[:, :], w1[:, :], pg[:, :], ALU.mult))
                link(v.tensor_tensor(w2[:, :], w1[:, :], ev[:, :], ALU.mult))
                dve.wait_ge(ranks_out, 2)
                link(v.tensor_copy(cnt_e[:, :], ps_c[:, :]))
                link(v.tensor_copy(rank[:, :, :], ps_r[:, :, :]))
                link(v.tensor_tensor(th[:, :, :], cnt_e[:, :].unsqueeze(2).broadcast_to([P, NE, MAX_OVER]),
                                     thr.unsqueeze(1).broadcast_to([P, NE, MAX_OVER]), ALU.is_gt))
                link(v.tensor_reduce(over_e[:, :], th[:, :, :], AXX, ALU.add))
                link(v.tensor_tensor_scan(cum[:, :], over_e[:, :], over_e[:, :], 0.0, ALU.add, ALU.bypass))
                link(v.tensor_tensor(over_start[:, :], cum[:, :], over_e[:, :], ALU.subtract))
                link(v.tensor_tensor(bh[:, :, :], cum[:, :].unsqueeze(1).broadcast_to([P, MAX_OVER, NE]),
                                     blk.unsqueeze(2).broadcast_to([P, MAX_OVER, NE]), ALU.is_le))
                link(v.tensor_reduce(info_f[:, 0:MAX_OVER], bh[:, :, :], AXX, ALU.add))
                link(v.tensor_scalar(info_f[:, 0:MAX_OVER], info_f[:, 0:MAX_OVER], float(NE - 1), None, ALU.min))
                link(v.tensor_copy(info_f[:, MAX_OVER:], cum[:, NE - 1:NE]))
                v.tensor_copy(info_i[:, :], info_f[:, :]).then_inc(slots_set, 1)
                for c, oh in enumerate((oh1, oh2)):
                    for o, col in ((rk, None), (en, eno), (ov, over_start[:, :])):
                        other = rank[:, :, :] if col is None else col.unsqueeze(1).broadcast_to([P, TT, NE])
                        link(v.tensor_tensor(f(tmp), f(oh), other, ALU.mult))
                        link(v.tensor_reduce(o[:, :, c:c + 1], f(tmp), AXX, ALU.add))
                fl = lambda a: a[...].rearrange("p t c -> p (t c)")
                link(v.tensor_tensor(fl(ov), fl(ov), fl(en), ALU.subtract))
                link(v.tensor_scalar(fl(ov), fl(ov), float(P), float(P * NE - P), ALU.mult, ALU.add))
                link(v.scalar_tensor_tensor(fl(ov), fl(rk), float(P), fl(ov), ALU.is_ge, ALU.mult))
                link(v.scalar_tensor_tensor(fl(slot), fl(en), float(P), fl(rk), ALU.mult, ALU.add))
                link(v.tensor_tensor(fl(slot), fl(slot), fl(ov), ALU.add))
                v.tensor_copy(slot_i[:, :, :], slot[:, :, :]).then_inc(slots_set, 1)
                dve.wait_ge(fill_set, 3)
                link(v.tensor_copy(entry[:, :, :, 0], tok[:, :, :]))
                link(v.tensor_scalar(rk[:, :, :], tok[:, :, :], 2.0, None, ALU.mult))
                link(v.tensor_scalar(rk[:, :, 1:2], rk[:, :, 1:2], 1.0, None, ALU.add))
                v.tensor_copy(entry[:, :, :, 1], rk[:, :, :]).then_inc(slots_set, 1)
                link(v.tensor_copy(entry[:, :, 0, 2].bitcast(F32), w1[:, :]))
                v.tensor_copy(entry[:, :, 1, 2].bitcast(F32), w2[:, :]).then_inc(slots_set, 1)


RAWS, SPLITS = 4, 3
GC, DC = CHUNKS, HID // P
PER = 2 * GC + DC
NB = D // HALF
XR = KT // KQ


def first_loads(w_gate, raw, w_loaded):
    assert RAWS == GC
    gv = w_gate.rearrange("e (p k) h -> e p k h", p=P)
    return [(raw[:, i, :], gv[0, :, i * KQ:(i + 1) * KQ, :].rearrange("p k h -> p (k h)"), w_loaded[i]) for i in range(RAWS)]


def experts(nc, xn, table, w_gate, w_up, w_down, ident_d, yk, raw, w_loaded):
    gv = w_gate.rearrange("e (p k) h -> e p k h", p=P)
    uv = w_up.rearrange("e (p k) h -> e p k h", p=P)
    dv = w_down.rearrange("e (p k) n -> e p k n", p=P)
    with ExitStack() as ctx:
        sb = lambda n, s, d=F32: ctx.enter_context(nc.sbuf_tensor(n, s, d))
        sem = semaphores(nc, ctx)
        ident = sb("ident_e", [P, P])
        slots = sb("slots", [P, BLOCKS, 3], I32)
        hi, lo = sb("w_hi_e", [P, SPLITS, 4 * HALF], F32R), sb("w_lo_e", [P, SPLITS, 4 * HALF], F32R)
        xg = sb("xg", [P, D])
        xT_hi, xT_lo = sb("xT_hi", [P, KT, P], F32R), sb("xT_lo", [P, KT, P], F32R)
        gidx, sidx, sw = sb("gidx", [P, 1], I32), sb("sidx", [P, 1], I32), sb("sw", [P, 1], I32)
        th, hid = sb("th_e", [P, HID]), sb("hid", [P, HID])
        hT_hi, hT_lo = sb("hT_hi", [P, DC, P], F32R), sb("hT_lo", [P, DC, P], F32R)
        y_sb = sb("y_sb", [P, D])
        ps_g, ps_u = (ctx.enter_context(nc.psum_tensor(n, [P, HALF], F32)) for n in ("ps_g", "ps_u"))
        ps_x = [ctx.enter_context(nc.psum_tensor(f"ps_x{i}", [P, HALF], F32)) for i in range(2)]
        ps_y = [ctx.enter_context(nc.psum_tensor(f"ps_y{i}", [P, HALF], F32)) for i in range(NB)]

        const_loaded, slots_loaded, cleared = sem("const_loaded_e"), sem("slots_loaded"), sem("cleared")
        seen = sem("seen_e")
        hi_set, lo_set, used = sem("hi_set_e"), sem("lo_set_e"), sem("used_e")
        gidx_set, sidx_set, gathered, scattered = sem("gidx_set"), sem("sidx_set"), sem("gathered"), sem("scattered_e")
        x_flip, x_hi, x_lo = sem("x_flip"), sem("x_hi"), sem("x_lo")
        tanh_set, act_set, hid_set = sem("tanh_set"), sem("act_set"), sem("hid_set")
        h_flip, h_hi, h_lo = sem("h_flip"), sem("h_hi"), sem("h_lo")
        y_set = sem("y_set_e")
        chunk = lambda e, i: 2 * GC + PER * (e - 1) + i
        TAIL = chunk(NE, 0)
        y_done = lambda e: chunk(e + 2, 0)
        raw_slot = lambda i: i % RAWS
        split_slot = lambda i: (i + 2 * GC) % SPLITS
        fills = lambda e, i: 2 * GC // RAWS + PER // RAWS * (e - 1) + i // RAWS + 1
        flat = lambda a: a.rearrange("p k c -> p (k c)")
        assert 2 * GC % RAWS == 0 and PER % RAWS == 0 and PER % SPLITS == 0

        with nc.Block() as block:
            @block.sync
            def _(sp):
                sp.dma_start(ident[:, :], ident_d).then_inc(const_loaded, 16)
                sp.dma_start(slots[:, :, :], table.rearrange("(b p) c -> p b c", p=P)).then_inc(slots_loaded, 16)

                def load(e, i, n, s):
                    sp.wait_ge(lo_set, n - RAWS + 1)
                    if i < 2 * GC:
                        v = (gv, uv)[i // GC]
                        src = v[bass.ds(e, 1), :, (i % GC) * KQ:(i % GC + 1) * KQ, :].rearrange("a p k h -> (a p) (k h)")
                    else:
                        src = dv[bass.ds(e, 1), :, i - 2 * GC, :].rearrange("a p n -> (a p) n")
                    sp.dma_start(raw[:, s, :], src).then_inc(w_loaded[s], 16)
                for i in range(RAWS, 2 * GC):
                    load(0, i, i, raw_slot(i))
                with sp.Fori(1, NE) as e:
                    for i in range(PER):
                        load(e if i < 2 * GC else e - 1, i, chunk(e, i), raw_slot(i))
                for i in range(DC):
                    load(NE - 1, 2 * GC + i, TAIL + i, raw_slot(i))

            @block.gpsimd
            def _(pool):
                def gather(e, free):
                    if free:
                        pool.wait_ge(x_flip, XR * e)
                        pool.wait_ge(gathered, 16 * e)
                    nc.gpsimd.tensor_copy(gidx[:, :], slots[:, bass.ds(e, 1), 0]).then_inc(gidx_set, 1)
                    pool.wait_ge(gidx_set, e + 1)
                    pool.sem_inc(seen, 1)
                    pool.indirect_dma_start(xg[:, :], None, xn[:, :], bass.IndirectOffsetOnAxis(ap=gidx[:, :].bitcast(U32), axis=0),
                                            bounds_check=SEQ - 1, oob_is_err=False).then_inc(gathered, 16)

                def scatter(e, free):
                    if free:
                        pool.wait_ge(scattered, 16 * e)
                        pool.wait_ge(y_set, NB * e)
                    nc.gpsimd.tensor_copy(sidx[:, :], slots[:, bass.ds(e, 1), 1])
                    nc.gpsimd.tensor_copy(sw[:, :], slots[:, bass.ds(e, 1), 2]).then_inc(sidx_set, 1)
                    pool.wait_ge(sidx_set, e + 1)
                    pool.wait_ge(y_set, NB * (e + 1))
                    pool.sem_inc(seen, 1)
                    pool.indirect_dma_start(yk[:, :], bass.IndirectOffsetOnAxis(ap=sidx[:, :].bitcast(U32), axis=0), y_sb[:, :], None,
                                            bounds_check=TOPK * SEQ - 1, oob_is_err=False).then_inc(scattered, 16)
                nc.gpsimd.memset(xg[:, :], 0.0).then_inc(cleared, 1)
                pool.wait_ge(cleared, 1)
                pool.wait_ge(slots_loaded, 16)
                gather(0, False)
                gather(1, True)
                gather(2, True)
                scatter(0, False)
                with pool.Fori(3, NE) as e:
                    gather(e, True)
                    scatter(e - 2, True)
                scatter(NE - 2, True)
                scatter(NE - 1, True)
                pool.wait_ge(scattered, 16 * NE)

            def split_hi(act, i, n, s, filled, free=True):
                act.wait_ge(w_loaded[i % RAWS], 16 * filled)
                if free:
                    act.wait_ge(used, n - SPLITS + 1)
                nc.scalar.activation(hi[:, s, :], raw[:, i % RAWS, :], ACT.Copy).then_inc(hi_set, 1)

            def x_to_hi(act, e, q):
                act.wait_ge(x_flip, XR * e + q + 1)
                nc.scalar.activation(flat(xT_hi[:, KQ * q:KQ * (q + 1), :]), ps_x[q % 2][:, :], ACT.Copy).then_inc(x_hi, 1)

            def h_to_hi(act, count):
                act.wait_ge(h_flip, count)
                nc.scalar.activation(flat(hT_hi[:, :, :]), ps_x[0][:, :], ACT.Copy).then_inc(h_hi, 1)

            def tanh(act, e, first=False):
                if not first:
                    act.wait_ge(hid_set, e)
                nc.scalar.activation(th[:, :], ps_g[:, :], ACT.Tanh, scale=0.5).then_inc(tanh_set, 1)

            def y_out(act, e, products):
                act.wait_ge(used, products)
                act.wait_ge(sidx_set, e + 1)
                for b in range(NB):
                    nc.scalar.activation(y_sb[:, b * HALF:(b + 1) * HALF], ps_y[b][:, :], ACT.Copy, scale=sw[:, :].bitcast(F32)).then_inc(y_set, 1)

            def scalar_turn(act, e, first=False, last=False):
                for i in range(PER):
                    split_hi(act, i, chunk(e, i), split_slot(i), fills(e, i))
                    if i in (0, 1):
                        x_to_hi(act, e, i + 2)
                    if i == 2 and not first:
                        y_out(act, e - 2, y_done(e - 2))
                    if i == GC + SPLITS - 1:
                        h_to_hi(act, e)
                    if i == 2 * GC - 1:
                        tanh(act, e)
                    if i in (PER - 2, PER - 1) and not last:
                        x_to_hi(act, e + 1, i - (PER - 2))

            @block.scalar
            def _(act):
                for i in range(2 * GC):
                    split_hi(act, i, i, i % SPLITS, i // RAWS + 1, i >= SPLITS)
                    if i == SPLITS - 1:
                        for q in range(XR):
                            x_to_hi(act, 0, q)
                    if i == GC + SPLITS - 1:
                        tanh(act, 0, first=True)
                for q in range(2):
                    x_to_hi(act, 1, q)
                scalar_turn(act, 1, first=True)
                with act.Fori(2, NE - 1) as e:
                    scalar_turn(act, e)
                scalar_turn(act, NE - 1, last=True)
                for i in range(DC):
                    split_hi(act, i, TAIL + i, split_slot(i), fills(NE, i))
                    if i == 0:
                        h_to_hi(act, NE)
                    if i == 2:
                        y_out(act, NE - 2, y_done(NE - 2))
                y_out(act, NE - 1, TAIL + DC)

            def split_lo(dve, i, n, s):
                dve.wait_ge(hi_set, n + 1)
                nc.vector.tensor_tensor(lo[:, s, :], raw[:, i % RAWS, :], hi[:, s, :].bitcast(F32), ALU.subtract).then_inc(lo_set, 1)

            def x_to_lo(dve, e, q):
                dve.wait_ge(x_hi, XR * e + q + 1)
                ks = slice(KQ * q, KQ * (q + 1))
                nc.vector.tensor_tensor(flat(xT_lo[:, ks, :]), ps_x[q % 2][:, :], flat(xT_hi[:, ks, :]).bitcast(F32), ALU.subtract).then_inc(x_lo, 1)

            def h_to_lo(dve, count):
                dve.wait_ge(h_hi, count)
                nc.vector.tensor_tensor(flat(hT_lo[:, :, :]), ps_x[0][:, :], flat(hT_hi[:, :, :]).bitcast(F32), ALU.subtract).then_inc(h_lo, 1)

            def swiglu(dve, e, products, first=False):
                dve.wait_ge(used, products)
                dve.wait_ge(tanh_set, e + 1)
                if not first:
                    dve.wait_ge(h_flip, e)
                nc.vector.scalar_tensor_tensor(hid[:, :], th[:, :], 1.0, ps_g[:, :], ALU.add, ALU.mult).then_inc(act_set, 1)
                dve.wait_ge(act_set, e + 1)
                nc.vector.scalar_tensor_tensor(hid[:, :], hid[:, :], 0.5, ps_u[:, :], ALU.mult, ALU.mult).then_inc(hid_set, 1)

            def vector_turn(dve, e, last=False):
                for i in range(PER):
                    split_lo(dve, i, chunk(e, i), split_slot(i))
                    if i in (0, 1):
                        x_to_lo(dve, e, i + 2)
                    if i == GC + SPLITS - 1:
                        h_to_lo(dve, e)
                    if i in (PER - 2, PER - 1) and not last:
                        x_to_lo(dve, e + 1, i - (PER - 2))
                    if i == PER - 2:
                        swiglu(dve, e, chunk(e, 2 * GC))

            @block.vector
            def _(dve):
                for i in range(2 * GC):
                    split_lo(dve, i, i, i % SPLITS)
                    if i == SPLITS - 1:
                        for q in range(XR):
                            x_to_lo(dve, 0, q)
                swiglu(dve, 0, 2 * GC, first=True)
                for q in range(2):
                    x_to_lo(dve, 1, q)
                with dve.Fori(1, NE - 1) as e:
                    vector_turn(dve, e)
                vector_turn(dve, NE - 1, last=True)
                for i in range(DC):
                    split_lo(dve, i, TAIL + i, split_slot(i))
                    if i == 0:
                        h_to_lo(dve, NE)

            def three(o, a_hi, a_lo, s, cols, start, stop):
                mm = nc.tensor.matmul
                mm(o, a_hi, hi[:, s, cols], start=start, stop=False)
                mm(o, a_hi, lo[:, s, cols], start=False, stop=False)
                return mm(o, a_lo, hi[:, s, cols], start=False, stop=stop)

            def flip_x(pe, e, q):
                if q == 0:
                    pe.wait_ge(gathered, 16 * (e + 1))
                if not (isinstance(e, int) and e == 0 and q < 2):
                    pe.wait_ge(x_lo, XR * e + q - 1)
                for j in range(KQ):
                    ins = nc.tensor.transpose(ps_x[q % 2][:, j * P:(j + 1) * P], xg[:, KQ * q + j::KT], ident[:, :])
                ins.then_inc(x_flip, 1)

            def flip_hid(pe, count):
                pe.wait_ge(hid_set, count)
                for j in range(DC):
                    ins = nc.tensor.transpose(ps_x[0][:, j * P:(j + 1) * P], hid[:, j::DC], ident[:, :])
                ins.then_inc(h_flip, 1)

            def gate_up(pe, e, i, n, s):
                if i < GC:
                    pe.wait_ge(x_lo, XR * e + i + 1)
                pe.wait_ge(lo_set, n + 1)
                o = (ps_g, ps_u)[i // GC][:, :]
                for j in range(KQ):
                    k = (i % GC) * KQ + j
                    ins = three(o, xT_hi[:, k, :], xT_lo[:, k, :], s, slice(j * HALF, (j + 1) * HALF), k == 0, k == KT - 1)
                ins.then_inc(used, 1)

            def down(pe, q, n, s):
                pe.wait_ge(lo_set, n + 1)
                for b in range(NB):
                    ins = three(ps_y[b][:, :], hT_hi[:, q, :], hT_lo[:, q, :], s, slice(b * HALF, (b + 1) * HALF), q == 0, q == DC - 1)
                ins.then_inc(used, 1)

            def tensor_turn(pe, e, first=False, last=False):
                pe.wait_ge(hid_set, e)
                for i in range(2 * GC):
                    gate_up(pe, e, i, chunk(e, i), split_slot(i))
                    if i == GC - 1:
                        flip_hid(pe, e)
                pe.wait_ge(h_lo, e)
                for q in range(DC):
                    if not last:
                        flip_x(pe, e + 1, q)
                    if q == 0 and not first:
                        pe.wait_ge(y_set, NB * (e - 1))
                    down(pe, q, chunk(e, 2 * GC + q), split_slot(2 * GC + q))

            @block.tensor
            def _(pe):
                pe.wait_ge(const_loaded, 16)
                pe.wait_ge(cleared, 1)
                for q in range(XR):
                    flip_x(pe, 0, q)
                for i in range(2 * GC):
                    gate_up(pe, 0, i, i, i % SPLITS)
                for q in range(XR):
                    flip_x(pe, 1, q)
                tensor_turn(pe, 1, first=True)
                with pe.Fori(2, NE - 1) as e:
                    tensor_turn(pe, e)
                tensor_turn(pe, NE - 1, last=True)
                flip_hid(pe, NE)
                pe.wait_ge(h_lo, NE)
                pe.wait_ge(y_set, NB * (NE - 1))
                for q in range(DC):
                    down(pe, q, TAIL + q, split_slot(q))


def experts_over(nc, xn, table, info, w_gate, w_up, w_down, ident_d, yk):
    gv = w_gate.rearrange("e (p k) h -> e p k h", p=P)
    uv = w_up.rearrange("e (p k) h -> e p k h", p=P)
    dv = w_down.rearrange("e (p k) n -> e p k n", p=P)
    with ExitStack() as ctx:
        sb = lambda n, s, d=F32: ctx.enter_context(nc.sbuf_tensor(n, s, d))
        sem = semaphores(nc, ctx)
        ident = sb("ident_o", [P, P])
        slots = sb("slots_o", [P, MAX_OVER, 3], I32)
        infos = sb("infos", [1, MAX_OVER + 1], I32)
        w = sb("w_o", [P, RAWS, 4 * HALF])
        xg, y_sb = sb("xg_o", [P, D]), sb("y_sb_o", [P, D])
        xT, hT = sb("xT_o", [P, KT, P]), sb("hT_o", [P, DC, P])
        th, hid = sb("th_o", [P, HID]), sb("hid_o", [P, HID])
        gidx, sidx, sw = sb("gidx_o", [P, 1], I32), sb("sidx_o", [P, 1], I32), sb("sw_o", [P, 1], I32)
        ps_g, ps_u, ps_h = (ctx.enter_context(nc.psum_tensor(n, [P, HALF], F32)) for n in ("ps_go", "ps_uo", "ps_ho"))
        ps_y = [ctx.enter_context(nc.psum_tensor(f"ps_yo{i}", [P, HALF], F32)) for i in range(NB)]
        loaded, slots_loaded, cleared = sem("loaded_o"), sem("slots_loaded_o"), sem("cleared_o")
        w_loaded = [sem(f"w_loaded_o{i}") for i in range(RAWS)]
        seen, blocks_done = sem("seen_o"), sem("blocks_done")
        picked, gathered, scattered, used = sem("picked_o"), sem("gathered_o"), sem("scattered_o"), sem("used_o")
        x_flip, x_set, h_flip, h_set = sem("x_flip_o"), sem("x_set_o"), sem("h_flip_o"), sem("h_set_o")
        tanh_set, act_set, hid_set, y_set = sem("tanh_o"), sem("act_o"), sem("hid_set_o"), sem("y_set_o")
        flat = lambda a: a.rearrange("p k c -> p (k c)")

        with nc.Block() as block:
            @block.sync
            def _(sp):
                sp.dma_start(infos[:, :], info).then_inc(loaded, 16)
                sp.dma_start(ident[:, :], ident_d).then_inc(loaded, 16)
                sp.dma_start(slots[:, :, :], table.rearrange("(b p) c -> p b c", p=P)[:, NE:, :]).then_inc(slots_loaded, 16)
                sp.wait_ge(loaded, 32)
                blocks = sp.value_load(infos[0:1, MAX_OVER:MAX_OVER + 1], min_val=0, max_val=MAX_OVER)
                with sp.Fori(0, MAX_OVER) as j:
                    with sp.If(j < blocks):
                        sp.wait_ge(blocks_done, j + 1)
                        e = sp.value_load(infos[0:1, bass.ds(j, 1)], min_val=0, max_val=NE - 1)
                        for i in range(PER):
                            if i >= RAWS:
                                sp.wait_ge(used, PER * j + i - RAWS + 1)
                            if i < 2 * GC:
                                v = (gv, uv)[i // GC]
                                src = v[bass.ds(e, 1), :, (i % GC) * KQ:(i % GC + 1) * KQ, :].rearrange("a p k h -> (a p) (k h)")
                            else:
                                src = dv[bass.ds(e, 1), :, i - 2 * GC, :].rearrange("a p n -> (a p) n")
                            sp.dma_start(w[:, i % RAWS, :], src).then_inc(w_loaded[i % RAWS], 16)

            @block.gpsimd
            def _(pool):
                pool.sem_inc(blocks_done, 1)
                nc.gpsimd.memset(xg[:, :], 0.0).then_inc(cleared, 1)
                pool.wait_ge(cleared, 1)
                pool.wait_ge(slots_loaded, 16)
                pool.wait_ge(loaded, 32)
                blocks = pool.value_load(infos[0:1, MAX_OVER:MAX_OVER + 1], min_val=0, max_val=MAX_OVER)
                with pool.Fori(0, MAX_OVER) as j:
                    with pool.If(j < blocks):
                        for c, o in enumerate((gidx, sidx, sw)):
                            nc.gpsimd.tensor_copy(o[:, :], slots[:, bass.ds(j, 1), c]).then_inc(picked, 1)
                        pool.wait_ge(picked, 3 * (j + 1))
                        pool.sem_inc(seen, 1)
                        pool.indirect_dma_start(xg[:, :], None, xn[:, :], bass.IndirectOffsetOnAxis(ap=gidx[:, :].bitcast(U32), axis=0),
                                                bounds_check=SEQ - 1, oob_is_err=False).then_inc(gathered, 16)
                        pool.wait_ge(y_set, NB * (j + 1))
                        pool.sem_inc(seen, 1)
                        pool.indirect_dma_start(yk[:, :], bass.IndirectOffsetOnAxis(ap=sidx[:, :].bitcast(U32), axis=0), y_sb[:, :], None,
                                                bounds_check=TOPK * SEQ - 1, oob_is_err=False).then_inc(scattered, 16)
                        pool.wait_ge(scattered, 16 * (j + 1))
                        pool.sem_inc(blocks_done, 1)

            @block.scalar
            def _(act):
                act.wait_ge(loaded, 32)
                blocks = act.value_load(infos[0:1, MAX_OVER:MAX_OVER + 1], min_val=0, max_val=MAX_OVER)
                with act.Fori(0, MAX_OVER) as j:
                    with act.If(j < blocks):
                        for q in range(XR):
                            act.wait_ge(x_flip, XR * j + q + 1)
                            nc.scalar.activation(flat(xT[:, KQ * q:KQ * (q + 1), :]), ps_y[q][:, :], ACT.Copy).then_inc(x_set, 1)
                        act.wait_ge(used, PER * j + GC)
                        nc.scalar.activation(th[:, :], ps_g[:, :], ACT.Tanh, scale=0.5).then_inc(tanh_set, 1)
                        act.wait_ge(h_flip, j + 1)
                        nc.scalar.activation(flat(hT[:, :, :]), ps_h[:, :], ACT.Copy).then_inc(h_set, 1)
                        act.wait_ge(used, PER * (j + 1))
                        act.wait_ge(picked, 3 * (j + 1))
                        act.wait_ge(blocks_done, j + 1)
                        for b in range(NB):
                            nc.scalar.activation(y_sb[:, b * HALF:(b + 1) * HALF], ps_y[b][:, :], ACT.Copy, scale=sw[:, :].bitcast(F32)).then_inc(y_set, 1)

            @block.vector
            def _(dve):
                dve.wait_ge(loaded, 32)
                blocks = dve.value_load(infos[0:1, MAX_OVER:MAX_OVER + 1], min_val=0, max_val=MAX_OVER)
                with dve.Fori(0, MAX_OVER) as j:
                    with dve.If(j < blocks):
                        dve.wait_ge(used, PER * j + 2 * GC)
                        dve.wait_ge(tanh_set, j + 1)
                        nc.vector.scalar_tensor_tensor(hid[:, :], th[:, :], 1.0, ps_g[:, :], ALU.add, ALU.mult).then_inc(act_set, 1)
                        dve.wait_ge(act_set, j + 1)
                        nc.vector.scalar_tensor_tensor(hid[:, :], hid[:, :], 0.5, ps_u[:, :], ALU.mult, ALU.mult).then_inc(hid_set, 1)

            @block.tensor
            def _(pe):
                pe.wait_ge(loaded, 32)
                pe.wait_ge(cleared, 1)
                blocks = pe.value_load(infos[0:1, MAX_OVER:MAX_OVER + 1], min_val=0, max_val=MAX_OVER)
                with pe.Fori(0, MAX_OVER) as j:
                    with pe.If(j < blocks):
                        pe.wait_ge(gathered, 16 * (j + 1))
                        pe.wait_ge(blocks_done, j + 1)
                        for q in range(XR):
                            for i in range(KQ):
                                ins = nc.tensor.transpose(ps_y[q][:, i * P:(i + 1) * P], xg[:, KQ * q + i::KT], ident[:, :])
                            ins.then_inc(x_flip, 1)
                        pe.wait_ge(x_set, XR * (j + 1))
                        for i in range(PER):
                            pe.wait_ge(w_loaded[i % RAWS], 16 * (PER // RAWS * j + i // RAWS + 1))
                            if i == 2 * GC:
                                pe.wait_ge(hid_set, j + 1)
                                for m in range(DC):
                                    ins = nc.tensor.transpose(ps_h[:, m * P:(m + 1) * P], hid[:, m::DC], ident[:, :])
                                ins.then_inc(h_flip, 1)
                                pe.wait_ge(h_set, j + 1)
                            for m in range(4):
                                k = (i % GC) * KQ + m
                                ws = w[:, i % RAWS, m * HALF:(m + 1) * HALF]
                                if i < 2 * GC:
                                    ins = nc.tensor.matmul((ps_g, ps_u)[i // GC][:, :], xT[:, k, :], ws, start=k == 0, stop=k == KT - 1)
                                else:
                                    q = i - 2 * GC
                                    ins = nc.tensor.matmul(ps_y[m][:, :], hT[:, q, :], ws, start=q == 0, stop=q == DC - 1)
                            ins.then_inc(used, 1)


def finish(nc, h_all, yk, norm_g, out):
    yv = yk.rearrange("(t p c) d -> p t c d", p=P, c=TOPK)
    ov = out.rearrange("(t p) d -> p t d", p=P)
    with ExitStack() as ctx:
        sb = lambda n, s, d=F32: ctx.enter_context(nc.sbuf_tensor(n, s, d))
        sem = semaphores(nc, ctx)
        gb, junk = sb("gb_f", [P, D]), sb("junk_f", [P, D])
        y2, o = sb("y2", [P, 2, TOPK, D]), sb("o_f", [P, 2, D])
        ss, rstd, mh = sb("ss_f", [P, TT]), sb("rstd_f", [P, TT]), sb("mh_f", [P, 1])
        loaded, mh_set, added = sem("loaded_f"), sem("mh_set_f"), sem("added_f")
        y_loaded = [sem(f"y2_loaded{i}") for i in range(2)]
        stored = [sem(f"stored_f{i}") for i in range(2)]
        squared, mean_set, rstd_set, out_set = sem("squared_f"), sem("mean_f"), sem("rstd_f_set"), sem("out_set_f")
        with nc.Block() as block:
            @block.sync
            def _(sp):
                sp.dma_start(gb[:, :], norm_g).then_inc(loaded, 16)
                for t in range(TT):
                    if t >= 2:
                        sp.wait_ge(added, 2 * (t - 1))
                    sp.dma_start(y2[:, t % 2, :, :], yv[:, t, :, :]).then_inc(y_loaded[t % 2], 16)
                    if t >= 2:
                        sp.wait_ge(out_set, t - 1)
                        sp.dma_start(ov[:, t - 2, :], o[:, t % 2, :]).then_inc(stored[t % 2], 16)
                for t in (TT - 2, TT - 1):
                    sp.wait_ge(out_set, t + 1)
                    sp.dma_start(ov[:, t, :], o[:, t % 2, :]).then_inc(stored[t % 2], 16)
                for i in range(2):
                    sp.wait_ge(stored[i], 16 * (TT // 2))

            @block.gpsimd
            def _(pool):
                nc.gpsimd.memset(mh[:, :], -0.5).then_inc(mh_set, 1)
                pool.wait_ge(mh_set, 1)
                for t in range(TT):
                    pool.wait_ge(mean_set, t + 1)
                    nc.gpsimd.tensor_tensor(rstd[:, t:t + 1], ss[:, t:t + 1], mh[:, :], ALU.pow).then_inc(rstd_set, 1)

            @block.scalar
            def _(act):
                for t in range(TT):
                    act.wait_ge(added, 2 * (t + 1))
                    if t:
                        act.wait_ge(squared, t)
                    nc.scalar.activation(junk[:, :], h_all[:, t, :], ACT.Square, accum_out=ss[:, t:t + 1]).then_inc(squared, 1)

            @block.vector
            def _(dve):
                v = nc.vector

                def scale(t):
                    dve.wait_ge(rstd_set, t + 1)
                    dve.wait_ge(loaded, 16)
                    if t >= 2:
                        dve.wait_ge(stored[t % 2], 16 * (t // 2))
                    v.scalar_tensor_tensor(o[:, t % 2, :], h_all[:, t, :], rstd[:, t:t + 1], gb[:, :], ALU.mult, ALU.mult).then_inc(out_set, 1)
                for t in range(TT):
                    dve.wait_ge(y_loaded[t % 2], 16 * (t // 2 + 1))
                    for c in range(TOPK):
                        v.tensor_tensor(h_all[:, t, :], h_all[:, t, :], y2[:, t % 2, c, :], ALU.add).then_inc(added, 1)
                        dve.wait_ge(added, 2 * t + c + 1)
                    if t:
                        scale(t - 1)
                    dve.wait_ge(squared, t + 1)
                    v.tensor_scalar(ss[:, t:t + 1], ss[:, t:t + 1], 1.0 / D, RMS_EPS, ALU.mult, ALU.add).then_inc(mean_set, 1)
                scale(TT - 1)


def mask_tables():
    r, c = np.arange(P)[:, None], np.arange(P)[None, :]
    ident = np.eye(P, dtype=np.float32)
    same_head = (r // HEAD == c // HEAD).astype(np.float32)
    head_of = np.stack([(np.arange(P) // HEAD == h) for h in range(2)], 1).astype(np.float32)
    before, upto = r < c, r <= c
    score_mask = np.concatenate([c < r, upto, before, upto], 1).astype(np.float32)
    levels = [((r >> i) % 2 == 0) & (c >> i == (r >> i) + 1) for i in range(LEVELS)]
    level_mask = np.concatenate([np.tile(m if i == 0 else m[:, (c[0] >> i) % 2 == 1], (1, 8 if i else 4))
                                 for i, m in enumerate(levels)], 1).astype(np.float32)
    heads = AW // HEAD
    i, k = np.arange(P)[:, None], np.arange(KW)[None, :]
    dist = np.abs(i - (k - HEAD)).astype(np.float32)
    seen = (k // HEAD == i // HEAD) | (k // HEAD == i // HEAD + 1)
    slope = (2.0 ** (-8.0 * np.arange(1, heads + 1) / heads)).astype(np.float32)
    bias = np.where(seen[:, None, :], -slope[None, :, None] * dist[:, None, :], np.float32(NEVER)).astype(np.float32).reshape(P, -1)
    cols = np.zeros(NG + 3 * NE + 2 * MAX_OVER, np.float32)
    known = np.concatenate([NG - np.arange(NG), NE - np.arange(NE), np.arange(NE),
                            P * (1 + np.arange(MAX_OVER)), np.arange(MAX_OVER)])
    cols[:known.size] = known
    return dict(ident=ident, same_head=same_head, head_of=head_of, score_mask=score_mask, level_mask=level_mask,
                bias=bias, cols=np.tile(cols, (P, 1)), before=before.astype(np.float32))


def lay_out(inputs):
    a = {n: np.asarray(v) for n, v in inputs.items()}
    one = lambda n: a[n][0]
    per_channel = lambda v: v.reshape(-1, P).T
    across = lambda v: np.tile(v.reshape(1, -1), (P, 1))
    w = one("w_in")
    starts = [P * i for i in range(COLT)] + [IN_TOTAL - P]
    mu = one("shift_mu")
    mu_lora = np.zeros((P, 3), np.float32)
    for i in range(3):
        part = mu[3 * RW + i * P:min(3 * RW + (i + 1) * P, RWKV_IN)]
        mu_lora[:part.size, i] = part
    router_w = np.concatenate([one("router_group_w"), one("router_expert_w").transpose(1, 0, 2).reshape(D, NE)], 1)
    arrays = dict(
        x=a["x"][0],
        norm_mix_g=per_channel(one("norm_mix_g")),
        w_in=np.stack([w[:, s:s + P].reshape(KT, P, P).transpose(1, 0, 2) for s in starts]),
        rwkv_params=np.stack([per_channel(v) for v in (
            mu[0:RW], mu[RW:2 * RW], mu[2 * RW:3 * RW], one("w0"), one("a0"), one("k_k"), one("k_a"),
            one("r_k").reshape(-1), one("ln_x_g"), one("ln_x_b"))], 2),
        mu_lora=mu_lora,
        w_lora_up=one("w_lora_up"), a_lora_up=one("a_lora_up"), g_lora_up=one("g_lora_up"),
        sinks=across(one("attn_sinks")),
        w_out=one("w_out"),
        norm_ffn_g=across(one("norm_ffn_g")),
        router_w=router_w.reshape(KT, P, NR).transpose(1, 0, 2),
        router_b=across(np.concatenate([one("router_group_b"), one("router_expert_b").reshape(-1)])),
        w_gate=one("expert_w_gate"), w_up=one("expert_w_up"), w_down=one("expert_w_down"),
        norm_final_g=across(a["norm_final_g"]))
    arrays.update(mask_tables())
    return {f"in_{n}": np.ascontiguousarray(v) for n, v in arrays.items()}


def build(nc, t, out):
    scratch = lambda n, s, d=F32: nc.dram_tensor(n, s, d, kind="Internal").ap()
    zT, yT = scratch("zT", (IN_TOTAL, SEQ)), scratch("yT", (D, SEQ))
    xn, yk = scratch("xn", (SEQ, D)), scratch("yk", (TOPK * SEQ, D))
    table, info = scratch("table", (BLOCKS * P, 3), I32), scratch("info", (1, MAX_OVER + 1), I32)
    project_in(nc, t["x"], t["norm_mix_g"], t["w_in"], zT, t["ident"])
    mix_heads(nc, zT, t["rwkv_params"], t["mu_lora"], t["w_lora_up"], t["a_lora_up"], t["g_lora_up"], t["sinks"], t["bias"],
              [t[n] for n in ("ident", "same_head", "head_of", "score_mask", "level_mask")], yT)
    with ExitStack() as ctx:
        h_all = ctx.enter_context(nc.sbuf_tensor("h_all", [P, TT, D], F32))
        project_out(nc, yT, t["w_out"], t["x"], h_all)
        weights = ctx.enter_context(ExitStack())
        sem = semaphores(nc, weights)
        w_loaded = [sem(f"w_loaded_e{i}") for i in range(RAWS)]
        raw = weights.enter_context(nc.sbuf_tensor("raw", [P, RAWS, 4 * HALF], F32))
        route(nc, h_all, t["norm_ffn_g"], t["router_w"], t["router_b"], (t["ident"], t["cols"], t["before"]), xn, table, info,
              first_loads(t["w_gate"], raw, w_loaded))
        experts(nc, xn, table, t["w_gate"], t["w_up"], t["w_down"], t["ident"], yk, raw, w_loaded)
        weights.close()
        experts_over(nc, xn, table, info, t["w_gate"], t["w_up"], t["w_down"], t["ident"], yk)
        finish(nc, h_all, yk, t["norm_final_g"], out)


def kernel(**inputs):
    import concourse.bacc as bacc
    from concourse.bass_utils import run_bass_kernel_spmd

    nc = bacc.Bacc("TRN2", target_bir_lowering=False, num_devices=1)
    arrays = lay_out(inputs)
    args = {n[3:]: nc.dram_tensor(n, v.shape, mybir.dt.from_np(v.dtype), kind="ExternalInput").ap() for n, v in arrays.items()}
    out = nc.dram_tensor("out", (SEQ, D), F32, kind="ExternalOutput").ap()
    build(nc, args, out)
    r = run_bass_kernel_spmd(nc, [arrays], core_ids=[0])
    return r.results[0]["out"].reshape(1, SEQ, D)
```
